# Optimizing a Trainium2 kernel written in Bass

```python
import math, functools
import jax, jax.numpy as jnp
from jax import lax
import numpy as np

D_MODEL = 1024
BATCH = 1
SEQ = 256
DEPTH = 2
DEC_BATCH = 8
DEC_SEQ = 4
PAST_LEN = 2048
PAGE_SIZE = 128

N_META = 16
CHUNK = 64
HA = 4
DK_A = 128
DV_A = 128
HB = 4
DK_B = 128
DV_B = 128
HC = 4
DK_C = 128
DV_C = 128
HD = 4
DK_D = 64
DV_D = 128
CONV_W = 4
GLA_RANK = 16
GLA_TAU = 16.0
D_FF = 2816
N_EXPERTS = 8
TOP_K = 2
MOE_FF = 1408
ROPE_BASE = 10000.0
LN_EPS = 1e-5
NORM_EPS = 1e-6
ALPHA = (2 * DEPTH) ** 0.25
BETA = (8 * DEPTH) ** -0.25
MIX0 = HA * DV_A + HB * DV_B
MIX1 = HC * DV_C + HD * DV_D
QKV_C = 2 * HC * DK_C + HC * DV_C
SPLITS0 = (HA * DK_A, HA * DK_A, HA * DV_A, HA * DV_A, HB * DK_B, HB * DK_B, HB * DV_B, HB * DV_B, HB, HB)
SPLITS1 = (QKV_C, HC * DV_C, HC, HC, HD * DK_D, HD * DK_D, HD * DV_D, HD * DV_D, GLA_RANK)
P0 = sum(SPLITS0)
P1 = sum(SPLITS1)

kernel_name = 'hybrid_retention_mlstm_gdn_gla_step'

def _split(a, sizes):
    idx = [int(i) for i in np.cumsum(sizes)[:-1]]
    return jnp.split(a, idx, axis=-1)

def _heads(a, h):
    b, t, w = a.shape
    return a.reshape(b, t, h, w // h).transpose(0, 2, 1, 3)

def _merge(a):
    b, h, t, d = a.shape
    return a.transpose(0, 2, 1, 3).reshape(b, t, h * d)

def _layer_norm(x, g, b):
    xf = x.astype(jnp.float32)
    mu = xf.mean(-1, keepdims=True)
    var = jnp.square(xf - mu).mean(-1, keepdims=True)
    return ((xf - mu) * lax.rsqrt(var + LN_EPS) * g.astype(jnp.float32) + b.astype(jnp.float32)).astype(x.dtype)

def _head_norm(o, g, rms=False):
    h, d = o.shape[1], o.shape[3]
    if rms:
        on = o * lax.rsqrt(jnp.square(o).mean(-1, keepdims=True) + NORM_EPS)
    else:
        oc = o - o.mean(-1, keepdims=True)
        on = oc * lax.rsqrt(jnp.square(oc).mean(-1, keepdims=True) + NORM_EPS)
    return on * g.astype(jnp.float32).reshape(h, 1, d)

def _l2norm(a):
    return a * lax.rsqrt(jnp.sum(jnp.square(a), -1, keepdims=True) + NORM_EPS)

def _rotary(a, pos):
    half = a.shape[-1] // 2
    inv = ROPE_BASE ** (-jnp.arange(half, dtype=jnp.float32) / half)
    ang = pos.astype(jnp.float32)[:, None] * inv[None, :]
    cos, sin = jnp.cos(ang), jnp.sin(ang)
    a1, a2 = a[..., :half], a[..., half:]
    return jnp.concatenate([a1 * cos - a2 * sin, a1 * sin + a2 * cos], -1)

def _causal(c, strict=False):
    t = jnp.arange(c)
    return (t[:, None] > t[None, :]) if strict else (t[:, None] >= t[None, :])

def _chunk_size(n):
    return CHUNK if n % CHUNK == 0 else n

def _to_chunks(a, c):
    n = a.shape[2] // c
    return jnp.moveaxis(a.reshape(a.shape[:2] + (n, c) + a.shape[3:]), 2, 0)

def _from_chunks(a):
    a = jnp.moveaxis(a, 0, 2)
    return a.reshape(a.shape[:2] + (a.shape[2] * a.shape[3],) + a.shape[4:])

def _run_segments(step, state, xs, segments):
    outs = []
    for start, stop, c in segments:
        seg = tuple(_to_chunks(a[:, :, start:stop], c) for a in xs)
        state, ys = lax.scan(step, state, seg)
        outs.append(_from_chunks(ys))
    return jnp.concatenate(outs, axis=2), state

def _retention_step(S, inp, log_gamma):
    q, k, v = inp
    c = q.shape[2]
    t = jnp.arange(c, dtype=jnp.float32)
    diff = t[:, None] - t[None, :]
    mask = diff >= 0
    dec = jnp.where(mask, jnp.exp(jnp.where(mask, diff, 0.0) * log_gamma[:, None, None]), 0.0)
    att = jnp.einsum('bhtd,bhsd->bhts', q, k) * dec
    carry_dec = jnp.exp((t[None, :] + 1.0) * log_gamma[:, None])[:, :, None]
    o = jnp.einsum('bhts,bhse->bhte', att, v) + carry_dec * jnp.einsum('bhtd,bhde->bhte', q, S)
    k_dec = k * jnp.exp((c - 1.0 - t[None, :]) * log_gamma[:, None])[:, :, None]
    S = jnp.exp(c * log_gamma)[:, None, None] * S + jnp.einsum('bhsd,bhse->bhde', k_dec, v)
    return S, o

def _mlstm_step(carry, inp):
    C, n, m = carry
    q, k, v, it, lf = inp
    c = q.shape[2]
    b = jnp.cumsum(lf, axis=-1)
    logw = jnp.where(_causal(c), b[..., :, None] - b[..., None, :] + it[..., None, :], -jnp.inf)
    m_t = jnp.maximum(b + m[..., None], logw.max(-1))
    w = jnp.exp(logw - m_t[..., None])
    carry_scale = jnp.exp(b + m[..., None] - m_t)
    qk = jnp.einsum('bhtd,bhsd->bhts', q, k) * w
    num = jnp.einsum('bhts,bhse->bhte', qk, v) + carry_scale[..., None] * jnp.einsum('bhtd,bhde->bhte', q, C)
    den = qk.sum(-1) + carry_scale * jnp.einsum('bhtd,bhd->bht', q, n)
    h = num / jnp.maximum(jnp.abs(den), jnp.exp(-m_t))[..., None]
    m_new = m_t[..., -1]
    w_last = jnp.exp(b[..., -1:] - b + it - m_new[..., None])
    decay = jnp.exp(b[..., -1] + m - m_new)
    C = decay[..., None, None] * C + jnp.einsum('bhs,bhsd,bhse->bhde', w_last, k, v)
    n = decay[..., None] * n + jnp.einsum('bhs,bhsd->bhd', w_last, k)
    return (C, n, m_new), h

def _gdn_step(S, inp):
    q, k, v, beta, g = inp
    c = q.shape[2]
    gc = jnp.cumsum(g, axis=-1)
    G = gc[..., :, None] - gc[..., None, :]
    strict, incl = _causal(c, True), _causal(c)
    dec_strict = jnp.exp(jnp.where(strict, G, -jnp.inf))
    dec_incl = jnp.exp(jnp.where(incl, G, -jnp.inf))
    A = beta[..., :, None] * jnp.einsum('bhtd,bhsd->bhts', k, k) * dec_strict
    rhs = jnp.concatenate([beta[..., None] * v, (beta * jnp.exp(gc))[..., None] * k], -1)
    sol = lax.linalg.triangular_solve(A + jnp.eye(c, dtype=A.dtype), rhs, left_side=True, lower=True, unit_diagonal=True)
    u_t, w = sol[..., :v.shape[-1]], sol[..., v.shape[-1]:]
    u = u_t - jnp.einsum('bhsd,bhde->bhse', w, S)
    qk = jnp.einsum('bhtd,bhsd->bhts', q, k) * dec_incl
    o = jnp.exp(gc)[..., None] * jnp.einsum('bhtd,bhde->bhte', q, S) + jnp.einsum('bhts,bhse->bhte', qk, u)
    gl = gc[..., -1]
    S = jnp.exp(gl)[..., None, None] * S + jnp.einsum('bhsd,bhse->bhde', k * jnp.exp(gl[..., None] - gc)[..., None], u)
    return S, o

def _gla_step(S, inp):
    q, k, v, la = inp
    c = q.shape[2]
    bc = jnp.cumsum(la, axis=2)
    diff = jnp.where(_causal(c)[:, :, None], bc[:, :, :, None, :] - bc[:, :, None, :, :], -jnp.inf)
    att = jnp.einsum('bhtd,bhsd,bhtsd->bhts', q, k, jnp.exp(diff))
    o = jnp.einsum('bhts,bhse->bhte', att, v) + jnp.einsum('bhtd,bhde->bhte', q * jnp.exp(bc), S)
    bl = bc[:, :, -1]
    S = jnp.exp(bl)[..., None] * S + jnp.einsum('bhsd,bhse->bhde', k * jnp.exp(bl[:, :, None, :] - bc), v)
    return S, o

def _swiglu(x, wg, wu, wd):
    return (jax.nn.silu(x @ wg) * (x @ wu)) @ wd

def _moe(x, w_router, b_router, w_gate, w_up, w_down):
    logits = (x @ w_router).astype(jnp.float32) + b_router.astype(jnp.float32)
    probs = jax.nn.softmax(logits, -1)
    top_p, top_i = lax.top_k(probs, TOP_K)
    top_p = top_p / top_p.sum(-1, keepdims=True)
    gates = jnp.sum(jax.nn.one_hot(top_i, N_EXPERTS, dtype=jnp.float32) * top_p[..., None], -2).astype(x.dtype)
    y = jnp.zeros_like(x)
    for e in range(N_EXPERTS):
        h = jax.nn.silu(x @ w_gate[e]) * (x @ w_up[e])
        y = y + gates[..., e:e + 1] * (h @ w_down[e])
    return y

def _mixer_even(x, state, pos, segments, p):
    f32 = jnp.float32
    s_ret, s_c, s_n, s_m = (s.astype(f32) for s in state)
    proj = (x @ p['w_in0']).astype(f32)
    qa, ka, va, ga, qb, kb, vb, ob, ib, fb = _split(proj, SPLITS0)
    qa = _rotary(_heads(qa, HA), pos)
    ka = _rotary(_heads(ka, HA), pos) * DK_A ** -0.5
    va = _heads(va, HA)
    log_gamma = jnp.log(1.0 - 2.0 ** (-5.0 - jnp.arange(HA, dtype=f32)))
    o_a, s_ret = _run_segments(functools.partial(_retention_step, log_gamma=log_gamma), s_ret, (qa, ka, va), segments)
    y_a = _merge(_head_norm(o_a, p['ret_norm_g'])) * jax.nn.silu(ga)
    gb = p['mlstm_gate_bias'].astype(f32)
    qb = _heads(qb, HB)
    kb = _heads(kb, HB) * DK_B ** -0.5
    vb = _heads(vb, HB)
    i_pre = (ib + gb[:HB]).transpose(0, 2, 1)
    log_f = jax.nn.log_sigmoid(fb + gb[HB:]).transpose(0, 2, 1)
    h_b, (s_c, s_n, s_m) = _run_segments(_mlstm_step, (s_c, s_n, s_m), (qb, kb, vb, i_pre, log_f), segments)
    h_b = jax.nn.sigmoid(_heads(ob, HB)) * h_b
    y_b = _merge(_head_norm(h_b, p['mlstm_norm_g']))
    y = jnp.concatenate([y_a, y_b], -1).astype(x.dtype) @ p['w_out0']
    return y, (s_ret, s_c, s_n, s_m)

def _mixer_odd(x, state, segments, p):
    f32 = jnp.float32
    s_gdn, s_conv, s_gla = state
    s_gdn = s_gdn.astype(f32)
    s_gla = s_gla.astype(f32)
    proj = x @ p['w_in1']
    qkv_c, z_c, b_c, a_c, q_d, k_d, v_d, r_d, lr_d = _split(proj, SPLITS1)
    xc = jnp.concatenate([s_conv.astype(proj.dtype), qkv_c], 1)
    new_conv = xc[:, xc.shape[1] - (CONV_W - 1):]
    conv = lax.conv_general_dilated(xc.astype(f32), p['gdn_conv_w'].astype(f32)[:, None, :], window_strides=(1,), padding='VALID', dimension_numbers=('NWC', 'WIO', 'NWC'), feature_group_count=QKV_C)
    qc, kc, vc = _split(jax.nn.silu(conv), (HC * DK_C, HC * DK_C, HC * DV_C))
    qc = _l2norm(_heads(qc, HC)) * DK_C ** -0.5
    kc = _l2norm(_heads(kc, HC))
    vc = _heads(vc, HC)
    beta = jax.nn.sigmoid(b_c.astype(f32)).transpose(0, 2, 1)
    g = (-jnp.exp(p['gdn_a_log'].astype(f32)) * jax.nn.softplus(a_c.astype(f32) + p['gdn_dt_bias'].astype(f32))).transpose(0, 2, 1)
    o_c, s_gdn = _run_segments(_gdn_step, s_gdn, (qc, kc, vc, beta, g), segments)
    y_c = _merge(_head_norm(o_c, p['gdn_norm_g'], rms=True)) * jax.nn.silu(z_c.astype(f32))
    qd = _heads(q_d.astype(f32), HD) * DK_D ** -0.5
    kd = _heads(k_d.astype(f32), HD)
    vd = _heads(v_d.astype(f32), HD)
    log_alpha = jax.nn.log_sigmoid(lr_d.astype(f32) @ p['gla_w_alpha'].astype(f32) + p['gla_b_alpha'].astype(f32)) / GLA_TAU
    o_d, s_gla = _run_segments(_gla_step, s_gla, (qd, kd, vd, _heads(log_alpha, HD)), segments)
    y_d = _merge(_head_norm(o_d, p['gla_norm_g'])) * jax.nn.silu(r_d.astype(f32))
    y = jnp.concatenate([y_c, y_d], -1).astype(x.dtype) @ p['w_out1']
    return y, (s_gdn, new_conv, s_gla)

def _trunk(x, st_even, st_odd, pos, segments, p):
    for layer in range(DEPTH):
        if layer % 2 == 0:
            h, st_even = _mixer_even(x, st_even, pos, segments, p)
            x = _layer_norm(ALPHA * x + h, p['ln0_mix_g'], p['ln0_mix_b'])
            f = _swiglu(x, p['ffn0_w_gate'], p['ffn0_w_up'], p['ffn0_w_down'])
            x = _layer_norm(ALPHA * x + f, p['ln0_ffn_g'], p['ln0_ffn_b'])
        else:
            h, st_odd = _mixer_odd(x, st_odd, segments, p)
            x = _layer_norm(ALPHA * x + h, p['ln1_mix_g'], p['ln1_mix_b'])
            f = _moe(x, p['moe_w_router'], p['moe_b_router'], p['moe_w_gate'], p['moe_w_up'], p['moe_w_down'])
            x = _layer_norm(ALPHA * x + f, p['ln1_ffn_g'], p['ln1_ffn_b'])
    return x, st_even, st_odd

def setup_inputs(seed: int = 0) -> dict:
    key = jax.random.key(seed)
    ks = jax.random.split(key, 64)
    cnt = [0]
    f32 = jnp.float32

    def nk():
        cnt[0] += 1
        return ks[cnt[0] - 1]

    def nrm(shape, scale):
        return jax.random.normal(nk(), shape, f32) * scale

    def gain(n):
        return 1.0 + nrm((n,), 0.02)

    def bias(n):
        return nrm((n,), 0.02)

    dt = jnp.exp(jax.random.uniform(nk(), (HC,), f32, math.log(1e-3), math.log(1e-1)))
    inp = {}
    inp['x_prompt'] = nrm((BATCH, SEQ, D_MODEL), 1.0)
    inp['x_sample'] = nrm((DEC_BATCH, DEC_SEQ, D_MODEL), 1.0)
    inp['state_ret'] = nrm((DEC_BATCH, HA, DK_A, DV_A), 0.5)
    inp['state_mlstm_c'] = nrm((DEC_BATCH, HB, DK_B, DV_B), 0.5)
    inp['state_mlstm_n'] = nrm((DEC_BATCH, HB, DK_B), 0.5)
    inp['state_mlstm_m'] = nrm((DEC_BATCH, HB), 1.0)
    inp['state_gdn'] = nrm((DEC_BATCH, HC, DK_C, DV_C), 0.3)
    inp['state_gdn_conv'] = nrm((DEC_BATCH, CONV_W - 1, QKV_C), 1.0)
    inp['state_gla'] = nrm((DEC_BATCH, HD, DK_D, DV_D), 0.5)
    inp['meta_tokens'] = nrm((N_META, D_MODEL), 1.0)
    inp['w_in0'] = nrm((D_MODEL, P0), D_MODEL ** -0.5)
    inp['ret_norm_g'] = gain(HA * DV_A)
    inp['mlstm_gate_bias'] = jnp.concatenate([nrm((HB,), 0.1), jnp.linspace(3.0, 6.0, HB, dtype=f32) + nrm((HB,), 0.1)])
    inp['mlstm_norm_g'] = gain(HB * DV_B)
    inp['w_out0'] = nrm((MIX0, D_MODEL), MIX0 ** -0.5 * BETA)
    inp['ln0_mix_g'] = gain(D_MODEL)
    inp['ln0_mix_b'] = bias(D_MODEL)
    inp['ffn0_w_gate'] = nrm((D_MODEL, D_FF), D_MODEL ** -0.5)
    inp['ffn0_w_up'] = nrm((D_MODEL, D_FF), D_MODEL ** -0.5)
    inp['ffn0_w_down'] = nrm((D_FF, D_MODEL), D_FF ** -0.5 * BETA)
    inp['ln0_ffn_g'] = gain(D_MODEL)
    inp['ln0_ffn_b'] = bias(D_MODEL)
    inp['w_in1'] = nrm((D_MODEL, P1), D_MODEL ** -0.5)
    inp['gdn_conv_w'] = nrm((CONV_W, QKV_C), CONV_W ** -0.5)
    inp['gdn_a_log'] = jnp.log(jax.random.uniform(nk(), (HC,), f32, 1.0, 16.0))
    inp['gdn_dt_bias'] = dt + jnp.log(-jnp.expm1(-dt))
    inp['gdn_norm_g'] = gain(HC * DV_C)
    inp['gla_w_alpha'] = nrm((GLA_RANK, HD * DK_D), GLA_RANK ** -0.5)
    inp['gla_b_alpha'] = bias(HD * DK_D)
    inp['gla_norm_g'] = gain(HD * DV_D)
    inp['w_out1'] = nrm((MIX1, D_MODEL), MIX1 ** -0.5 * BETA)
    inp['ln1_mix_g'] = gain(D_MODEL)
    inp['ln1_mix_b'] = bias(D_MODEL)
    inp['moe_w_router'] = nrm((D_MODEL, N_EXPERTS), D_MODEL ** -0.5)
    inp['moe_b_router'] = nrm((N_EXPERTS,), 0.01)
    inp['moe_w_gate'] = nrm((N_EXPERTS, D_MODEL, MOE_FF), D_MODEL ** -0.5)
    inp['moe_w_up'] = nrm((N_EXPERTS, D_MODEL, MOE_FF), D_MODEL ** -0.5)
    inp['moe_w_down'] = nrm((N_EXPERTS, MOE_FF, D_MODEL), MOE_FF ** -0.5 * BETA)
    inp['ln1_ffn_g'] = gain(D_MODEL)
    inp['ln1_ffn_b'] = bias(D_MODEL)
    return inp

def reference(x_prompt, x_sample, state_ret, state_mlstm_c, state_mlstm_n, state_mlstm_m, state_gdn, state_gdn_conv, state_gla, meta_tokens, w_in0, ret_norm_g, mlstm_gate_bias, mlstm_norm_g, w_out0, ln0_mix_g, ln0_mix_b, ffn0_w_gate, ffn0_w_up, ffn0_w_down, ln0_ffn_g, ln0_ffn_b, w_in1, gdn_conv_w, gdn_a_log, gdn_dt_bias, gdn_norm_g, gla_w_alpha, gla_b_alpha, gla_norm_g, w_out1, ln1_mix_g, ln1_mix_b, moe_w_router, moe_b_router, moe_w_gate, moe_w_up, moe_w_down, ln1_ffn_g, ln1_ffn_b):
    p = dict(w_in0=w_in0, ret_norm_g=ret_norm_g, mlstm_gate_bias=mlstm_gate_bias, mlstm_norm_g=mlstm_norm_g, w_out0=w_out0, ln0_mix_g=ln0_mix_g, ln0_mix_b=ln0_mix_b, ffn0_w_gate=ffn0_w_gate, ffn0_w_up=ffn0_w_up, ffn0_w_down=ffn0_w_down, ln0_ffn_g=ln0_ffn_g, ln0_ffn_b=ln0_ffn_b, w_in1=w_in1, gdn_conv_w=gdn_conv_w, gdn_a_log=gdn_a_log, gdn_dt_bias=gdn_dt_bias, gdn_norm_g=gdn_norm_g, gla_w_alpha=gla_w_alpha, gla_b_alpha=gla_b_alpha, gla_norm_g=gla_norm_g, w_out1=w_out1, ln1_mix_g=ln1_mix_g, ln1_mix_b=ln1_mix_b, moe_w_router=moe_w_router, moe_b_router=moe_b_router, moe_w_gate=moe_w_gate, moe_w_up=moe_w_up, moe_w_down=moe_w_down, ln1_ffn_g=ln1_ffn_g, ln1_ffn_b=ln1_ffn_b)
    f32 = jnp.float32
    bp, _, d = x_prompt.shape
    meta = jnp.broadcast_to(meta_tokens.astype(x_prompt.dtype)[None], (bp, N_META, d))
    xp = jnp.concatenate([meta, x_prompt], 1)
    tp = xp.shape[1]
    st_even_p = (jnp.zeros((bp, HA, DK_A, DV_A), f32), jnp.zeros((bp, HB, DK_B, DV_B), f32), jnp.zeros((bp, HB, DK_B), f32), jnp.zeros((bp, HB), f32))
    st_odd_p = (jnp.zeros((bp, HC, DK_C, DV_C), f32), jnp.zeros((bp, CONV_W - 1, QKV_C), xp.dtype), jnp.zeros((bp, HD, DK_D, DV_D), f32))
    segs_p = ((0, N_META, N_META), (N_META, tp, _chunk_size(tp - N_META)))
    yp, (p_ret, p_mc, p_mn, p_mm), (p_gdn, p_conv, p_gla) = _trunk(xp, st_even_p, st_odd_p, jnp.arange(tp), segs_p, p)
    y_prompt = yp[:, N_META:]
    ts = x_sample.shape[1]
    segs_s = ((0, ts, _chunk_size(ts)),)
    pos_s = PAST_LEN + jnp.arange(ts)
    y_sample, (s_ret, s_mc, s_mn, s_mm), (s_gdn, s_conv, s_gla) = _trunk(x_sample, (state_ret, state_mlstm_c, state_mlstm_n, state_mlstm_m), (state_gdn, state_gdn_conv, state_gla), pos_s, segs_s, p)
    return (y_prompt, y_sample, p_ret, p_mc, p_mn, p_mm, p_gdn, p_conv, p_gla, s_ret, s_mc, s_mn, s_mm, s_gdn, s_conv, s_gla)


_drawn_inputs = setup_inputs


def setup_inputs(seed=0):
    import zlib

    import numpy as np

    out = dict(_drawn_inputs(seed))
    spreads = {}
    factors = {'ret_norm_g': 8.0,
     'mlstm_norm_g': 7.562,
     'gdn_norm_g': 8.0,
     'gla_b_alpha': 7.158,
     'gla_norm_g': 18.767,
     'moe_b_router': 9.247,
     'ln1_ffn_g': 7.43,
     'ln1_ffn_b': 7.044}
    for name, (base, spread) in spreads.items():
        noise = np.random.default_rng([zlib.crc32(name.encode()), seed]).standard_normal(out[name].shape)
        drawn = base * np.exp(spread * noise) if base else spread * noise
        out[name] = __import__('jax').numpy.asarray(drawn.astype(out[name].dtype))
    for name, factor in factors.items():
        out[name] = (out[name] * factor).astype(out[name].dtype)
    return out
```

```python
import math
from contextlib import ExitStack

import concourse.bass as bass
from concourse import mybir

D, KT = 1024, 8
NMETA, SEQ, NB, NS = 16, 256, 8, 4
TP, TS = NMETA + SEQ, NB * NS
T = TP + TS
TILES = [(0, 128), (128, 128), (256, T - 256)]
R2 = T - 256
PR2 = TP - 256
H = 4
HT = H * T
FT = 11
NE = 8
FE = 2
QKV = 1536
LN_EPS, EPS = 1e-5, 1e-6
ALPHA = 4 ** 0.25
ATT = 464
A1, A2 = TP, TP + (TP - 128)
SEGS = 1 + NB
NVEC, NCONV = 82, 48
CONVW = 3 + TP + NB * (3 + NS)
CC = dict(ident=(0, 128), meanD=(128, 128), meanE=(256, 128), ones=(384, 128))
C0 = dict(rot=(0, 128), cos=(128, 2 * T), sin=(128 + 2 * T, 2 * T), dec=(128 + 4 * T, 4 * ATT),
          mask=(128 + 4 * T + 4 * ATT, ATT), gq=(128 + 4 * T + 5 * ATT, 128),
          gk=(256 + 4 * T + 5 * ATT, 8), gk2=(264 + 4 * T + 5 * ATT, 36), blk=(300 + 4 * T + 5 * ATT, 9))
C1 = dict(incl=(0, T), strict=(T, T), same8=(2 * T, T), eye=(3 * T, T), gla=(4 * T, T), rst=(5 * T, T),
          seg9=(6 * T, SEGS * R2), blk=(6 * T + SEGS * R2, 9), tri=(6 * T + SEGS * R2 + 9, 64))
N0, N1 = 309 + 4 * T + 5 * ATT, 6 * T + SEGS * R2 + 73
C4 = dict(rst0=(0, T), rneg=(T, T), rstg=(2 * T, T))
N4 = 3 * T


def build(nc, I, O):
    F32 = mybir.dt.float32
    ALU, ACT, AX = mybir.AluOpType, mybir.ActivationFunctionType, mybir.AxisListType
    MUL, ADD, SUB, MAX, MIN = ALU.mult, ALU.add, ALU.subtract, ALU.max, ALU.min
    EXP, LN, COPY, IDN, SQR, SILU, SIGM = ACT.Exp, ACT.Ln, ACT.Copy, ACT.Identity, ACT.Square, ACT.Silu, ACT.Sigmoid
    V, S_, G, PEE = nc.vector, nc.scalar, nc.gpsimd, nc.tensor
    ctx = ExitStack()
    sems = {}

    SHARED = {
        "mean": [("r_", 1), ("m_", 1), ("l_", 1)], "cent": [("r_", 1), ("m_", 1), ("l_", 1)],
        "sq": [("r_", 1), ("m_", 1), ("g_", 1), ("l_", 1)], "var": [("r_", 1), ("m_", 1), ("g_", 1), ("l_", 1)],
        "rstd": [("r_", 1), ("m_", 1), ("g_", 1), ("l_", 1)], "out": [("r_", 1), ("m_", 1), ("g_", 1), ("l_", 1)],
        "state_pe": [("r_", 4), ("m_", 4), ("g_", 4), ("l_", 4)], "stu": [("r_", 4), ("m_", 4), ("g_", 4), ("l_", 4)],
        "vb": [("r_", 4), ("m_", 4), ("g_", 4), ("l_", 4)], "vd": [("r_", 1), ("m_", 1)], "pst": [("r_", 1), ("m_", 1)],
        "o": [("r_", 4), ("m_", 4), ("g_", 4), ("l_", 4)], "att": [("r_", 4), ("m_", 4), ("g_", 1), ("l_", 4)],
        "qk": [("r_", 4), ("m_", 4), ("g_", 4), ("l_", 4)], "qs": [("r_", 1), ("m_", 1)],
        "bc": [("m_", 4), ("g_", 1)], "colpe": [("m_", 1), ("g_", 1)], "col": [("m_", 1), ("g_", 1)],
        "abs": [("m_", 1), ("g_", 1), ("l_", 1)], "lse": [("m_", 1), ("g_", 1), ("l_", 1)], "rows": [("m_", 1), ("g_", 1)],
        "kt": [("r_", 3), ("g_", 3), ("l_", 1)], "vt": [("r_", 3), ("g_", 3), ("l_", 3)],
        "normmean": [("n0m_", 1), ("n0f_", 1), ("n1m_", 1), ("n1f_", 1)], "normcent": [("n0m_", 1), ("n0f_", 1), ("n1m_", 1), ("n1f_", 1)],
        "normsq": [("n0m_", 1), ("n0f_", 1), ("n1m_", 1), ("n1f_", 1)], "normvar": [("n0m_", 1), ("n0f_", 1), ("n1m_", 1), ("n1f_", 1)],
        "normrstd": [("n0m_", 1), ("n0f_", 1), ("n1m_", 1), ("n1f_", 1)], "normx": [("n0m_", 1), ("n0f_", 1), ("n1m_", 1), ("n1f_", 1)],
        "normz": [("n0m_", 1), ("n1m_", 1)],
        "w0": [("f0_", 192), ("f1_", 0)], "w1": [("f0_", 192), ("f1_", 0)], "w2": [("f0_", 192), ("f1_", 0)], "w3": [("f0_", 128), ("f1_", 0)],
        "d0": [("f0_", 64), ("f1_", 0)], "d1": [("f0_", 64), ("f1_", 0)], "d2": [("f0_", 64), ("f1_", 0)], "d3": [("f0_", 64), ("f1_", 0)],
    }
    CHAINS = {
        "router_pe": [("x_log", 1), ("x_gt", 1), ("x_bc", 8)], "router_dve": [("x_lm", 1), ("x_gate", 1), ("x_gtev", 1)],
        "tok_act": [("r_vtok", 3), ("r_ktok", 3), ("m_tok", 6), ("g_tok_a", 3), ("l_tok", 6)],
        "oev_act": [("r_oev", 4), ("g_oev", 1), ("l_oev", 1)],
        "late_load": [("ld_halo", 16), ("ld_stG", 32), ("ld_router", 32)], "silu": [("f0_silu", FE * FT), ("f1_silu", 0)],
        "rope_pe": [("vec_pe", 1), ("rot", 1)], "rows_exp": [("m_exp", 1), ("g_eg", 1)],
    }
    WHERE = {}
    for kind, users in CHAINS.items():
        base = 0
        for name, count in users:
            WHERE[name] = (kind, base)
            base += count
    for kind, users in SHARED.items():
        base = 0
        for prefix, count in users:
            WHERE[prefix + kind.removeprefix("norm")] = (kind, base)
            base += count

    def s(name):
        kind = WHERE.get(name, (name, 0))[0]
        if kind not in sems:
            sems[kind] = ctx.enter_context(nc.semaphore(kind))
        return sems[kind]

    def at(name, n):
        return s(name), n + WHERE.get(name, (name, 0))[1]

    with ctx:
        def sb(name, shape):
            return ctx.enter_context(nc.sbuf_tensor(name, shape, F32))

        xT = sb("xT", [128, KT, T])
        zT = sb("zT", [128, KT, T])
        mix = sb("mix", [128, KT, T])
        wring = sb("wring", [128, 8192])
        dring = sb("dring", [128, 4 * FT * 128])
        proj = sb("proj", [128, 32 * T])
        stA = sb("stA", [128, 32, 128])
        stB = sb("stB", [128, 32, 128])
        cst = sb("cst", [128, max(N0, N1)])
        cc = sb("cc", [128, 512])
        vec = sb("vec", [128, NVEC + NCONV])
        arena = sb("arena", [128, 9600])
        PS = ctx.enter_context(nc.psum_tensor("PS", [128, 8, 512], F32))

        def const(table, name):
            a, n = table[name]
            return (cc if table is CC else cst)[:, a:a + n]

        ident, meanD, meanE, ones = (const(CC, n) for n in ("ident", "meanD", "meanE", "ones"))
        halves = [wring[:, 4096 * i:4096 * (i + 1)].rearrange("p (k n) -> p k n", k=KT) for i in range(2)]
        slots = [wring[:, 2048 * i:2048 * (i + 1)].rearrange("p (g k n) -> p g k n", g=2, k=KT) for i in range(4)]
        dslots = [dring[:, 1408 * i:1408 * (i + 1)].rearrange("p (k n) -> p k n", k=FT) for i in range(4)]
        P = proj[:].rearrange("p (m t) -> p m t", t=T)

        VEC = {n: 8 * i for i, n in enumerate(["mix0_g", "mix0_b", "ffn0_g", "ffn0_b", "mix1_g", "mix1_b", "ffn1_g", "ffn1_b"])}
        VEC |= {"ret": 64, "mlstm": 68, "gdn": 72, "gla": 76, "balpha": 80}

        def carve(base, at, n, *shape):
            v = base[:, at:at + n]
            if len(shape) == 2:
                v = v.rearrange("p (a b) -> p a b", a=shape[0])
            if len(shape) == 3:
                v = v.rearrange("p (a b c) -> p a b c", a=shape[0], b=shape[1])
            return v

        ktok = carve(arena, 0, 1536, 3, 512)
        vtok = carve(arena, 1536, 1536, 3, 512)
        att = carve(arena, 3072, 1856, 4, ATT)
        vd = carve(arena, 4928, 1024, 2, 4, 128)
        pst = carve(arena, 5952, 512, 4, 128)
        ebc = carve(arena, 6464, 1376, 4, 344)
        qs = carve(arena, 7840, 128, 4, 32)
        mcol = carve(arena, 7968, 24)
        wl2 = carve(arena, 7992, 36, 4, 9)
        nT = carve(arena, 8032, 36)
        nrow = carve(arena, 8068, 128)
        gates0 = carve(arena, 8196, 2)
        m0 = carve(arena, 8198, 9)
        wsm = carve(arena, 8208, KT * 24, KT, 24)
        nload = carve(arena, 8400, 128)
        r4 = carve(dring, 0, N4)
        ROW = [dring[0:4, N4 + 344 * i:N4 + 344 * (i + 1)] for i in range(8)]
        vb = [carve(dring, 4480, 1152, SEGS, 128), mix[:, 4:8, :].rearrange("p a b -> p (a b)")[:, 0:1152]
              .rearrange("p (a b) -> p a b", a=SEGS)]
        xtok = proj[:, 0:3072].rearrange("p (a b) -> p a b", a=3)
        vrows = proj[:, 3072:3328]

        mixf, zf = mix[:].rearrange("p a b -> p (a b)"), zT[:].rearrange("p a b -> p (a b)")
        stBf = stB[:].rearrange("p a b -> p (a b)")
        cin = carve(mixf, 0, 4 * CONVW, 4, CONVW)
        cacc = carve(mixf, 4 * CONVW, 2 * CONVW, 2, CONVW)
        convT = carve(zf, 0, 288, 12, 24)
        lastT = carve(zf, 288, 324, 12, 27)
        lastrow = carve(arena, 6400, 1536)
        sqn = carve(arena, 0, 2432, 8, T)
        decI = carve(arena, 0, HT, 4, T)
        attg = carve(arena, HT, HT, 4, T)
        kb = carve(arena, 2 * HT, HT, 4, T)
        qe = carve(arena, 3 * HT, HT, 4, T)
        ktg = carve(arena, 4864, 1536, 3, 512)
        ug = carve(arena, 6400, 1536, 3, 512)
        sg = carve(arena, 7936, 1536, 3, 4, 128)
        gcol = carve(arena, 9472, 48, 4, 3, 4)
        dbc = carve(arena, 9520, 44, 4, 11)
        SDT, SD = carve(zf, 0, HT, 4, T), carve(zf, HT, HT, 4, T)
        SRT, SO = carve(mixf, 0, HT, 4, T), carve(mixf, HT, HT, 4, T)
        SP_, SPT = carve(dring, 0, HT, 4, T), carve(dring, HT, HT, 4, T)
        rhsk = carve(dring, 2432, 1536, 3, 512)
        rhsv = carve(dring, 3968, 1536, 3, 512)
        ub = [carve(dring, 0, 1152, SEGS, 128), carve(dring, HT, 1152, SEGS, 128)]
        r4b = carve(stBf, 0, N4)
        GROW = [stBf[0:4, N4 + 315 * i:N4 + 315 * (i + 1)] for i in range(7)]
        wtm = carve(stBf, 2368, 4 * SEGS * R2, 4, SEGS, R2)
        lrT, walpha = P[0:16, 28, :], P[0:16, 29, 0:256]
        bc_, cb_, kx_, e1, e2, e3, q1, k1, _, k2 = (carve(arena, 608 * i, 608, 2, T) for i in range(10))
        q2 = carve(arena, 608 * 3, HT, 4, T)
        ktl = carve(arena, 6080, 768, 3, 256)
        vtl = carve(arena, 6848, 1536, 3, 512)
        attl = carve(arena, 8384, HT, 4, T)
        sc = carve(dring, 0, 1280, 5, 2, 128)
        lb = [carve(dring, 1280, 1152, SEGS, 128), carve(dring, 2432, 1152, SEGS, 128)]
        lvp = carve(dring, 3584, 512, 4, 128)
        stG = stB[:, 0:16, :]

        SOLVE = [("split", None, SDT, None, None),
                 ("copy", SP_, SDT, SD, 0),
                 ("copy", SPT, SD, SDT, 0),
                 ("add", SRT, SP_, SRT, 1),
                 ("copy", SD, SPT, SP_, 2),
                 ("add", SRT, SD, SRT, 4),
                 ("copy", SP_, SRT, SO, 5),
                 ("copyz", SPT, SO, SRT, 5),
                 ("transpose", SDT, SRT, None, 5),
                 ("copy", SD, SPT, SP_, 7),
                 ("copy", SRT, SP_, SPT, 8),
                 ("add", SO, SD, SO, 9),
                 ("copy", SP_, SRT, SD, 10),
                 ("copy", SPT, SD, SRT, 10),
                 ("add", SO, SP_, SO, 12),
                 ("copy", SD, SPT, SP_, 13),
                 ("add", SO, SD, SO, 15),
                 ("copy", SRT, SDT, SO, 16)]
        ORDER = [(k, i) for k in range(len(SOLVE)) for i in range(3) if i < 2 or k <= 8 or k == 17]
        AT = {ki: n for n, ki in enumerate(ORDER)}

        def solve_after(k, i):
            w = SOLVE[k][4]
            if i == 2 and k == 17:
                w = 8
            return 0 if w is None else AT[(w, i)] + 1

        hid = P[:, 0:11, :]
        gact = P[:, 11:13, :]
        gtmp = P[:, 13:15, :]
        gbc = P[:, 15:23, :]
        rt = proj[:, 23 * T:32 * T]
        lt, lm, gate = (carve(rt, 24 * i, 24, 3, 8) for i in range(3))
        gcmp, geq = (carve(rt, 72 + 192 * i, 192, 3, 64) for i in range(2))
        st3 = carve(rt, 456, 24, 3, 8)
        gT = rt[:, 480:480 + T]
        brt = rt[:, 800:808]
        wrt = carve(rt, 832, 64, KT, 8)

        def bank4(a):
            return PS[:, a:a + 4, 0:T]

        def smp(ap):
            return ap[:, TP:T].rearrange("p (b t) -> p b t", b=NB)

        def cins(m):
            return cin[:, m % 4, 3 + TP:CONVW].rearrange("p (b t) -> p b t", b=NB)

        def cconv(m):
            return cacc[:, m % 2, 3 + TP:CONVW].rearrange("p (b t) -> p b t", b=NB)[:, :, 0:NS]

        in0 = [512 * g for g in range(8)]
        in1 = [0, 512, 1024, 1536, 2056, 2568, 3080]
        groups = [(I["w_in0"], c) for c in in0] + [(I["w_out0"], c) for c in (0, 512)] \
            + [(I["w_in1"], c) for c in in1] + [(I["w_out1"], c) for c in (0, 512)]
        OUT0, IN1, OUT1, GEND = 8, 10, 17, 19

        def ffn_weights(layer):
            if layer == 0:
                g, u = (I[n].rearrange("(k p) (e j f) -> e j p k f", p=128, e=FE, j=FT) for n in ("ffn0_w_gate", "ffn0_w_up"))
                d = I["ffn0_w_down"].rearrange("(e j p) (d f) -> e d p j f", p=128, e=FE, d=KT)
            else:
                g, u = (I[n].rearrange("e (k p) (j f) -> e j p k f", p=128, j=FT) for n in ("moe_w_gate", "moe_w_up"))
                d = I["moe_w_down"].rearrange("e (j p) (d f) -> e d p j f", p=128, d=KT)
            return g, u, d, (FE, NE)[layer]

        block = ctx.enter_context(nc.Block())

        @block.sync
        def _(sp):
            def group(g):
                w, c = groups[g]
                if g >= 2:
                    sp.wait_ge(*at("proj_pe", 4 * (g - 1)))
                sp.dma_start(halves[g % 2], w[:, c:c + 512].rearrange("(k p) n -> p k n", p=128)).then_inc(s(f"ring{g % 2}"), 16)

            for i, (a, n) in enumerate(TILES):
                sp.dma_start(xtok[0:n, i, :], I["x_all"][a:a + n]).then_inc(s("ld_x"), 16)
            group(0)
            group(1)
            for g in range(2, OUT0 + 2):
                group(g)

            def ffn(layer):
                wg, wu, wd, E = ffn_weights(layer)
                p = f"f{layer}_"
                sp.wait_ge(*at("proj_pe", 4 * (OUT0 + 2 if layer == 0 else GEND)))
                with sp.Fori(0, E) as e:
                    for j in range(FT):
                        back = {0: -2, 1: -1, 2: 0, 3: -3}[j] if j < 4 else j - 3
                        sp.wait_ge(*at(p + "hid_pe", e * FT + (back + 4)))
                        sp.dma_start(slots[j % 4][:, 0], wg[e, j]).then_inc(s(p + f"w{j % 4}"), 16)
                        sp.dma_start(slots[j % 4][:, 1], wu[e, j]).then_inc(s(p + f"w{j % 4}"), 16)
                    for d in range(KT):
                        sp.wait_ge(*at(p + "down_pe", e * KT + (d + 1)))
                        sp.dma_start(dslots[d % 4], wd[e, d]).then_inc(s(p + f"d{d % 4}"), 16)

            ffn(0)
            for g in range(IN1, GEND):
                if g == IN1:
                    sp.wait_ge(*at("f0_hid_pe", 4 + FE * FT))
                group(g)
            ffn(1)
            sp.wait_ge(*at("y_ev", 6))
            ytok = proj[:, 0:3072].rearrange("p (a b) -> p a b", a=3)
            for i, (a, n) in enumerate(TILES):
                sp.dma_start(O["y_all"][a:a + n], ytok[0:n, i, :]).then_inc(s("st_y"), 16)
            sp.wait_ge(*at("st_y", 48))

        @block.tensor
        def _(pe):
            mm = PEE.matmul

            def tr(out, in_, n):
                return PEE.transpose(out, in_, ident[0:n, 0:n])

            def row(h, n=4):
                return ident[0:n, h:h + 1].to_broadcast([n, 128])

            pe.wait_ge(*at("ld_x", 48))
            pe.wait_ge(*at("ld_v", 64))
            for k in range(KT):
                for i, (a, n) in enumerate(TILES):
                    last = tr(PS[:, k, a:a + n], xtok[0:n, i, 128 * k:128 * k + 128], n)
                last.then_inc(s("xt_pe"), 1)
            pe.wait_ge(*at("xT", KT))
            tr(PS[:, 0, 0:NVEC], vrows[0:NVEC, 0:128], NVEC)
            tr(PS[:, 0, 128:128 + NCONV], vrows[0:NCONV, 128:256], NCONV)
            tr(PS[:, 0, 256:288], nload[0:32, :], 32).then_inc(s("vec_pe"), 1)

            def narrow(layer, parts):
                pe.wait_ge(*at(("ld_wsm", "ld_l1")[layer], (16, 80)[layer]))
                for c, n, b in parts:
                    for k in range(KT):
                        last = mm(PS[0:n, b, 0:T], wsm[:, k, c:c + n], xT[:, k, :], start=k == 0, stop=k == KT - 1)
                last.then_inc(s("small_pe"), 1)

            narrow(0, [(0, 4, 6), (4, 4, 7)])

            def tile_mm(half, t, rhs):
                for k in range(KT):
                    last = mm(PS[:, 4 * half + t, 0:T], halves[half][:, k, 128 * t:128 * t + 128], rhs[:, k, :],
                              start=k == 0, stop=k == KT - 1)
                last.then_inc(s("proj_pe"), 1)

            def group(g, rhs, banks_free=True):
                pe.wait_ge(*at(f"ring{g % 2}", 16 * (g // 2 + 1)))
                for t in range(4):
                    if not banks_free:
                        pe.wait_ge(*at("proj_ev", 4 * (g - 2) + t + 1))
                    tile_mm(g % 2, t, rhs)

            def group_pairs(lo, hi):
                with pe.Fori(lo, hi) as p:
                    for half in range(2):
                        pe.wait_ge(*at(f"ring{half}", p * 16 + 16))
                        for t in range(4):
                            pe.wait_ge(*at("proj_ev", p * 8 + (4 * half + t - 7)))
                            tile_mm(half, t, xT)

            pe.wait_ge(*at("vec_ev", 1))
            group(0, xT)
            pe.wait_ge(*at("small_ev", 1))
            group(1, xT)
            group_pairs(1, 4)

            def state_mm(p, h, kt_, vdec, vblk, kcols, banks, pbank):
                for i in range(2):
                    mm(PS[:, pbank, 128 * h:128 * h + 128], kt_[:, i, kcols], vdec[:, i, h, :], start=i == 0, stop=False)
                mm(PS[:, pbank, 128 * h:128 * h + 128], kt_[0:R2, 2, kcols], vblk[0:R2, 0, :], start=False, stop=True)
                for j, b in enumerate(banks):
                    last = mm(PS[:, b, :], kt_[0:R2, 2, kcols], vblk[0:R2, 1 + 4 * j:5 + 4 * j, :].rearrange("p a b -> p (a b)"),
                              start=True, stop=True)
                last.then_inc(s(p + "state_pe"), 1)

            def out_mm(bank, lhs, h, final):
                mm(PS[:, bank, 0:TP], lhs[0], att[:, h, 0:A1], start=True, stop=False)
                mm(PS[:, bank, 128:TP], lhs[1], att[:, h, A1:A2], start=False, stop=False)
                mm(PS[:, bank, 256:TP], lhs[2], att[0:R2, h, A2:A2 + PR2], start=False, stop=False)
                mm(PS[:, bank, TP:T], lhs[2], att[0:R2, h, A2 + PR2:ATT], start=False, stop=False)
                for b in range(NB):
                    last = mm(PS[:, bank, TP + 4 * b:TP + 4 * b + 4], final(b), qs[:, h, 4 * b:4 * b + 4],
                              start=False, stop=b == NB - 1)
                return last

            def scores(bank, h, q0, k0):
                mm(PS[:, bank, 0:A1], P[:, k0 + h, 0:128], P[:, q0 + h, 0:TP], start=True, stop=True)
                mm(PS[:, bank, A1:A2], P[:, k0 + h, 128:256], P[:, q0 + h, 128:TP], start=True, stop=True)
                return mm(PS[0:R2, bank, A2:ATT], P[:, k0 + h, 256:T], P[:, q0 + h, 256:T], start=True, stop=True)

            def tokens(bank, i, m0_, n=4):
                a, r = TILES[i]
                for h in range(n):
                    last = tr(PS[0:r, bank, 128 * h:128 * h + 128], P[:, m0_ + h, a:a + r], 128)
                return last

            def norm(p, rms=False, mean_at=0, var_at=4):
                o = zT[:, 0:4, :]
                if not rms:
                    for h in range(H):
                        last = mm(PS[:, mean_at + h, 0:T], meanE, o[:, h, :], start=True, stop=True)
                    last.then_inc(s(p + "mean"), 1)
                pe.wait_ge(*at(p + "sq", 1))
                for h in range(H):
                    last = mm(PS[:, var_at + h, 0:T], meanE, zT[:, 4 + h, :], start=True, stop=True)
                last.then_inc(s(p + "var"), 1)

            pe.wait_ge(*at("proj_ev", 32))
            pe.wait_ge(*at("ld_c0", 16))
            for m in range(8):
                last = mm(PS[:, m, 0:T], const(C0, "rot"), P[:, m, :], start=True, stop=True)
            last.then_inc(s("rot"), 1)
            pe.wait_ge(*at("rotm", 1))
            for i in range(3):
                tokens(3 + i, i, 8).then_inc(s("r_vt"), 1)
            pe.wait_ge(*at("rope", 1))
            for i in range(3):
                tokens(i, i, 4).then_inc(s("r_kt"), 1)
            for h, b in enumerate([6, 7, 3, 4]):
                if h == 2:
                    pe.wait_ge(*at("r_vtok", 3))
                scores(b, h, 0, 4).then_inc(s("r_qk"), 1)
            pe.wait_ge(*at("r_ktok", 3))
            pe.wait_ge(*at("r_qs", 1))
            pe.wait_ge(*at("ld_stA", 16))
            for h, b in enumerate([0, 1, 2, 5]):
                pe.wait_ge(*at("r_att", h + 1))
                v = [vtok[:, 0, 128 * h:128 * h + 128], vtok[:, 1, 128 * h:128 * h + 128], vtok[0:R2, 2, 128 * h:128 * h + 128]]
                out_mm(b, v, h, lambda b_: stA[:, 4 * b_ + h, :]).then_inc(s("r_o"), 1)
            pe.wait_ge(*at("r_oev", 4))
            for h in range(H):
                if h == 0:
                    pe.wait_ge(*at("r_vd", 1))
                pe.wait_ge(*at("r_vb", h + 1))
                if h >= 2:
                    pe.wait_ge(*at("r_stu", h - 1))
                state_mm("r_", h, ktok, vd, vb[h % 2], slice(128 * h, 128 * h + 128), [(7, 3), (4, 5)][h % 2], 6)
            pe.wait_ge(*at("r_stu", 4))
            norm("r_", mean_at=0, var_at=0)

            pe.wait_ge(*at("r_out", 1))
            pe.wait_ge(*at("r_pst", 1))
            pe.wait_ge(*at("m_rows", 1))
            pe.wait_ge(*at("m_exp", 1))
            for i, (a, n) in enumerate(TILES):
                tr(PS[0:n, 7, 4 * i:4 * i + 4], ROW[3][:, a:a + n], 4)
                last = tr(PS[0:n, 7, 12 + 4 * i:16 + 4 * i], ROW[5][:, a:a + n], 4)
            last.then_inc(s("m_colpe"), 1)
            for h in range(H):
                mm(PS[:, h, 0:T], row(h), ROW[4][:, 0:T], start=True, stop=True)
                if h == 3:
                    pe.wait_ge(*at("m_col", 1))
                mm(PS[:, 4 + h, 0:344], row(h), ROW[6], start=True, stop=True).then_inc(s("m_bc"), 1)
            for h in range(H):
                pe.wait_ge(*at("m_ex", h + 1))
                scores(h, h, 16, 20).then_inc(s("m_qk"), 1)
            pe.wait_ge(*at("m_ebc", 1))
            for n_, (b, i, m_) in enumerate([(4, 0, 20), (5, 1, 20), (6, 2, 20), (7, 0, 24), (4, 1, 24), (5, 2, 24)]):
                if n_ >= 4:
                    pe.wait_ge(*at("m_tok", n_ - 3))
                tokens(b, i, m_).then_inc(s("m_tpe"), 1)
            pe.wait_ge(*at("m_tok", 6))
            pe.wait_ge(*at("m_qs", 1))
            pe.wait_ge(*at("ld_stB", 16))
            for h in range(H):
                pe.wait_ge(*at("m_att", h + 1))
                out_mm(4 + h, [ones, ones, ones[0:R2, :]], h, lambda b_: nT[:, 4 * b_ + h:4 * b_ + h + 1].to_broadcast([128, 128]))
                v = [vtok[:, 0, 128 * h:128 * h + 128], vtok[:, 1, 128 * h:128 * h + 128], vtok[0:R2, 2, 128 * h:128 * h + 128]]
                out_mm(h, v, h, lambda b_: stB[:, 4 * b_ + h, :]).then_inc(s("m_o"), 1)
            pe.wait_ge(*at("m_oev", 1))
            pe.wait_ge(*at("m_vd", 1))
            for h in range(H):
                kc = slice(128 * h, 128 * h + 128)
                mm(PS[:, 5, 9 * h:9 * h + 9], ktok[0:R2, 2, kc], wl2[0:R2, h, :], start=True, stop=False)
                for i in range(2):
                    mm(PS[:, 5, 9 * h:9 * h + 1], ktok[:, i, kc], mcol[:, 12 + 4 * i + h:13 + 4 * i + h], start=False, stop=i == 1)
            for h in range(H):
                pe.wait_ge(*at("m_vb", h + 1))
                if h >= 2:
                    pe.wait_ge(*at("m_stu", h - 1))
                kc = slice(128 * h, 128 * h + 128)
                state_mm("m_", h, ktok, vd, vb[h % 2], kc, [(7, 3), (4, 2)][h % 2], 6)
            pe.wait_ge(*at("m_stu", 4))
            pe.wait_ge(*at("m_nst", 1))
            tr(PS[0:36, 0, 0:128], nT[:, 0:36], 128).then_inc(s("m_npe"), 1)
            pe.wait_ge(*at("m_nrow", 1))
            norm("m_", mean_at=0, var_at=0)

            def layer_norm(p, ready, count):
                pe.wait_ge(*at(ready, count))
                for k in range(KT):
                    last = mm(PS[:, 0, 0:T], meanD, zT[:, k, :], start=k == 0, stop=k == KT - 1)
                last.then_inc(s(p + "mean"), 1)
                pe.wait_ge(*at(p + "sq", 1))
                for k in range(KT):
                    last = mm(PS[:, 1, 0:T], meanD, mix[:, k, :], start=k == 0, stop=k == KT - 1)
                last.then_inc(s(p + "var"), 1)

            def ffn(layer):
                p, E = f"f{layer}_", (FE, NE)[layer]
                pe.sem_inc(s(p + "hid_pe"), 4)
                pe.sem_inc(s(p + "down_pe"), 4)
                with pe.Fori(0, E) as e:
                    uses = [0] * 4
                    for j in range(FT):
                        uses[j % 4] += 1
                        pe.wait_ge(*at(p + f"w{j % 4}", e * (32 * (2 + (j % 4 < 3))) + 32 * uses[j % 4]))
                        pe.wait_ge(*at(p + "hid_ev", e * FT + max(j, 1)))
                        for gu in range(2):
                            for k in range(KT):
                                last = mm(PS[:, 2 * (j % 2) + gu, 0:T], slots[j % 4][:, gu, k, :], xT[:, k, :],
                                          start=k == 0, stop=k == KT - 1)
                        last.then_inc(s(p + "hid_pe"), 1)
                    for d in range(KT):
                        pe.wait_ge(*at(p + f"d{d % 4}", e * 32 + 16 * (d // 4 + 1)))
                        pe.wait_ge(*at(p + "down_ev", e * KT + d + 1))
                        for j in range(FT):
                            if d == 0 and j >= FT - 2:
                                pe.wait_ge(*at(p + "hid_ev", e * FT + j + 2))
                            last = mm(PS[:, 4 + d % 4, 0:T], dslots[d % 4][:, j, :], hid[:, j, :], start=j == 0, stop=j == FT - 1)
                        last.then_inc(s(p + "down_pe"), 1)

            pe.wait_ge(*at("m_out", 1))
            group(8, mix)
            group(9, mix)
            layer_norm("n0m_", "proj_ev", 40)
            pe.wait_ge(*at("n0m_x", 1))
            ffn(0)
            layer_norm("n0f_", "f0_down_ev", 4 + FE * KT)
            pe.wait_ge(*at("n0f_x", 1))

            pe.wait_ge(*at("ld_halo", 16))
            for m in range(12):
                last = tr(PS[:, 4, 24 * m:24 * m + 24], dring[0:24, 128 * m:128 * m + 128], 24)
            last.then_inc(s("halo_pe"), 1)
            narrow(1, [(0, 4, 5), (4, 4, 6), (8, 16, 7)])
            group(10, xT)
            pe.wait_ge(*at("small_ev", 2))
            group(11, xT)
            group_pairs(6, 8)
            group(16, xT, banks_free=False)

            pe.wait_ge(*at("last", 12))
            pe.wait_ge(*at("proj_ev", 4 * OUT1))
            for m in range(12):
                last = tr(PS[0:27, m // 4, 128 * (m % 4):128 * (m % 4) + 128], lastT[:, m, :], 128)
            last.then_inc(s("last_pe"), 1)
            pe.wait_ge(*at("last_ev", 1))
            pe.wait_ge(*at("g_sqn", 1))
            for m in range(8):
                last = mm(PS[:, m, 0:T], ones, sqn[:, m, :], start=True, stop=True)
            last.then_inc(s("g_l2pe"), 1)
            pe.wait_ge(*at("g_l2a", 1))
            pe.wait_ge(*at("g_rows", 1))
            for r in range(4):
                for i, (a, n) in enumerate(TILES):
                    last = tr(PS[0:n, 0, 12 * r + 4 * i:12 * r + 4 * i + 4], [GROW[0], GROW[3], GROW[4], GROW[5]][r][:, a:a + n], 4)
            last.then_inc(s("g_colpe"), 1)
            pe.wait_ge(*at("g_col", 1))
            for h in range(H):
                mm(PS[:, h, 0:315], row(h), GROW[2], start=True, stop=True)
                last = mm(PS[:, 4 + h, 0:T], row(h), GROW[0][:, 0:T], start=True, stop=True)
            last.then_inc(s("g_bc"), 1)
            pe.wait_ge(*at("g_bcev", 1))
            pe.wait_ge(*at("g_kb", 1))
            for h in range(H):
                for a, n in TILES:
                    last = mm(PS[0:n, h, a:a + n], P[:, 4 + h, a:a + n], kb[:, h, a:a + n], start=True, stop=True)
                last.then_inc(s("g_aa"), 1)
            for h in range(H):
                for a, n in TILES:
                    last = mm(PS[0:n, 4 + h, a:a + n], P[:, 4 + h, a:a + n], P[:, h, a:a + n], start=True, stop=True)
                last.then_inc(s("g_qk"), 1)
            pe.wait_ge(*at("g_at", 1))
            for i in range(3):
                tokens(i, i, 4).then_inc(s("g_kt"), 1)
            pe.wait_ge(*at("g_att", 1))
            for i in range(3):
                tokens(4 + i, i, 8).then_inc(s("g_vt"), 1)
            pe.wait_ge(*at("g_tok_a", 3))
            pe.wait_ge(*at("g_tok_d", 6))

            for n_, (k, i) in enumerate(ORDER):
                what, out, lhs, rhs, _ = SOLVE[k]
                a, n = TILES[i]
                if solve_after(k, i):
                    pe.wait_ge(*at("sv_ev", solve_after(k, i)))
                if n_ >= 8:
                    pe.wait_ge(*at("sv_ev", n_ - 7))
                for h in range(H):
                    o = PS[0:n, n_ % 8, n * h:n * h + n]
                    if what in ("split", "transpose"):
                        last = tr(o, lhs[0:n, h, a:a + n], n)
                    else:
                        last = mm(o, lhs[0:n, h, a:a + n], rhs[0:n, h, a:a + n], start=True, stop=True)
                last.then_inc(s("sv_pe"), 1)
            pe.wait_ge(*at("sv_ev", len(ORDER)))

            for i, (a, n) in enumerate(TILES):
                for h in range(H):
                    last = mm(PS[:, i, n * h:n * h + n], rhsk[0:n, i, 128 * h:128 * h + 128], SRT[0:n, h, a:a + n], start=True, stop=True)
                last.then_inc(s("g_w"), 1)
            for i, (a, n) in enumerate(TILES):
                if i == 2:
                    pe.wait_ge(*at("g_wtm", 1))
                if i > 0:
                    pe.wait_ge(*at("g_s", i))
                    pe.wait_ge(*at("g_wev", 3))
                for h in range(H):
                    o = PS[0:n, 3, 128 * h:128 * h + 128]
                    last = mm(o, SRT[0:n, h, a:a + n], rhsv[0:n, i, 128 * h:128 * h + 128], start=True, stop=i == 0)
                    if i == 1:
                        last = mm(o, kb[:, h, a:a + n], sg[:, 0, h, :], start=False, stop=True)
                    if i == 2:
                        mm(o, wtm[:, h, 0, :], sg[:, 1, h, :], start=False, stop=False)
                        for b in range(NB):
                            last = mm(o, wtm[:, h, 1 + b, :], stA[:, 4 * b + h, :], start=False, stop=b == NB - 1)
                last.then_inc(s("g_upe"), 1)
                pe.wait_ge(*at("g_ua", i + 1))
                pe.wait_ge(*at("g_ue", i + 1))
                if i < 2:
                    for h in range(H):
                        last = mm(PS[:, 5, 128 * h:128 * h + 128], ktg[:, i, 128 * h:128 * h + 128], rhsk[:, i, 128 * h:128 * h + 128],
                                  start=True, stop=True)
                    last.then_inc(s("g_spe"), 1)
            pe.wait_ge(*at("g_wev", 3))
            for h, b in enumerate([0, 1, 2, 5]):
                for i, (a, n) in enumerate(TILES):
                    mm(PS[:, b, a:a + n], ug[0:n, i, 128 * h:128 * h + 128], attg[0:n, h, a:a + n], start=i == 0, stop=False)
                    if i == 1:
                        mm(PS[:, b, a:a + n], sg[:, 0, h, :], qe[:, h, a:a + n], start=False, stop=False)
                mm(PS[:, b, 256:TP], sg[:, 1, h, :], qe[:, h, 256:TP], start=False, stop=False)
                for b_ in range(NB):
                    last = mm(PS[:, b, TP + 4 * b_:TP + 4 * b_ + 4], stA[:, 4 * b_ + h, :], qe[:, h, TP + 4 * b_:TP + 4 * b_ + 4],
                              start=False, stop=b_ == NB - 1)
                last.then_inc(s("g_o"), 1)
            pe.wait_ge(*at("g_oev", 1))
            for h in range(H):
                pe.wait_ge(*at("g_vb", h + 1))
                if h >= 2:
                    pe.wait_ge(*at("g_stu", h - 1))
                kc = slice(128 * h, 128 * h + 128)
                mm(PS[:, 6, kc], ktg[0:R2, 2, kc], ub[h % 2][0:R2, 0, :], start=True, stop=True)
                for j, b in enumerate([(7, 3), (4, 5)][h % 2]):
                    last = mm(PS[:, b, :], ktg[0:R2, 2, kc], ub[h % 2][0:R2, 1 + 4 * j:5 + 4 * j, :].rearrange("p a b -> p (a b)"),
                              start=True, stop=True)
                last.then_inc(s("g_state_pe"), 1)
            pe.wait_ge(*at("g_stu", 4))
            norm("g_", rms=True, var_at=0)

            pe.wait_ge(*at("g_out", 1))
            pe.wait_ge(*at("g_pst", 1))
            for p in range(2):
                last = mm(PS[:, 6 + p, 0:T], walpha[:, 128 * p:128 * p + 128], lrT, start=True, stop=True)
            last.then_inc(s("l_alpha"), 1)
            for i in range(3):
                tokens(i, i, 20).then_inc(s("l_vt"), 1)
            pe.wait_ge(*at("l_dqk", 1))
            for i, (a, n) in enumerate(TILES):
                for p in range(2):
                    last = tr(PS[0:n, 3 + i // 2, 256 * (i % 2) + 128 * p:256 * (i % 2) + 128 * p + 128], k2[:, p, a:a + n], 128)
            last.then_inc(s("l_kt"), 1)
            pe.wait_ge(*at("l_tok", 6))
            for h, b in enumerate([5, 6, 7, 0]):
                r = slice(64 * (h % 2), 64 * (h % 2) + 64)
                for a, n in TILES:
                    last = mm(PS[0:n, b, a:a + n], k1[r, h // 2, a:a + n], q1[r, h // 2, a:a + n], start=True, stop=True)
                last.then_inc(s("l_qk"), 1)
            pe.wait_ge(*at("l_vb0", 1))
            for p in range(2):
                if p == 1:
                    pe.wait_ge(*at("l_sc", 1))
                for c in range(4):
                    r = slice(64 * (c % 2), 64 * (c % 2) + 64)
                    mm(PS[:, 1 + c % 2, 256 * (c // 2):256 * (c // 2) + 256], ktl[r, c // 2, 128 * p:128 * p + 128],
                       vtl[r, c // 2, 256 * p:256 * p + 256], start=True, stop=True)
                for q in range(2):
                    last = mm(PS[:, 3, 128 * q:128 * q + 128], ktl[0:R2, 2, 128 * p:128 * p + 128], lvp[0:R2, 2 * p + q, :],
                              start=True, stop=True)
                last.then_inc(s("l_upe"), 1)
            pe.wait_ge(*at("l_sc", 2))
            pe.wait_ge(*at("ld_stG", 32))
            pe.wait_ge(*at("l_att", 4))
            for h in range(H):
                r, p = slice(64 * (h % 2), 64 * (h % 2) + 64), h // 2
                for i in (2, 0, 1):
                    a, n = TILES[i]
                    mm(PS[:, h, a:a + n], vtl[0:n, i, 128 * h:128 * h + 128], attl[0:n, h, a:a + n], start=i == 2, stop=False)
                for c in range(1, 5):
                    n = 64 if c < 4 else PR2
                    mm(PS[:, h, 64 * c:64 * c + n], sc[:, c - 1, p, :], q2[:, h, 64 * c:64 * c + n], start=False, stop=False)
                for b in range(NB):
                    last = mm(PS[:, h, TP + 4 * b:TP + 4 * b + 4], stG[:, 2 * b + p, :], q2[:, h, TP + 4 * b:TP + 4 * b + 4],
                              start=False, stop=b == NB - 1)
                last.then_inc(s("l_o"), 1)
            for h in range(H):
                pe.wait_ge(*at("l_vb", h + 1))
                if h >= 2:
                    pe.wait_ge(*at("l_stu", h - 1))
                for j, b in enumerate([(4, 5), (6, 7)][h % 2]):
                    last = mm(PS[:, b, :], ktl[0:R2, 2, 128 * (h // 2):128 * (h // 2) + 128],
                              lb[h % 2][0:R2, 1 + 4 * j:5 + 4 * j, :].rearrange("p a b -> p (a b)"), start=True, stop=True)
                last.then_inc(s("l_state_pe"), 1)
            pe.wait_ge(*at("l_oev", 1))
            norm("l_", var_at=0)

            pe.wait_ge(*at("l_out", 1))
            group(17, mix)
            group(18, mix)
            layer_norm("n1m_", "proj_ev", 4 * GEND)
            pe.wait_ge(*at("n1m_x", 1))

            pe.wait_ge(*at("ld_router", 32))
            for i, (a, n) in enumerate(TILES):
                for k in range(KT):
                    mm(PS[0:n, 2, 8 * i:8 * i + 8], xT[:, k, a:a + n], wrt[:, k, :], start=k == 0, stop=False)
                last = mm(PS[0:n, 2, 8 * i:8 * i + 8], ones[0:1, 0:n], brt[0:1, :], start=False, stop=True)
            last.then_inc(s("x_log"), 1)
            pe.wait_ge(*at("x_gate", 1))
            for i, (a, n) in enumerate(TILES):
                last = tr(PS[0:8, 3, a:a + n], gate[0:n, i, :], n)
            last.then_inc(s("x_gt"), 1)
            pe.wait_ge(*at("x_gtev", 1))
            for e in range(NE):
                mm(PS[:, e, 0:T], row(e, 8), gT[0:8, :], start=True, stop=True).then_inc(s("x_bc"), 1)
            pe.wait_ge(*at("x_bcev", 2))
            ffn(1)
            layer_norm("n1f_", "f1_down_ev", 4 + NE * KT)
            pe.wait_ge(*at("n1f_x", 1))
            for i, (a, n) in enumerate(TILES):
                for q in range(2):
                    for k in range(4):
                        last = tr(PS[0:n, 2 * i + q, 128 * k:128 * k + 128], xT[:, 4 * q + k, a:a + n], 128)
                    last.then_inc(s("y_pe"), 1)

        @block.scalar
        def _(act):
            A = S_.activation
            chain = [0]

            def link(ins):
                chain[0] += 1
                ins.then_inc(s("act_chain"), 1)
                act.wait_ge(*at("act_chain", chain[0]))

            act.dma_start(cc[:], I["c_common"]).then_inc(s("ld_v"), 16)
            act.dma_start(vrows[0:NVEC, 0:128], I["vec_rows"]).then_inc(s("ld_v"), 16)
            act.dma_start(vrows[0:NCONV, 128:256], I["conv_rows"]).then_inc(s("ld_v"), 16)
            act.dma_start(nload[0:32, :], I["state_mlstm_n"].rearrange("b h d -> (b h) d")).then_inc(s("ld_v"), 16)
            act.dma_start(wsm[:, :, 0:8], I["w_in0"][:, 4096:4104].rearrange("(k p) n -> p k n", p=128)).then_inc(s("ld_wsm"), 16)
            act.dma_start(gates0[0:4, :], I["gate_cols"][:, 0:2]).then_inc(s("ld_r"), 16)
            act.dma_start(m0[0:4, 0:8], I["m_rows"]).then_inc(s("ld_r"), 16)
            act.dma_start(r4[0:4, :], I["c_rows"]).then_inc(s("ld_r"), 16)
            act.dma_start(cst[:, 0:N0], I["c_layer0"]).then_inc(s("ld_c0"), 16)
            act.dma_start(stA[:], I["state_ret"].rearrange("b h d e -> d (b h) e")).then_inc(s("ld_stA"), 16)
            act.dma_start(stB[:], I["state_mlstm_c"].rearrange("b h d e -> d (b h) e")).then_inc(s("ld_stB"), 16)

            for k in range(1, KT, 2):
                act.wait_ge(*at("xt_pe", k + 1))
                A(xT[:, k, :], PS[:, k, 0:T], COPY).then_inc(s("xT"), 1)

            act.wait_ge(*at("m_abs", 1))
            link(A(ROW[5][:, 0:T], ROW[7][:, 0:T], EXP, scale=-1.0))
            A(ROW[5][:, 0:T], ROW[5][:, 0:T], LN, bias=1.0).then_inc(s("m_lse"), 1)

            for g in range(8):
                f = [COPY, COPY, COPY, SILU, COPY, COPY, COPY, SIGM][g]
                for t in range(4):
                    act.wait_ge(*at("proj_pe", 4 * g + t + 1))
                    A(P[:, 4 * g + t, :], PS[:, 4 * (g % 2) + t, 0:T], f, scale=128 ** -0.5 if g == 5 else 1.0).then_inc(s("proj_ev"), 1)

            def norm(p):
                act.wait_ge(*at(p + "cent", 1))
                A(zT[:, 4:8, :], zT[:, 0:4, :], SQR).then_inc(s(p + "sq"), 1)
                act.wait_ge(*at(p + "var", 1))
                link(A(zT[:, 4:8, :], bank4(0), LN, bias=EPS))
                A(zT[:, 4:8, :], zT[:, 4:8, :], EXP, scale=-0.5).then_inc(s(p + "rstd"), 1)

            for i in range(3):
                n = TILES[i][1]
                act.wait_ge(*at("r_vt", i + 1))
                A(vtok[0:n, i, :], PS[0:n, 3 + i, :], COPY).then_inc(s("r_vtok"), 1)
            for i in range(3):
                n = TILES[i][1]
                act.wait_ge(*at("r_kt", i + 1))
                A(ktok[0:n, i, :], PS[0:n, i, :], COPY).then_inc(s("r_ktok"), 1)
            for h, b in enumerate([0, 1, 2, 5]):
                act.wait_ge(*at("r_o", h + 1))
                A(zT[:, h, :], PS[:, b, 0:T], COPY).then_inc(s("r_oev"), 1)
            act.wait_ge(*at("r_state_pe", 4))
            A(pst[:], PS[:, 6, :].rearrange("p (a b) -> p a b", a=4), COPY).then_inc(s("r_pst"), 1)
            norm("r_")

            act.wait_ge(*at("m_rows", 1))
            A(ROW[6], ROW[6], EXP)
            A(ROW[5][:, 0:T], ROW[5][:, 0:T], EXP).then_inc(s("m_exp"), 1)
            act.wait_ge(*at("m_bc", 4))
            A(ebc, PS[:, 4:8, 0:344], COPY).then_inc(s("m_ebc"), 1)
            act.wait_ge(*at("m_col", 1))
            for h in range(H):
                act.wait_ge(*at("m_ex", h + 1))
                A(att[:, h, 0:A1], att[:, h, 0:A1], EXP, bias=mcol[:, h:h + 1])
                A(att[:, h, A1:A2], att[:, h, A1:A2], EXP, bias=mcol[:, 4 + h:5 + h])
                A(att[0:R2, h, A2:ATT], att[0:R2, h, A2:ATT], EXP, bias=mcol[0:R2, 8 + h:9 + h]).then_inc(s("m_w"), 1)
            for n_, (b, i, dst) in enumerate([(4, 0, ktok), (5, 1, ktok), (6, 2, ktok), (7, 0, vtok), (4, 1, vtok), (5, 2, vtok)]):
                n = TILES[i][1]
                act.wait_ge(*at("m_tpe", n_ + 1))
                A(dst[0:n, i, :], PS[0:n, b, :], COPY).then_inc(s("m_tok"), 1)
            act.wait_ge(*at("m_state_pe", 4))
            act.wait_ge(*at("st_rp", 16))
            A(pst[:], PS[:, 6, :].rearrange("p (a b) -> p a b", a=4), COPY).then_inc(s("m_pst"), 1)
            act.wait_ge(*at("m_npe", 1))
            A(nrow[0:36, :], PS[0:36, 0, 0:128], COPY).then_inc(s("m_nrow"), 1)
            norm("m_")

            def layer_norm(p, scaled):
                act.wait_ge(*at(p + "cent", 1))
                A(mix[:], zT[:], SQR).then_inc(s(p + "sq"), 1)
                act.wait_ge(*at(p + "var", 1))
                link(A(mix[:, 1, :], PS[:, 1, 0:T], LN, bias=LN_EPS))
                A(mix[:, 0, :], mix[:, 1, :], EXP, scale=-0.5).then_inc(s(p + "rstd"), 1)
                if scaled:
                    act.wait_ge(*at(p + "x", 1))
                    A(zT[:], xT[:], COPY, scale=ALPHA).then_inc(s(p + "z"), 1)

            def ffn(layer):
                p, E = f"f{layer}_", (FE, NE)[layer]
                with act.Fori(0, E) as e:
                    for j in range(FT):
                        act.wait_ge(*at(p + "hid_pe", e * FT + (j + 5)))
                        A(gact[:, j % 2, :], PS[:, 2 * (j % 2), 0:T], SILU).then_inc(s(p + "silu"), 1)

            layer_norm("n0m_", True)
            ffn(0)
            layer_norm("n0f_", False)

            act.wait_ge(*at("small_pe", 2))
            A(GROW[0][:, 0:T], PS[0:4, 5, 0:T], SIGM).then_inc(s("g_beta"), 1)
            act.wait_ge(*at("g_abs", 1))
            A(gates0[0:4, 0:1], gates0[0:4, 0:1], EXP)
            link(A(GROW[6][:, 0:T], GROW[6][:, 0:T], EXP, scale=-1.0))
            A(GROW[6][:, 0:T], GROW[6][:, 0:T], LN, bias=1.0).then_inc(s("g_lse"), 1)
            act.wait_ge(*at("g_gc", 1))
            A(GROW[3][:, 0:T], GROW[2][:, 0:T], EXP)
            A(GROW[5][:, 0:T], GROW[5][:, 0:T], EXP)
            A(GROW[1][:, 0:11], GROW[2][:, T:T + 11], EXP).then_inc(s("g_eg"), 1)

            act.wait_ge(*at("cin0", 1))

            def conv_out(m):
                act.wait_ge(*at("conv", m + 1))
                A(P[:, m, 0:TP], cacc[:, m % 2, 0:TP], SILU)
                A(smp(P[:, m, :]), cconv(m), SILU).then_inc(s("convs"), 1)

            for g in range(IN1, OUT1):
                for t in range(4):
                    m = 4 * (g - IN1) + t
                    act.wait_ge(*at("proj_pe", 4 * g + t + 1))
                    ps = PS[:, 4 * (g % 2) + t, 0:T]
                    if m < 12:
                        if m >= 4:
                            act.wait_ge(*at("conv", m - 3))
                            act.wait_ge(*at("last", m - 3))
                        A(cin[:, m % 4, 3:3 + TP], ps[:, 0:TP], COPY)
                        A(cins(m)[:, :, 3:7], smp(ps), COPY).then_inc(s("cin"), 1)
                        act.wait_ge(*at("cin", m + 1))
                        act.sem_inc(s("proj_ev"), 1)
                        if m:
                            conv_out(m - 1)
                    else:
                        if m == 12:
                            conv_out(11)
                        f = SILU if m < 16 or m >= 24 else COPY
                        A(P[:, m, :], ps, f, scale=64 ** -0.5 if m in (16, 17) else 1.0).then_inc(s("proj_ev"), 1)

            act.wait_ge(*at("convs", 12))
            A(sqn, P[:, 0:8, :], SQR).then_inc(s("g_sqn"), 1)
            act.wait_ge(*at("last_pe", 1))
            A(lastrow[0:27, :], PS[0:27, 0:3, :], COPY).then_inc(s("last_ev"), 1)
            act.wait_ge(*at("g_l2pe", 1))
            A(sqn, PS[:, 0:8, 0:T], LN, bias=EPS).then_inc(s("g_l2a"), 1)
            act.wait_ge(*at("g_l2a", 1))
            A(sqn[:, 0:4, :], sqn[:, 0:4, :], EXP, scale=-0.5, bias=-0.5 * math.log(128))
            A(sqn[:, 4:8, :], sqn[:, 4:8, :], EXP, scale=-0.5).then_inc(s("g_l2r"), 1)
            act.wait_ge(*at("g_bc", 1))
            A(dbc, PS[:, 0:4, T:T + 11], COPY)
            A(qe, bank4(0), EXP).then_inc(s("g_eq"), 1)
            for h in range(H):
                act.wait_ge(*at("g_dx", h + 1))
                for i, (a, n) in enumerate(TILES):
                    last = A(decI[0:n, h, a:a + n], decI[0:n, h, a:a + n], EXP, bias=gcol[0:n, 2, i, h:h + 1])
                last.then_inc(s("g_dec"), 1)
            for i, (a, n) in enumerate(TILES):
                act.wait_ge(*at("g_kt", i + 1))
                A(ktg[0:n, i, :], PS[0:n, i, :], COPY).then_inc(s("g_tok_a"), 1)
            for i, (a, n) in enumerate(TILES):
                act.wait_ge(*at("g_w", i + 1))
                A(kb[:, :, a:a + n], PS[:, i, 0:4 * n].rearrange("p (a b) -> p a b", a=4), COPY, scale=-1.0).then_inc(s("g_wev"), 1)
            act.wait_ge(*at("st_conv", 32))
            for i, (a, n) in enumerate(TILES):
                act.wait_ge(*at("g_upe", i + 1))
                A(ug[0:n, i, :], PS[0:n, 3, :], COPY).then_inc(s("g_ua"), 1)
            act.wait_ge(*at("g_o", 4))
            A(zT[:, 0:3, :], PS[:, 0:3, 0:T], COPY)
            A(zT[:, 3, :], PS[:, 5, 0:T], COPY).then_inc(s("g_oev"), 1)
            act.wait_ge(*at("g_oev", 1))
            A(zT[:, 4:8, :], zT[:, 0:4, :], SQR).then_inc(s("g_sq"), 1)
            act.wait_ge(*at("g_var", 1))
            link(A(zT[:, 4:8, :], bank4(0), LN, bias=EPS))
            A(zT[:, 4:8, :], zT[:, 4:8, :], EXP, scale=-0.5).then_inc(s("g_rstd"), 1)

            act.wait_ge(*at("l_abs", 1))
            link(A(cb_, cb_, EXP, scale=-1.0))
            A(cb_, cb_, LN, bias=1.0).then_inc(s("l_lse"), 1)
            for i, (a, n) in enumerate(TILES):
                act.wait_ge(*at("l_vt", i + 1))
                A(vtl[0:n, i, :], PS[0:n, i, :], COPY).then_inc(s("l_tok"), 1)
            act.wait_ge(*at("l_x", 1))
            A(e1, cb_, EXP)
            A(e2, cb_, EXP, scale=-1.0)
            A(e3, bc_, EXP)
            A(kx_, kx_, EXP).then_inc(s("l_e"), 1)
            act.wait_ge(*at("l_kt", 1))
            for i in range(3):
                n = TILES[i][1]
                A(ktl[0:n, i, :], PS[0:n, 3 + i // 2, 256 * (i % 2):256 * (i % 2) + 256], COPY).then_inc(s("l_tok"), 1)
            act.wait_ge(*at("l_o", 4))
            A(zT[:, 0:4, :], bank4(0), COPY).then_inc(s("l_oev"), 1)
            norm("l_")

            layer_norm("n1m_", True)
            act.wait_ge(*at("x_lm", 1))
            A(lt, lt, EXP).then_inc(s("x_exp"), 1)
            act.wait_ge(*at("x_bc", 8))
            A(gbc[:, 0:4, :], bank4(0), COPY).then_inc(s("x_bcev"), 1)
            ffn(1)
            layer_norm("n1f_", False)
            for n_ in range(1, 6, 2):
                i, q = n_ // 2, n_ % 2
                n = TILES[i][1]
                act.wait_ge(*at("y_pe", n_ + 1))
                A(proj[0:n, 1024 * i + 512 * q:1024 * i + 512 * q + 512], PS[0:n, n_, :], COPY).then_inc(s("y_ev"), 1)

        @block.gpsimd
        def _(pool):
            pool.wait_ge(*at("ld_c0", 16))
            pool.wait_ge(*at("rot", 1))
            cos = const(C0, "cos").rearrange("p (a b) -> p a b", a=2)
            for a in range(2):
                q = P[:, 4 * a:4 * a + 4, :]
                G.tensor_tensor(q, q, cos[:, a:a + 1, :].to_broadcast([128, 4, T]), MUL).then_inc(s("ropec"), 1)

            def out_state(p, st, dram_s, dram_p):
                for h in range(H):
                    pool.wait_ge(*at(p + "stu", h + 1))
                    pool.dma_start(dram_s[:, h].rearrange("b d e -> d b e"), st[:, h::4, :]).then_inc(s("st_all"), 16)
                pool.wait_ge(*at(p + "pst", 1))
                pool.dma_start(dram_p.rearrange("h d e -> d h e"), pst[:]).then_inc(s("st_" + p[0] + "p"), 16)

            pool.wait_ge(*at("r_vtok", 3))
            gk = const(C0, "gk").rearrange("p (a b) -> p a b", a=2)
            gk2 = const(C0, "gk2").rearrange("p (a b) -> p a b", a=4)
            for i in range(2):
                last = G.tensor_tensor(vd[:, i], vtok[:, i, :].rearrange("p (a b) -> p a b", a=4),
                                       gk[:, i, :].unsqueeze(2).to_broadcast([128, 4, 128]), MUL)
            last.then_inc(s("r_vd"), 1)
            for h in range(H):
                if h >= 2:
                    pool.wait_ge(*at("r_state_pe", h - 1))
                G.tensor_tensor(vb[h % 2][0:R2], vtok[0:R2, 2, 128 * h:128 * h + 128].unsqueeze(1).to_broadcast([R2, SEGS, 128]),
                                gk2[0:R2, h, :].unsqueeze(2).to_broadcast([R2, SEGS, 128]), MUL).then_inc(s("r_vb"), 1)
            out_state("r_", stA, O["sample_ret"], O["prompt_ret"][0])

            pool.wait_ge(*at("m_wl2", 1))
            pool.wait_ge(*at("m_tok", 6))
            for i in range(2):
                last = G.tensor_tensor(vd[:, i], vtok[:, i, :].rearrange("p (a b) -> p a b", a=4),
                                       mcol[:, 12 + 4 * i:16 + 4 * i].unsqueeze(2).to_broadcast([128, 4, 128]), MUL)
            last.then_inc(s("m_vd"), 1)
            for h in range(H):
                if h >= 2:
                    pool.wait_ge(*at("m_state_pe", h - 1))
                G.tensor_tensor(vb[h % 2][0:R2], vtok[0:R2, 2, 128 * h:128 * h + 128].unsqueeze(1).to_broadcast([R2, SEGS, 128]),
                                wl2[0:R2, h, :].unsqueeze(2).to_broadcast([R2, SEGS, 128]), MUL).then_inc(s("m_vb"), 1)
            out_state("m_", stB, O["sample_c"], O["prompt_c"][0])
            pool.wait_ge(*at("m_nrow", 1))
            pool.dma_start(O["sample_n"].rearrange("b h d -> (b h) d"), nrow[0:32, :]).then_inc(s("st_all"), 16)
            pool.dma_start(O["prompt_n"].rearrange("b h d -> (b h) d"), nrow[32:36, :]).then_inc(s("st_all"), 16)
            pool.wait_ge(*at("m_mt", 1))
            pool.dma_start(O["m_rows"], m0[0:4, 0:9]).then_inc(s("st_all"), 16)

            pool.wait_ge(*at("m_out", 1))
            pool.dma_start(cst[:, 0:N1], I["c_layer1"]).then_inc(s("ld_l1"), 16)
            pool.dma_start(gates0[0:4, :], I["gate_cols"][:, 2:4]).then_inc(s("ld_l1"), 16)
            pool.dma_start(wsm[:, :, 0:8], I["w_in1"][:, 2048:2056].rearrange("(k p) n -> p k n", p=128)).then_inc(s("ld_l1"), 16)
            pool.dma_start(wsm[:, :, 8:24], I["w_in1"][:, 3592:3608].rearrange("(k p) n -> p k n", p=128)).then_inc(s("ld_l1"), 16)
            pool.dma_start(walpha, I["gla_w_alpha"]).then_inc(s("ld_l1"), 16)
            pool.wait_ge(*at("st_all", 16 * 11))
            pool.wait_ge(*at("st_rp", 16))
            pool.wait_ge(*at("st_mp", 16))
            pool.dma_start(stA[:], I["state_gdn"].rearrange("b h d e -> d (b h) e")).then_inc(s("ld_gdn"), 16)
            pool.dma_start(r4b[0:4, :], I["c_rows"]).then_inc(s("ld_gdn"), 16)
            pool.wait_ge(*at("f0_down_pe", 4 + FE * KT))
            pool.dma_start(dring[0:24, 0:1536], I["state_gdn_conv"].rearrange("b w c -> (b w) c")).then_inc(s("ld_halo"), 16)

            for m in range(12):
                pool.wait_ge(*at("cin", m + 1))
                G.tensor_copy(lastT[:, m, 0:3], cin[:, m % 4, TP:TP + 3])
                G.tensor_copy(lastT[:, m, 3:27].rearrange("p (b t) -> p b t", b=NB), cins(m)[:, :, 4:7]).then_inc(s("last"), 1)
            pool.wait_ge(*at("last_ev", 1))
            pool.dma_start(O["prompt_conv"][0], lastrow[0:3, :]).then_inc(s("st_conv"), 16)
            pool.dma_start(O["sample_conv"].rearrange("b w c -> (b w) c"), lastrow[3:27, :]).then_inc(s("st_conv"), 16)

            pool.wait_ge(*at("g_ue", 3))
            blk = const(C1, "blk")
            for h in range(H):
                if h >= 2:
                    pool.wait_ge(*at("g_state_pe", h - 1))
                G.tensor_tensor(ub[h % 2][0:R2], rhsk[0:R2, 2, 128 * h:128 * h + 128].unsqueeze(1).to_broadcast([R2, SEGS, 128]),
                                blk[0:R2].unsqueeze(2).to_broadcast([R2, SEGS, 128]), MUL).then_inc(s("g_vb"), 1)
            pool.wait_ge(*at("g_upe", 3))
            for r in range(2):
                pool.dma_start(stG[64 * r:64 * r + 64], I["state_gla"][:, r::2].rearrange("b p d e -> d b p e")).then_inc(s("ld_stG"), 16)
            for h in range(H):
                pool.wait_ge(*at("g_stu", h + 1))
                pool.dma_start(O["sample_gdn"][:, h].rearrange("b d e -> d b e"), stA[:, h::4, :]).then_inc(s("st_all"), 16)
            pool.wait_ge(*at("g_pst", 1))
            pool.dma_start(O["prompt_gdn"][0].rearrange("h d e -> d h e"), sg[:, 2]).then_inc(s("st_gp"), 16)

            pool.wait_ge(*at("l_tok", 3))
            last = G.tensor_tensor(lvp[0:R2], vtl[0:R2, 2, :].rearrange("p (a b) -> p a b", a=4),
                                   blk[0:R2, 0:1].unsqueeze(2).to_broadcast([R2, 4, 128]), MUL)
            last.then_inc(s("l_vb0"), 1)
            for h in range(H):
                if h >= 2:
                    pool.wait_ge(*at("l_state_pe", h - 1))
                G.tensor_tensor(lb[h % 2][0:R2], vtl[0:R2, 2, 128 * h:128 * h + 128].unsqueeze(1).to_broadcast([R2, SEGS, 128]),
                                blk[0:R2].unsqueeze(2).to_broadcast([R2, SEGS, 128]), MUL).then_inc(s("l_vb"), 1)
            pool.wait_ge(*at("l_sc", 2))
            for r in range(2):
                pool.dma_start(O["prompt_gla"][0, r::2].rearrange("p d e -> d p e"), sc[64 * r:64 * r + 64, 4]).then_inc(s("st_all"), 16)
            pool.wait_ge(*at("l_stu", 4))
            for r in range(2):
                pool.dma_start(O["sample_gla"][:, r::2].rearrange("b p d e -> d b p e"), stG[64 * r:64 * r + 64]).then_inc(s("st_all"), 16)
            pool.wait_ge(*at("l_out", 1))
            pool.dma_start(wrt, I["moe_w_router"].rearrange("(k p) n -> p k n", p=128)).then_inc(s("ld_router"), 16)
            pool.dma_start(brt[0:1, :], I["moe_b_router"].rearrange("(a n) -> a n", a=1)).then_inc(s("ld_router"), 16)
            pool.wait_ge(*at("st_all", 16 * 19))
            pool.wait_ge(*at("st_gp", 16))
            pool.wait_ge(*at("st_conv", 32))

        @block.vector
        def _(dve):
            TT, TSC, STT, CP = V.tensor_tensor, V.tensor_scalar, V.scalar_tensor_tensor, V.tensor_copy
            chain = [0]

            def link(ins):
                chain[0] += 1
                ins.then_inc(s("dve_chain"), 1)
                dve.wait_ge(*at("dve_chain", chain[0]))

            for k in range(0, KT, 2):
                dve.wait_ge(*at("xt_pe", k + 1))
                CP(xT[:, k, :], PS[:, k, 0:T]).then_inc(s("xT"), 1)
            dve.wait_ge(*at("vec_pe", 1))
            CP(vec[:, 0:NVEC], PS[:, 0, 0:NVEC])
            CP(vec[:, NVEC:NVEC + NCONV], PS[:, 0, 128:128 + NCONV])
            CP(nT[:, 0:32], PS[:, 0, 256:288]).then_inc(s("vec_ev"), 1)

            f, i_, b_, a_, M = ROW[1][:, 0:T], ROW[0][:, 0:T], ROW[2][:, 0:T], ROW[3][:, 0:T], ROW[4][:, 0:T]
            ab, l_, pk = ROW[7][:, 0:T], ROW[5][:, 0:T], ROW[6]
            dve.wait_ge(*at("small_pe", 1))
            dve.wait_ge(*at("ld_r", 48))
            TSC(i_, PS[0:4, 6, 0:T], gates0[0:4, 0:1], None, ADD)
            link(TSC(f, PS[0:4, 7, 0:T], gates0[0:4, 1:2], None, ADD))
            STT(ab, f, -1.0, f, MUL, MAX).then_inc(s("m_abs"), 1)
            dve.sem_inc(s("small_ev"), 1)
            dve.wait_ge(*at("m_lse", 1))
            link(STT(f, f, 0.0, l_, MIN, SUB))
            link(V.tensor_tensor_scan(b_, r4[0:4, 0:T], f, 0.0, MUL, ADD))
            link(TT(a_, i_, b_, SUB))
            link(CP(ab, a_))
            link(TSC(ab[:, 0:1], ab[:, 0:1], 0.0, None, MAX))
            link(TT(smp(ab)[:, :, 0], smp(ab)[:, :, 0], m0[0:4, 0:8], MAX))
            link(V.tensor_tensor_scan(M, r4[0:4, T:2 * T], ab, 0.0, ADD, MAX))
            STT(pk[:, 0:T], b_, -1.0, M, MUL, SUB)
            TT(pk[:, T:T + TS].rearrange("p (b t) -> p b t", b=NB), m0[0:4, 0:8].unsqueeze(2).to_broadcast([4, NB, NS]), smp(M), SUB)
            TT(pk[:, T + TS:T + TS + NB], m0[0:4, 0:8], smp(M)[:, :, NS - 1], SUB)
            TSC(l_[:, 0:TP], a_[:, 0:TP], M[:, TP - 1:TP], None, SUB)
            link(TT(smp(l_), smp(a_), smp(M)[:, :, NS - 1:NS].to_broadcast([4, NB, NS]), SUB))
            link(STT(m0[0:4, 0:8], smp(b_)[:, :, NS - 1], 0.0, smp(M)[:, :, NS - 1], ADD, ADD))
            TT(m0[0:4, 8:9], b_[:, TP - 1:TP], M[:, TP - 1:TP], ADD).then_inc(s("m_mt"), 1)
            dve.sem_inc(s("m_rows"), 1)

            def norm(p, dst, gate0, gain, rms=False):
                if not rms:
                    dve.wait_ge(*at(p + "mean", 1))
                    TT(zT[:, 0:4, :], zT[:, 0:4, :], bank4(0), SUB).then_inc(s(p + "cent"), 1)
                dve.wait_ge(*at(p + "rstd", 1))
                link(TT(zT[:, 0:4, :], zT[:, 0:4, :], zT[:, 4:8, :], MUL))
                for h in range(H):
                    g = vec[:, VEC[gain] + h:VEC[gain] + h + 1]
                    if gate0 is None:
                        last = TSC(mix[:, dst + h, :], zT[:, h, :], g, None, MUL)
                    else:
                        last = STT(mix[:, dst + h, :], zT[:, h, :], g, P[:, gate0 + h, :], MUL, MUL)
                last.then_inc(s(p + "out"), 1)

            def state_update(p, st, h, banks, decay):
                v = st[:, h::4, :]
                if decay is None:
                    for j, b in enumerate(banks):
                        last = STT(v[:, 4 * j:4 * j + 4, :], v[:, 4 * j:4 * j + 4, :], math.exp(4 * math.log(1 - 2.0 ** (-5 - h))),
                                   PS[:, b, :].rearrange("p (a b) -> p a b", a=4), MUL, ADD)
                else:
                    link(TT(v, v, decay.unsqueeze(2).to_broadcast([128, NB, 128]), MUL))
                    for j, b in enumerate(banks):
                        last = TT(v[:, 4 * j:4 * j + 4, :], v[:, 4 * j:4 * j + 4, :], PS[:, b, :].rearrange("p (a b) -> p a b", a=4), ADD)
                last.then_inc(s(p + "stu"), 1)

            dve.wait_ge(*at("ld_c0", 16))
            dve.wait_ge(*at("rot", 1))
            sin = const(C0, "sin").rearrange("p (a b) -> p a b", a=2)
            for a in range(2):
                last = TT(zT[:, 4 * a:4 * a + 4, :], bank4(4 * a), sin[:, a:a + 1, :].to_broadcast([128, 4, T]), MUL)
            link(last)
            dve.sem_inc(s("rotm"), 1)
            dve.wait_ge(*at("ropec", 2))
            link(TT(P[:, 0:8, :], P[:, 0:8, :], zT[:], ADD))
            dve.sem_inc(s("rope"), 1)
            TT(qs, P[:, 0:4, TP:T], const(C0, "gq").rearrange("p (a b) -> p a b", a=4), MUL).then_inc(s("r_qs"), 1)
            dec = const(C0, "dec").rearrange("p (a b) -> p a b", a=4)
            for h, b in enumerate([6, 7, 3, 4]):
                dve.wait_ge(*at("r_qk", h + 1))
                TT(att[:, h, 0:A2], PS[:, b, 0:A2], dec[:, h, 0:A2], MUL)
                TT(att[0:R2, h, A2:ATT], PS[0:R2, b, A2:ATT], dec[0:R2, h, A2:ATT], MUL).then_inc(s("r_att"), 1)
            for h in range(H):
                dve.wait_ge(*at("r_state_pe", h + 1))
                state_update("r_", stA, h, [(7, 3), (4, 5)][h % 2], None)
            norm("r_", 0, 12, "ret")

            mask = const(C0, "mask")
            dve.wait_ge(*at("m_colpe", 1))
            CP(mcol[:, 0:8], PS[:, 7, 0:8])
            CP(mcol[0:R2, 8:12], PS[0:R2, 7, 8:12])
            CP(mcol[:, 12:20], PS[:, 7, 12:20])
            link(CP(mcol[0:R2, 20:24], PS[0:R2, 7, 20:24]))
            dve.sem_inc(s("m_col"), 1)
            TT(wl2[0:R2], mcol[0:R2, 20:24].unsqueeze(2).to_broadcast([R2, 4, 9]), const(C0, "blk")[0:R2].unsqueeze(1).to_broadcast([R2, 4, 9]),
               MUL).then_inc(s("m_wl2"), 1)
            for h in range(H):
                dve.wait_ge(*at("m_bc", h + 1))
                TT(att[:, h, 0:A1], mask[:, 0:A1], PS[:, h, 0:TP], SUB)
                TT(att[:, h, A1:A2], mask[:, A1:A2], PS[:, h, 128:TP], SUB)
                TT(att[0:R2, h, A2:ATT], mask[0:R2, A2:ATT], PS[0:R2, h, 256:T], SUB).then_inc(s("m_ex"), 1)
            dve.wait_ge(*at("m_ebc", 1))
            TT(qs, P[:, 16:20, TP:T], ebc[:, :, T:T + TS], MUL).then_inc(s("m_qs"), 1)
            for h in range(H):
                dve.wait_ge(*at("m_qk", h + 1))
                dve.wait_ge(*at("m_w", h + 1))
                TT(att[:, h, 0:A2], PS[:, h, 0:A2], att[:, h, 0:A2], MUL)
                TT(att[0:R2, h, A2:ATT], PS[0:R2, h, A2:ATT], att[0:R2, h, A2:ATT], MUL).then_inc(s("m_att"), 1)
            dve.wait_ge(*at("m_o", 4))
            o, d = zT[:, 0:4, :], zT[:, 4:8, :]
            link(TT(d, bank4(4), ebc[:, :, 0:T], MAX))
            link(STT(d, bank4(4), -1.0, d, MUL, MAX))
            link(V.reciprocal(d, d))
            link(TT(d, d, P[:, 28:32, :], MUL))
            TT(o, bank4(0), d, MUL).then_inc(s("m_oev"), 1)
            for h in range(H):
                dve.wait_ge(*at("m_state_pe", h + 1))
                state_update("m_", stB, h, [(7, 3), (4, 2)][h % 2], ebc[:, h, T + TS:T + TS + NB])
                n = nT[:, h:32:4]
                link(TT(n, n, ebc[:, h, T + TS:T + TS + NB], MUL))
                TT(n, n, PS[:, 5, 9 * h + 1:9 * h + 9], ADD)
                last = CP(nT[:, 32 + h:33 + h], PS[:, 5, 9 * h:9 * h + 1])
            last.then_inc(s("m_nst"), 1)
            norm("m_", 4, None, "mlstm")

            def residual(g0):
                for g in range(g0, g0 + 2):
                    for t in range(4):
                        k = 4 * (g - g0) + t
                        dve.wait_ge(*at("proj_pe", 4 * g + t + 1))
                        STT(zT[:, k, :], xT[:, k, :], ALPHA, PS[:, 4 * (g % 2) + t, 0:T], MUL, ADD).then_inc(s("proj_ev"), 1)

            def layer_norm(p, gain):
                dve.wait_ge(*at(p + "mean", 1))
                TT(zT[:], zT[:], PS[:, 0:1, 0:T].to_broadcast([128, KT, T]), SUB).then_inc(s(p + "cent"), 1)
                dve.wait_ge(*at(p + "rstd", 1))
                link(TT(zT[:], zT[:], mix[:, 0:1, :].to_broadcast([128, KT, T]), MUL))
                for k in range(KT):
                    g = VEC[gain + "_g"] + k
                    last = TSC(xT[:, k, :], zT[:, k, :], vec[:, g:g + 1], vec[:, g + 8:g + 9], MUL, ADD)
                last.then_inc(s(p + "x"), 1)

            def ffn(layer):
                p, E = f"f{layer}_", (FE, NE)[layer]
                dve.sem_inc(s(p + "hid_ev"), 1)
                dve.sem_inc(s(p + "down_ev"), 4)
                with dve.Fori(0, E) as e:
                    for j in range(FT):
                        dve.wait_ge(*at(p + "silu", e * FT + j + 1))
                        if layer == 0:
                            TT(hid[:, j, :], gact[:, j % 2, :], PS[:, 2 * (j % 2) + 1, 0:T], MUL).then_inc(s(p + "hid_ev"), 1)
                        else:
                            TT(gtmp[:, j % 2, :], gact[:, j % 2, :], PS[:, 2 * (j % 2) + 1, 0:T], MUL).then_inc(s(p + "gu"), 1)
                            dve.wait_ge(*at(p + "gu", e * FT + j + 1))
                            TT(hid[:, j, :], gtmp[:, j % 2, :], gbc[:, e, :], MUL).then_inc(s(p + "hid_ev"), 1)
                    for d in range(KT):
                        dve.wait_ge(*at(p + "down_pe", e * KT + (d + 5)))
                        TT(zT[:, d, :], zT[:, d, :], PS[:, 4 + d % 4, 0:T], ADD).then_inc(s(p + "down_ev"), 1)

            residual(8)
            layer_norm("n0m_", "mix0")
            dve.wait_ge(*at("n0m_z", 1))
            ffn(0)
            layer_norm("n0f_", "ffn0")

            V.memset(cin[:, :, 0:3], 0.0)
            dve.wait_ge(*at("halo_pe", 1))
            link(CP(convT, PS[:, 4, 0:288].rearrange("p (a b) -> p a b", a=12)))
            dve.sem_inc(s("cin0"), 1)
            x_, tmp, gc = GROW[1][:, 0:T], GROW[6][:, 0:T], GROW[2]
            dve.wait_ge(*at("small_pe", 2))
            dve.wait_ge(*at("ld_l1", 80))
            dve.wait_ge(*at("ld_gdn", 32))
            CP(lrT, PS[0:16, 7, 0:T])
            link(TSC(x_, PS[0:4, 6, 0:T], gates0[0:4, 1:2], None, ADD))
            STT(tmp, x_, -1.0, x_, MUL, MAX).then_inc(s("g_abs"), 1)
            dve.wait_ge(*at("g_beta", 1))
            dve.sem_inc(s("small_ev"), 1)
            dve.wait_ge(*at("g_lse", 1))
            link(STT(x_, x_, 0.0, tmp, MAX, ADD))
            link(TSC(x_, x_, gates0[0:4, 0:1], -1.0, MUL, MUL))
            link(V.tensor_tensor_scan(gc[:, 0:T], r4b[0:4, 2 * T:3 * T], x_, 0.0, MUL, ADD))
            CP(gc[:, T:T + 2], gc[:, 127:256:128])
            CP(gc[:, T + 2:T + 3], gc[:, TP - 1:TP])
            CP(gc[:, T + 3:T + 11], smp(gc)[:, :, NS - 1])
            TSC(GROW[4][:, 0:T], gc[:, 0:T], -1.0, None, MUL)
            for a, n in [(0, 128), (128, 128), (256, PR2)]:
                TSC(GROW[5][:, a:a + n], gc[:, a:a + n], -1.0, gc[:, a + n - 1:a + n], MUL, ADD)
            TT(smp(GROW[5]), smp(gc)[:, :, NS - 1:NS].to_broadcast([4, NB, NS]), smp(gc), SUB).then_inc(s("g_gc"), 1)
            dve.wait_ge(*at("g_eg", 1))
            TT(GROW[3][:, 0:T], GROW[3][:, 0:T], GROW[0][:, 0:T], MUL)
            CP(gc[:, T:T + 11], GROW[1][:, 0:11]).then_inc(s("g_rows"), 1)

            n_ = CONVW - 3
            for m in range(12):
                if m >= 4:
                    dve.wait_ge(*at("conv", m - 3))
                    dve.wait_ge(*at("last", m - 3))
                dve.wait_ge(*at("cin", m + 1))
                link(CP(cins(m)[:, :, 0:3], convT[:, m, :].rearrange("p (b t) -> p b t", b=NB)))
                if m >= 2:
                    dve.wait_ge(*at("convs", m - 1))
                w = [vec[:, NVEC + 12 * j + m:NVEC + 12 * j + m + 1] for j in range(4)]
                acc, src = cacc[:, m % 2, 0:n_], cin[:, m % 4, :]
                link(TSC(acc, src[:, 0:n_], w[0], None, MUL))
                link(STT(acc, src[:, 1:1 + n_], w[1], acc, MUL, ADD))
                link(STT(acc, src[:, 2:2 + n_], w[2], acc, MUL, ADD))
                STT(acc, src[:, 3:3 + n_], w[3], acc, MUL, ADD).then_inc(s("conv"), 1)

            dve.wait_ge(*at("g_l2r", 1))
            link(TT(P[:, 0:8, :], P[:, 0:8, :], sqn, MUL))
            dve.sem_inc(s("g_qk_n"), 1)
            dve.wait_ge(*at("g_colpe", 1))
            CP(gcol[:, :, 0:2, :], PS[:, 0, 0:48].rearrange("p (a b c) -> p a b c", a=4, b=3)[:, :, 0:2, :])
            CP(gcol[0:R2, :, 2, :], PS[0:R2, 0, 0:48].rearrange("p (a b c) -> p a b c", a=4, b=3)[:, :, 2, :]).then_inc(s("g_col"), 1)
            dve.wait_ge(*at("g_bc", 1))
            dve.wait_ge(*at("g_eq", 1))
            incl, strict = const(C1, "incl"), const(C1, "strict")
            for h in range(H):
                TT(decI[:, h, 0:256], PS[:, h, 0:256], incl[:, 0:256], ADD)
                TT(decI[0:R2, h, 256:T], PS[0:R2, h, 256:T], incl[0:R2, 256:T], ADD).then_inc(s("g_dx"), 1)
            dve.wait_ge(*at("g_dx", 4))
            dve.sem_inc(s("g_bcev"), 1)
            TT(kb, P[:, 4:8, :], bank4(4), MUL).then_inc(s("g_kb"), 1)
            TT(qe, qe, P[:, 0:4, :], MUL).then_inc(s("g_qe"), 1)

            def parts(v):
                return [v[:, :, 0:256], v[0:R2, :, 256:T]]

            def maskb(name):
                v = const(C1, name)
                return [v[:, 0:256].unsqueeze(1).to_broadcast([128, H, 256]), v[0:R2, 256:T].unsqueeze(1).to_broadcast([R2, H, R2])]

            dve.wait_ge(*at("g_aa", 4))
            dve.wait_ge(*at("g_dec", 4))
            for v, p_, d_ in zip(parts(SDT), parts(bank4(0)), parts(decI)):
                last = TT(v, p_, d_, MUL)
            link(last)
            for v, m_ in zip(parts(SDT), maskb("strict")):
                last = TT(v, v, m_, MUL)
            last.then_inc(s("g_at"), 1)
            dve.wait_ge(*at("g_qk", 4))
            for v, p_, d_ in zip(parts(attg), parts(bank4(4)), parts(decI)):
                last = TT(v, p_, d_, MUL)
            last.then_inc(s("g_att"), 1)

            def scaled_tokens(dst, i, bank, col):
                n = TILES[i][1]
                return TT(dst[0:n, i, :].rearrange("p (a b) -> p a b", a=4), PS[0:n, bank, :].rearrange("p (a b) -> p a b", a=4),
                          gcol[0:n, col, i, :].unsqueeze(2).to_broadcast([n, 4, 128]), MUL)

            dve.wait_ge(*at("g_tok_a", 3))
            for i in range(3):
                scaled_tokens(rhsk, i, i, 1).then_inc(s("g_tok_d"), 1)
            for i in range(3):
                dve.wait_ge(*at("g_vt", i + 1))
                scaled_tokens(rhsv, i, 4 + i, 0).then_inc(s("g_tok_d"), 1)

            def tile(v, i):
                a, n = TILES[i]
                return v[0:n, :, a:a + n]

            def tmask(name, i):
                a, n = TILES[i]
                return const(C1, name)[0:n, a:a + n].unsqueeze(1).to_broadcast([n, H, n])

            for n_, (k, i) in enumerate(ORDER):
                what, out, lhs, rhs, _ = SOLVE[k]
                n = TILES[i][1]
                dve.wait_ge(*at("sv_pe", n_ + 1))
                ps = PS[0:n, n_ % 8, 0:4 * n].rearrange("p (a b) -> p a b", a=4)
                if what == "split":
                    TT(tile(SD, i), ps, tmask("same8", i), MUL)
                    link(TT(tile(SDT, i), tile(SDT, i), tmask("same8", i), MUL))
                    TT(tile(SO, i), ps, tile(SD, i), SUB)
                    TT(tile(SRT, i), tmask("eye", i), tile(SDT, i), SUB).then_inc(s("sv_ev"), 1)
                elif what == "add":
                    TT(tile(out, i), tile(out, i), ps, ADD).then_inc(s("sv_ev"), 1)
                else:
                    last = CP(tile(out, i), ps)
                    if what == "copyz":
                        last = TT(tile(SO, i), tmask("eye", i), ps, SUB)
                    last.then_inc(s("sv_ev"), 1)

            dve.wait_ge(*at("g_wev", 3))
            for h in range(H):
                last = TT(wtm[:, h], kb[:, h:h + 1, 256:T].to_broadcast([128, SEGS, R2]),
                          const(C1, "seg9").rearrange("p (a b) -> p a b", a=SEGS), MUL)
            last.then_inc(s("g_wtm"), 1)
            for i in range(3):
                dve.wait_ge(*at("g_upe", i + 1))
                dve.wait_ge(*at("g_ua", i + 1))
                scaled_tokens(rhsk, i, 3, 3).then_inc(s("g_ue"), 1)
                if i == 0:
                    dve.wait_ge(*at("g_spe", 1))
                    CP(sg[:, 0], PS[:, 5, :].rearrange("p (a b) -> p a b", a=4)).then_inc(s("g_s"), 1)
                if i == 1:
                    dve.wait_ge(*at("g_spe", 2))
                    for h in range(H):
                        last = STT(sg[:, 1, h, :], sg[:, 0, h, :], dbc[:, h, 1:2], PS[:, 5, 128 * h:128 * h + 128], MUL, ADD)
                    last.then_inc(s("g_s"), 1)
            for h in range(H):
                dve.wait_ge(*at("g_state_pe", h + 1))
                state_update("g_", stA, h, [(7, 3), (4, 5)][h % 2], dbc[:, h, 3:11])
            for h in range(H):
                last = STT(sg[:, 2, h, :], sg[:, 1, h, :], dbc[:, h, 2:3], PS[:, 6, 128 * h:128 * h + 128], MUL, ADD)
            last.then_inc(s("g_pst"), 1)
            norm("g_", 0, 12, "gdn", rms=True)

            dve.wait_ge(*at("l_alpha", 1))
            dve.wait_ge(*at("g_stu", 4))
            for p in range(2):
                last = TSC(bc_[:, p, :], PS[:, 6 + p, 0:T], vec[:, VEC["balpha"] + p:VEC["balpha"] + p + 1], None, ADD)
            link(last)
            STT(cb_, bc_, -1.0, bc_, MUL, MAX).then_inc(s("l_abs"), 1)
            dve.wait_ge(*at("l_lse", 1))
            link(STT(bc_, bc_, 0.0, cb_, MIN, SUB))
            link(TSC(kx_, bc_, 1.0 / 16.0, None, MUL))
            for p in range(2):
                last = V.tensor_tensor_scan(bc_[:, p, :], const(C1, "rst"), kx_[:, p, :], 0.0, MUL, ADD)
            link(last)
            for p in range(2):
                for v, n, k, mid in ((slice(0, 256), 64, 4, 31), (slice(256, TP), PR2, 1, 7), (slice(TP, T), NS, NB, 1)):
                    x4 = bc_[:, p, v].rearrange("p (c t) -> p c t", t=n)
                    TT(cb_[:, p, v].rearrange("p (c t) -> p c t", t=n), x4, x4[:, :, mid:mid + 1].to_broadcast([128, k, n]), SUB)
                    last = TT(kx_[:, p, v].rearrange("p (c t) -> p c t", t=n), x4[:, :, n - 1:n].to_broadcast([128, k, n]), x4, SUB)
            last.then_inc(s("l_x"), 1)
            dve.wait_ge(*at("l_e", 1))
            TT(q1, P[:, 16:18, :], e1, MUL)
            TT(k1, P[:, 18:20, :], e2, MUL)
            link(TT(k2, P[:, 18:20, :], kx_, MUL))
            V.memset(q2[64:128, 0:4:2, :], 0.0)
            link(V.memset(q2[0:64, 1:4:2, :], 0.0))
            for h in range(H):
                r = slice(64 * (h % 2), 64 * (h % 2) + 64)
                last = TT(q2[r, h, :], P[r, 16 + h // 2, :], e3[r, h // 2, :], MUL)
            last.then_inc(s("l_dqk"), 1)
            for h, b in enumerate([5, 6, 7, 0]):
                dve.wait_ge(*at("l_qk", h + 1))
                if h == 0:
                    dve.wait_ge(*at("st_gp", 16))
                gm = const(C1, "gla")
                TT(attl[:, h, 0:256], PS[:, b, 0:256], gm[:, 0:256], MUL)
                TT(attl[0:R2, h, 256:T], PS[0:R2, b, 256:T], gm[0:R2, 256:T], MUL).then_inc(s("l_att"), 1)
            for p in range(2):
                dve.wait_ge(*at("l_upe", p + 1))
                for c in range(5):
                    for q in range(2):
                        r = slice(64 * q, 64 * q + 64)
                        u = PS[r, 3, 128 * q:128 * q + 128] if c == 4 else PS[r, 1 + c % 2, 256 * (c // 2) + 128 * q:256 * (c // 2) + 128 * q + 128]
                        end = 64 * c + 63 if c < 4 else TP - 1
                        if c == 0:
                            last = CP(sc[r, 0, p, :], u)
                        else:
                            last = STT(sc[r, c, p, :], sc[r, c - 1, p, :], e3[r, p, end:end + 1], u, MUL, ADD)
                    link(last)
                dve.sem_inc(s("l_sc"), 1)
            for h in range(H):
                r, p = slice(64 * (h % 2), 64 * (h % 2) + 64), h // 2
                dve.wait_ge(*at("l_state_pe", h + 1))
                v = stG[r, p::2, :]
                link(TT(v, v, smp(e3[r, p, :])[:, :, NS - 1:NS].to_broadcast([64, NB, 128]), MUL))
                for j, b in enumerate([(4, 5), (6, 7)][h % 2]):
                    last = TT(v[:, 4 * j:4 * j + 4, :], v[:, 4 * j:4 * j + 4, :], PS[r, b, :].rearrange("p (a b) -> p a b", a=4), ADD)
                last.then_inc(s("l_stu"), 1)
            norm("l_", 4, 24, "gla")

            residual(17)
            layer_norm("n1m_", "mix1")

            link(V.memset(lt, 0.0))
            dve.wait_ge(*at("x_log", 1))
            CP(lt[:, 0:2, :], PS[:, 2, 0:16].rearrange("p (a b) -> p a b", a=2))
            link(CP(lt[0:R2, 2, :], PS[0:R2, 2, 16:24]))
            link(V.tensor_reduce(st3[:, :, 0], lt, AX.X, MAX))
            TT(lt, lt, st3[:, :, 0:1].to_broadcast([128, 3, NE]), SUB).then_inc(s("x_lm"), 1)
            dve.wait_ge(*at("x_exp", 1))
            link(V.tensor_reduce(st3[:, :, 1], lt, AX.X, ADD))
            link(V.reciprocal(st3[:, :, 2], st3[:, :, 1]))
            link(TT(lt, lt, st3[:, :, 2:3].to_broadcast([128, 3, NE]), MUL))
            for i in range(3):
                other = lt[:, i:i + 1, :].to_broadcast([128, NE, NE])
                own = lt[:, i, :].unsqueeze(2).to_broadcast([128, NE, NE])
                TT(gcmp[:, i, :].rearrange("p (a b) -> p a b", a=NE), other, own, ALU.is_gt)
                last = TT(geq[:, i, :].rearrange("p (a b) -> p a b", a=NE), other, own, ALU.is_equal)
            link(last)
            link(TT(geq, geq, const(C1, "tri").unsqueeze(1).to_broadcast([128, 3, 64]), MUL))
            link(TT(gcmp, gcmp, geq, ADD))
            link(V.tensor_reduce(lm, gcmp.rearrange("p a (b c) -> p a b c", b=NE), AX.X, ADD))
            link(TSC(lm, lm, 1.5, None, ALU.is_lt))
            link(TT(gate, lm, lt, MUL))
            link(V.tensor_reduce(st3[:, :, 3], gate, AX.X, ADD))
            link(V.reciprocal(st3[:, :, 4], st3[:, :, 3]))
            TT(gate, gate, st3[:, :, 4:5].to_broadcast([128, 3, NE]), MUL).then_inc(s("x_gate"), 1)
            dve.wait_ge(*at("x_gt", 1))
            CP(gT[0:8, :], PS[0:8, 3, 0:T]).then_inc(s("x_gtev"), 1)
            dve.wait_ge(*at("x_bc", 8))
            CP(gbc[:, 4:8, :], bank4(4)).then_inc(s("x_bcev"), 1)
            dve.wait_ge(*at("n1m_z", 1))
            ffn(1)
            layer_norm("n1f_", "ffn1")
            for n_ in range(0, 6, 2):
                i, q = n_ // 2, n_ % 2
                n = TILES[i][1]
                dve.wait_ge(*at("y_pe", n_ + 1))
                CP(proj[0:n, 1024 * i:1024 * i + 512], PS[0:n, n_, :]).then_inc(s("y_ev"), 1)


def _constants(np):
    f = np.float32
    cc = np.zeros((128, 512), f)
    cc[:, 0:128] = np.eye(128)
    cc[:, 128:256] = 1.0 / D
    cc[:, 256:384] = 1.0 / 128
    cc[:, 384:512] = 1.0
    c0 = np.zeros((128, N0), f)

    def put(c, table, name, v):
        a, n = table[name]
        v = np.asarray(v, np.float64).reshape(v.shape[0], n)
        c[:v.shape[0], a:a + n] = v

    rot = np.zeros((128, 128))
    for j in range(64):
        rot[64 + j, j] = -1.0
        rot[j, 64 + j] = 1.0
    put(c0, C0, "rot", rot)
    pos = np.concatenate([np.arange(TP), np.tile(2048 + np.arange(NS), NB)]).astype(f)
    inv = (10000.0 ** (-np.arange(64, dtype=f) / f(64))).astype(f)
    ang = np.tile((pos[None, :] * inv[:, None]).astype(f), (2, 1)).astype(np.float64)
    for name, v in (("cos", np.cos(ang)), ("sin", np.sin(ang))):
        put(c0, C0, name, np.stack([v, v * 128 ** -0.5], 1))
    seq = np.concatenate([np.zeros(TP, int), 1 + np.arange(TS) // NS])
    idx = np.concatenate([np.arange(TP), np.arange(TS) % NS])
    ln = np.concatenate([np.full(TP, TP), np.full(TS, NS)])
    gam = 1.0 - 2.0 ** (-5.0 - np.arange(H))
    ok = (seq[:, None] == seq[None, :]) & (idx[None, :] >= idx[:, None])
    diff = np.where(ok, idx[None, :] - idx[:, None], 0)
    dec = np.zeros((128, H, ATT))
    mask = np.full((128, ATT), -1e30)
    for (a, n), (lo, hi), at in zip(TILES, ((0, TP), (128, TP), (256, T)), (0, A1, A2)):
        w = hi - lo
        mask[:n, at:at + w] = np.where(ok[a:a + n, lo:hi], 0.0, -1e30)
        for h in range(H):
            dec[:n, h, at:at + w] = np.where(ok[a:a + n, lo:hi], gam[h] ** diff[a:a + n, lo:hi], 0.0)
    put(c0, C0, "dec", dec)
    put(c0, C0, "mask", mask)
    put(c0, C0, "gq", np.broadcast_to((gam[:, None] ** (idx[TP:] + 1.0)[None, :])[None], (128, H, TS)))
    gk = gam[None, :] ** (ln - 1 - idx)[:, None]
    put(c0, C0, "gk", np.stack([gk[0:128], gk[128:256]], 1))
    blk = (seq[256:, None] == np.arange(SEGS)[None, :]).astype(f)
    put(c0, C0, "gk2", gk[256:, :, None] * blk[:, None, :])
    put(c0, C0, "blk", blk)
    c1 = np.zeros((128, N1), f)
    chunk = np.concatenate([np.arange(256) // 64, np.full(PR2, 4), 5 + np.arange(TS) // NS])
    tabs = {n: np.zeros((128, T)) for n in ("strict", "same8", "eye", "gla")}
    incl = np.full((128, T), -1e30)
    for a, n in TILES:
        q = ok[a:a + n, a:a + n]
        r = np.arange(n)
        incl[:n, a:a + n] = np.where(q, 0.0, -1e30)
        tabs["strict"][:n, a:a + n] = q & (r[None, :] > r[:, None])
        tabs["same8"][:n, a:a + n] = (r[None, :] // 8) == (r[:, None] // 8)
        tabs["eye"][:n, a:a + n] = np.eye(n)
        tabs["gla"][:n, a:a + n] = q & (chunk[a:a + n, None] == chunk[None, a:a + n])
    put(c1, C1, "incl", incl)
    for n_, v in tabs.items():
        put(c1, C1, n_, v)
    start = np.ones(T)
    start[[0, 64, 128, 192, 256, *range(TP, T, NS)]] = 0
    put(c1, C1, "rst", np.broadcast_to(start, (128, T)))
    put(c1, C1, "seg9", np.broadcast_to(blk.T[None], (128, SEGS, R2)))
    put(c1, C1, "blk", blk)
    put(c1, C1, "tri", np.broadcast_to(np.tril(np.ones((NE, NE)), -1)[None], (128, NE, NE)))
    r4 = np.zeros((4, N4), f)
    first = idx == 0
    r4[:, 0:T] = np.where(first, 0.0, 1.0)
    r4[:, T:2 * T] = np.where(first, -3e38, 0.0)
    g = np.where(first, 0.0, 1.0)
    g[[128, 256]] = 0.0
    r4[:, 2 * T:3 * T] = g
    return {"c_common": cc, "c_layer0": c0, "c_layer1": c1, "c_rows": r4}


_DIRECT = ["state_ret", "state_mlstm_c", "state_mlstm_n", "state_gdn", "state_gdn_conv", "state_gla", "w_in0", "w_out0",
           "ffn0_w_gate", "ffn0_w_up", "ffn0_w_down", "w_in1", "gla_w_alpha", "w_out1", "moe_w_router", "moe_b_router",
           "moe_w_gate", "moe_w_up", "moe_w_down"]
_OUTS = {"y_all": (T, D), "prompt_ret": (1, 4, 128, 128), "prompt_c": (1, 4, 128, 128), "prompt_n": (1, 4, 128), "m_rows": (4, 9),
         "prompt_gdn": (1, 4, 128, 128), "prompt_conv": (1, 3, QKV), "prompt_gla": (1, 4, 64, 128), "sample_ret": (NB, 4, 128, 128),
         "sample_c": (NB, 4, 128, 128), "sample_n": (NB, 4, 128), "sample_gdn": (NB, 4, 128, 128), "sample_conv": (NB, 3, QKV),
         "sample_gla": (NB, 4, 64, 128)}


def kernel(**inputs):
    import numpy as np
    import concourse.bacc as bacc
    from concourse.bass_utils import run_bass_kernel_spmd

    x = {k: np.asarray(v) for k, v in inputs.items()}
    arrays = {n: np.ascontiguousarray(x[n]) for n in _DIRECT}
    arrays["x_all"] = np.concatenate([x["meta_tokens"], x["x_prompt"].reshape(SEQ, D), x["x_sample"].reshape(TS, D)])
    norms = [x[n] for n in ("ln0_mix_g", "ln0_mix_b", "ln0_ffn_g", "ln0_ffn_b", "ln1_mix_g", "ln1_mix_b", "ln1_ffn_g", "ln1_ffn_b",
                            "ret_norm_g", "mlstm_norm_g", "gdn_norm_g", "gla_norm_g", "gla_b_alpha")]
    arrays["vec_rows"] = np.concatenate([v.reshape(-1, 128) for v in norms])
    arrays["conv_rows"] = np.ascontiguousarray(x["gdn_conv_w"]).reshape(NCONV, 128)
    arrays["gate_cols"] = np.stack([x["mlstm_gate_bias"][0:4], x["mlstm_gate_bias"][4:8], x["gdn_a_log"], x["gdn_dt_bias"]], 1)
    arrays["m_rows"] = np.ascontiguousarray(x["state_mlstm_m"].T)
    arrays |= _constants(np)
    nc = bacc.Bacc("TRN2", target_bir_lowering=False, num_devices=1)
    I = {n: nc.dram_tensor("in_" + n, a.shape, mybir.dt.float32, kind="ExternalInput").ap() for n, a in arrays.items()}
    O = {n: nc.dram_tensor("out_" + n, shape, mybir.dt.float32, kind="ExternalOutput").ap() for n, shape in _OUTS.items()}
    build(nc, I, O)
    r = run_bass_kernel_spmd(nc, [{"in_" + n: a for n, a in arrays.items()}], core_ids=[0]).results[0]
    o = {n: r["out_" + n] for n in _OUTS}
    y, m = o["y_all"], o["m_rows"]
    return (y[NMETA:TP].reshape(1, SEQ, D), y[TP:].reshape(NB, NS, D),
            o["prompt_ret"], o["prompt_c"], o["prompt_n"], np.ascontiguousarray(m[:, 8:9].T), o["prompt_gdn"], o["prompt_conv"], o["prompt_gla"],
            o["sample_ret"], o["sample_c"], o["sample_n"], np.ascontiguousarray(m[:, 0:8].T), o["sample_gdn"], o["sample_conv"], o["sample_gla"])
```

```python
import math
from contextlib import ExitStack

import concourse.bass as bass
from concourse import mybir

D, KT = 1024, 8
NMETA, SEQ, NB, NS = 16, 256, 8, 4
TP, TS = NMETA + SEQ, NB * NS
T = TP + TS
TILES = [(0, 128), (128, 128), (256, T - 256)]
R2 = T - 256
PR2 = TP - 256
H = 4
HT = H * T
FT = 11
NE = 8
FE = 2
UN = FT + KT
UC = UN - FT + 1
QKV = 1536
LN_EPS, EPS = 1e-5, 1e-6
ALPHA = 4 ** 0.25
ATT = 464
A1, A2 = TP, TP + (TP - 128)
SEGS = 1 + NB
NVEC, NCONV = 82, 48
CONVW = 3 + TP + NB * (3 + NS)
CC = dict(ident=(0, 128), meanD=(128, 128), meanE=(256, 128), ones=(384, 128))
C0 = dict(rot=(0, 128), cos=(128, 2 * T), sin=(128 + 2 * T, 2 * T), dec=(128 + 4 * T, 4 * ATT),
          mask=(128 + 4 * T + 4 * ATT, ATT), gq=(128 + 4 * T + 5 * ATT, 128),
          gk=(256 + 4 * T + 5 * ATT, 8), gk2=(264 + 4 * T + 5 * ATT, 36), blk=(300 + 4 * T + 5 * ATT, 9))
C1 = dict(incl=(0, T), strict=(T, T), same8=(2 * T, T), eye=(3 * T, T), gla=(4 * T, T), rst=(5 * T, T),
          seg9=(6 * T, SEGS * R2), blk=(6 * T + SEGS * R2, 9), tri=(6 * T + SEGS * R2 + 9, 64))
N0, N1 = 309 + 4 * T + 5 * ATT, 6 * T + SEGS * R2 + 73
C4 = dict(rst0=(0, T), rneg=(T, T), rstg=(2 * T, T))
N4 = 3 * T


def build(nc, I, O):
    SBUF0 = -(-nc.sbuf_base // 32) * 32
    F32 = mybir.dt.float32
    ALU, ACT, AX = mybir.AluOpType, mybir.ActivationFunctionType, mybir.AxisListType
    MUL, ADD, SUB, MAX, MIN = ALU.mult, ALU.add, ALU.subtract, ALU.max, ALU.min
    EXP, LN, COPY, IDN, SQR, SILU, SIGM = ACT.Exp, ACT.Ln, ACT.Copy, ACT.Identity, ACT.Square, ACT.Silu, ACT.Sigmoid
    V, S_, G, PEE = nc.vector, nc.scalar, nc.gpsimd, nc.tensor
    ctx = ExitStack()
    sems = {}

    SHARED = {
        "mean": [("r_", 1), ("m_", 1), ("l_", 1)], "cent": [("r_", 1), ("m_", 1), ("l_", 1)],
        "sq": [("r_", 1), ("m_", 1), ("g_", 1), ("l_", 1)], "var": [("r_", 1), ("m_", 1), ("g_", 1), ("l_", 1)],
        "rstd": [("r_", 1), ("m_", 1), ("g_", 1), ("l_", 1)], "out": [("r_", 1), ("m_", 1), ("g_", 1), ("l_", 1)],
        "state_pe": [("r_", 4), ("m_", 4), ("g_", 4), ("l_", 4)], "stu": [("r_", 4), ("m_", 4), ("g_", 4), ("l_", 4)],
        "vb": [("r_", 4), ("m_", 4), ("g_", 4), ("l_", 4)], "vd": [("r_", 1), ("m_", 1)], "pst": [("r_", 1), ("m_", 1)],
        "o": [("r_", 4), ("m_", 4), ("g_", 4), ("l_", 4)], "att": [("r_", 4), ("m_", 4), ("g_", 1), ("l_", 4)],
        "qk": [("r_", 4), ("m_", 4), ("g_", 4), ("l_", 4)], "qs": [("r_", 1), ("m_", 1)],
        "bc": [("m_", 4), ("g_", 1)], "colpe": [("m_", 1), ("g_", 1)], "col": [("m_", 1), ("g_", 1)],
        "abs": [("m_", 1), ("g_", 1), ("l_", 1)], "lse": [("m_", 1), ("g_", 1), ("l_", 1)], "rows": [("m_", 1), ("g_", 1)],
        "kt": [("r_", 3), ("g_", 3), ("l_", 1)], "vt": [("r_", 3), ("g_", 3), ("l_", 3)],
        "normmean": [("n0m_", 1), ("n0f_", 1), ("n1m_", 1), ("n1f_", 1)], "normcent": [("n0m_", 2), ("n0f_", 2), ("n1m_", 2), ("n1f_", 2)],
        "normsq": [("n0m_", 2), ("n0f_", 2), ("n1m_", 2), ("n1f_", 2)], "normvar": [("n0m_", 1), ("n0f_", 1), ("n1m_", 1), ("n1f_", 1)],
        "normrstd": [("n0m_", 1), ("n0f_", 1), ("n1m_", 1), ("n1f_", 1)], "normx": [("n0m_", 2), ("n0f_", 2), ("n1m_", 2), ("n1f_", 2)],
        "normz": [("n0m_", 1), ("n1m_", 1)],
        "w0": [("f0_", 96 * FE), ("f1_", 0)], "w1": [("f0_", 96 * FE), ("f1_", 0)],
        "d0": [("f0_", 32 * FE), ("f1_", 0)], "d1": [("f0_", 32 * FE), ("f1_", 0)],
        "hi": [("a_", 2 * 10), ("f0_", UN * FE), ("b_", 2 * 9), ("f1_", 0)],
        "lo": [("a_", 2 * 10), ("f0_", UN * FE + UC), ("b_", 2 * 9), ("f1_", 0)],
    }
    CHAINS = {
        "router_pe": [("x_log", 1), ("x_gt", 1), ("x_bc", 8)], "router_dve": [("x_lm", 1), ("x_gate", 1), ("x_gtev", 1)],
        "tok_act": [("r_vtok", 3), ("r_ktok", 3), ("m_tok", 6), ("g_tok_a", 3), ("l_tok", 6)],
        "oev_act": [("r_oev", 4), ("g_oev", 1), ("l_oev", 1)],
        "late_load": [("ld_halo", 16), ("ld_stG", 32), ("ld_router", 32)], "silu": [("f0_silu", FE * FT), ("f1_silu", 0)],
        "rope_pe": [("vec_pe", 1), ("rot", 1)], "rows_exp": [("m_exp", 1), ("g_eg", 1)],
    }
    WHERE = {}
    for kind, users in CHAINS.items():
        base = 0
        for name, count in users:
            WHERE[name] = (kind, base)
            base += count
    for kind, users in SHARED.items():
        base = 0
        for prefix, count in users:
            WHERE[prefix + kind.removeprefix("norm")] = (kind, base)
            base += count

    def s(name):
        kind = WHERE.get(name, (name, 0))[0]
        if kind not in sems:
            sems[kind] = ctx.enter_context(nc.semaphore(kind))
        return sems[kind]

    def at(name, n):
        return s(name), n + WHERE.get(name, (name, 0))[1]

    with ctx:
        F32R = mybir.dt.float32r
        words = [0]

        def sb(name, shape):
            n = 8 * -(-math.prod(shape[1:]) // 8)
            t = nc.alloc_sbuf_tensor_at(name, shape, F32, offset=SBUF0 + 4 * words[0])
            words[0] += n
            return t

        def split(name, at_, shape):
            return nc.alloc_sbuf_tensor_at(name, shape, F32R, offset=SBUF0 + 4 * at_)

        xT = sb("xT", [128, KT, T])
        wring = sb("wring", [128, 8192])
        cst = sb("cst", [128, max(N0, N1)])
        cc = sb("cc", [128, 512])
        vec = sb("vec", [128, NVEC + NCONV])
        zT_at = words[0]
        zT = sb("zT", [128, KT, T])
        d_at = words[0]
        dring = sb("dring", [128, 4 * FT * 128])
        st_at = words[0]
        stA = sb("stA", [128, 32, 128])
        stB = sb("stB", [128, 32, 128])
        mix_at = words[0]
        mix = sb("mix", [128, KT, T])
        p_at = words[0]
        proj = sb("proj", [128, 32 * T])
        a_at = words[0]
        arena = sb("arena", [128, 9600])
        xsplit = {n: [split(f"x_{n}_{part}", where[i], [128, KT, T]) for i, part in enumerate(("hi", "lo"))]
                  for n, where in {"in0": (zT_at, mix_at), "in1": (d_at, d_at + KT * T), "out": (p_at, p_at + KT * T)}.items()}
        hsplit = [split(f"hid_{part}", st_at + FT * T * i, [128, FT, T]) for i, part in enumerate(("hi", "lo"))]
        wc = split("w_parts", a_at, [128, 2, 2, 2048])
        dc = split("d_parts", st_at + 2 * FT * T, [128, 2, FT, 128])
        PS = ctx.enter_context(nc.psum_tensor("PS", [128, 8, 512], F32))

        def const(table, name):
            a, n = table[name]
            return (cc if table is CC else cst)[:, a:a + n]

        ident, meanD, meanE, ones = (const(CC, n) for n in ("ident", "meanD", "meanE", "ones"))
        halves = [wring[:, 4096 * i:4096 * (i + 1)].rearrange("p (k n) -> p k n", k=KT) for i in range(2)]
        slots = [wring[:, 4096 * i:4096 * (i + 1)].rearrange("p (g k n) -> p g k n", g=2, k=KT) for i in range(2)]
        dslots = [dring[:, 2816 * i:2816 * (i + 1)].rearrange("p (k n) -> p k n", k=FT) for i in range(2)]

        def proj_parts(i, part):
            return wc[:, i % 2, part].rearrange("p (k n) -> p k n", k=KT)

        def gu_parts(j, part):
            return wc[:, j % 2, part].rearrange("p (g k n) -> p g k n", g=2, k=KT)

        def down_parts(d, part):
            if d % 2:
                return wc[:, 1, part, 0:FT * 128].rearrange("p (k n) -> p k n", k=FT)
            return dc[:, part]

        def raw_proj(g, q):
            return halves[g % 2][:, :, 256 * q:256 * q + 256]

        def raw_gu(j):
            return slots[j // 2 % 2][:, :, :, 128 * (j % 2):128 * (j % 2) + 128]

        def raw_down(d):
            return dslots[d // 2 % 2][:, :, 128 * (d % 2):128 * (d % 2) + 128]

        P = proj[:].rearrange("p (m t) -> p m t", t=T)

        VEC = {n: 8 * i for i, n in enumerate(["mix0_g", "mix0_b", "ffn0_g", "ffn0_b", "mix1_g", "mix1_b", "ffn1_g", "ffn1_b"])}
        VEC |= {"ret": 64, "mlstm": 68, "gdn": 72, "gla": 76, "balpha": 80}

        def carve(base, at, n, *shape):
            v = base[:, at:at + n]
            if len(shape) == 2:
                v = v.rearrange("p (a b) -> p a b", a=shape[0])
            if len(shape) == 3:
                v = v.rearrange("p (a b c) -> p a b c", a=shape[0], b=shape[1])
            return v

        ktok = carve(arena, 0, 1536, 3, 512)
        vtok = carve(arena, 1536, 1536, 3, 512)
        att = carve(arena, 3072, 1856, 4, ATT)
        vd = carve(arena, 4928, 1024, 2, 4, 128)
        pst = carve(arena, 5952, 512, 4, 128)
        ebc = carve(arena, 6464, 1376, 4, 344)
        qs = carve(arena, 7840, 128, 4, 32)
        mcol = carve(arena, 9008, 24)
        wl2 = carve(arena, 9032, 36, 4, 9)
        nT = carve(arena, 9072, 36)
        nrow = carve(arena, 9108, 128)
        gates0 = carve(arena, 9236, 2)
        m0 = carve(arena, 9238, 9)
        wsm = carve(arena, 9248, KT * 24, KT, 24)
        nload = carve(arena, 9440, 128)
        r4 = carve(dring, 0, N4)
        ROW = [dring[0:4, N4 + 344 * i:N4 + 344 * (i + 1)] for i in range(8)]
        vb = [carve(dring, 4480, 1152, SEGS, 128), mix[:, 4:8, :].rearrange("p a b -> p (a b)")[:, 0:1152]
              .rearrange("p (a b) -> p a b", a=SEGS)]
        xtok = proj[:, 0:3072].rearrange("p (a b) -> p a b", a=3)
        vrows = proj[:, 3072:3328]

        mixf, zf = mix[:].rearrange("p a b -> p (a b)"), zT[:].rearrange("p a b -> p (a b)")
        stBf = stB[:].rearrange("p a b -> p (a b)")
        cin = carve(mixf, 0, 4 * CONVW, 4, CONVW)
        cacc = carve(mixf, 4 * CONVW, 2 * CONVW, 2, CONVW)
        convT = carve(zf, 0, 288, 12, 24)
        halo = zf[0:24, 612:612 + QKV]
        lastT = carve(zf, 288, 324, 12, 27)
        lastrow = carve(arena, 6400, 1536)
        sqn = carve(arena, 0, 2432, 8, T)
        decI = carve(arena, 0, HT, 4, T)
        attg = carve(arena, HT, HT, 4, T)
        kb = carve(arena, 2 * HT, HT, 4, T)
        qe = carve(arena, 3 * HT, HT, 4, T)
        ktg = carve(arena, 4864, 1536, 3, 512)
        ug = carve(arena, 6400, 1536, 3, 512)
        sg = carve(arena, 7936, 1536, 3, 4, 128)
        gcol = carve(arena, 9472, 48, 4, 3, 4)
        dbc = carve(arena, 9520, 44, 4, 11)
        SDT, SD = carve(zf, 0, HT, 4, T), carve(zf, HT, HT, 4, T)
        SRT, SO = carve(mixf, 0, HT, 4, T), carve(mixf, HT, HT, 4, T)
        SP_, SPT = carve(dring, 0, HT, 4, T), carve(dring, HT, HT, 4, T)
        rhsk = carve(dring, 2432, 1536, 3, 512)
        rhsv = carve(dring, 3968, 1536, 3, 512)
        ub = [carve(dring, 0, 1152, SEGS, 128), carve(dring, HT, 1152, SEGS, 128)]
        r4b = carve(stBf, 0, N4)
        GROW = [stBf[0:4, N4 + 315 * i:N4 + 315 * (i + 1)] for i in range(7)]
        wtm = carve(stBf, 2368, 4 * SEGS * R2, 4, SEGS, R2)
        lrT, walpha = P[0:16, 28, :], P[0:16, 29, 0:256]
        bc_, cb_, kx_, e1, e2, e3, q1, k1, _, k2 = (carve(arena, 608 * i, 608, 2, T) for i in range(10))
        q2 = carve(arena, 608 * 3, HT, 4, T)
        ktl = carve(arena, 6080, 768, 3, 256)
        vtl = carve(arena, 6848, 1536, 3, 512)
        attl = carve(arena, 8384, HT, 4, T)
        sc = carve(dring, 0, 1280, 5, 2, 128)
        lb = [carve(dring, 1280, 1152, SEGS, 128), carve(dring, 2432, 1152, SEGS, 128)]
        lvp = carve(dring, 3584, 512, 4, 128)
        stG = stB[:, 0:16, :]

        SOLVE = [("split", None, SDT, None, None),
                 ("copy", SP_, SDT, SD, 0),
                 ("copy", SPT, SD, SDT, 0),
                 ("add", SRT, SP_, SRT, 1),
                 ("copy", SD, SPT, SP_, 2),
                 ("add", SRT, SD, SRT, 4),
                 ("copy", SP_, SRT, SO, 5),
                 ("copyz", SPT, SO, SRT, 5),
                 ("transpose", SDT, SRT, None, 5),
                 ("copy", SD, SPT, SP_, 7),
                 ("copy", SRT, SP_, SPT, 8),
                 ("add", SO, SD, SO, 9),
                 ("copy", SP_, SRT, SD, 10),
                 ("copy", SPT, SD, SRT, 10),
                 ("add", SO, SP_, SO, 12),
                 ("copy", SD, SPT, SP_, 13),
                 ("add", SO, SD, SO, 15),
                 ("copy", SRT, SDT, SO, 16)]
        ORDER = [(k, i) for k in range(len(SOLVE)) for i in range(3) if i < 2 or k <= 8 or k == 17]
        AT = {ki: n for n, ki in enumerate(ORDER)}

        def solve_after(k, i):
            w = SOLVE[k][4]
            if i == 2 and k == 17:
                w = 8
            return 0 if w is None else AT[(w, i)] + 1

        gact = P[:, 16:18, :]
        gu_raw = P[:, 18, :]
        hraw = mix[:, 6:8, :]
        gbc = P[:, 20:28, :]
        rt = proj[:, 28 * T:32 * T]
        lt, lm, gate = (carve(rt, 24 * i, 24, 3, 8) for i in range(3))
        gcmp, geq = (carve(rt, 72 + 192 * i, 192, 3, 64) for i in range(2))
        st3 = carve(rt, 456, 24, 3, 8)
        gT = rt[:, 480:480 + T]
        brt = rt[:, 800:808]
        wrt = carve(rt, 832, 64, KT, 8)

        LNB = {"n0m_": 0, "n0f_": 0, "n1m_": 4, "n1f_": 0}

        def bank4(a):
            return PS[:, a:a + 4, 0:T]

        def smp(ap):
            return ap[:, TP:T].rearrange("p (b t) -> p b t", b=NB)

        def cins(m):
            return cin[:, m % 4, 3 + TP:CONVW].rearrange("p (b t) -> p b t", b=NB)

        def cconv(m):
            return cacc[:, m % 2, 3 + TP:CONVW].rearrange("p (b t) -> p b t", b=NB)[:, :, 0:NS]

        in0 = [512 * g for g in range(8)]
        in1 = [0, 512, 1024, 1536, 2056, 2568, 3080]
        groups = [(I["w_in0"], c) for c in in0] + [(I["w_out0"], c) for c in (0, 512)] \
            + [(I["w_in1"], c) for c in in1] + [(I["w_out1"], c) for c in (0, 512)]
        OUT0, IN1, OUT1, GEND = 8, 10, 17, 19

        def ffn_weights(layer):
            if layer == 0:
                g, u = (I[n].rearrange("(k p) (e f) -> e p k f", p=128, e=FE) for n in ("ffn0_w_gate", "ffn0_w_up"))
                d = I["ffn0_w_down"].rearrange("(e j p) d -> e p j d", p=128, e=FE)
            else:
                g, u = (I[n].rearrange("e (k p) f -> e p k f", p=128) for n in ("moe_w_gate", "moe_w_up"))
                d = I["moe_w_down"].rearrange("e (j p) d -> e p j d", p=128)
            return g, u, d

        def over_experts(engine, E, body):
            with engine.Fori(0, E - 1) as e:
                body(e, False)
            body(E - 1, True)

        block = ctx.enter_context(nc.Block())

        @block.sync
        def _(sp):
            def group(g):
                w, c = groups[g]
                if 2 <= g < IN1:
                    sp.wait_ge(*at("a_lo", 2 * (g - 1)))
                elif g >= IN1 + 2:
                    sp.wait_ge(*at("b_lo", 2 * (g - 1 - IN1)))
                sp.dma_start(halves[g % 2], w[:, c:c + 512].rearrange("(k p) n -> p k n", p=128)).then_inc(s(f"ring{g % 2}"), 16)

            for i, (a, n) in enumerate(TILES):
                sp.dma_start(xtok[0:n, i, :], I["x_all"][a:a + n]).then_inc(s("ld_x"), 16)
            group(0)
            group(1)
            for g in range(2, OUT0 + 2):
                group(g)

            def ffn(layer, ring_free, dring_free):
                wg, wu, wd = ffn_weights(layer)
                p, E = f"f{layer}_", (FE, NE)[layer]

                def hidden_pair(e, q):
                    n = min(256, FT * 128 - 256 * q)
                    for gu, w in enumerate((wg, wu)):
                        sp.dma_start(slots[q % 2][:, gu, :, 0:n], w[e, :, :, 256 * q:256 * q + n]).then_inc(s(p + f"w{q % 2}"), 16)

                def down_pair(e, q):
                    sp.dma_start(dslots[q % 2], wd[e, :, :, 256 * q:256 * q + 256]).then_inc(s(p + f"d{q % 2}"), 16)

                def body(e, is_last):
                    sp.wait_ge(*at(p + "lo", e * UN + (UC - 2)))
                    down_pair(e, 0)
                    sp.wait_ge(*at(p + "lo", e * UN + UC))
                    down_pair(e, 1)
                    for q in range(2, 6):
                        sp.wait_ge(*at(p + "lo", e * UN + (UC + 2 * q - 2)))
                        hidden_pair(e, q)
                    if not is_last:
                        for q in range(2):
                            sp.wait_ge(*at(p + "lo", e * UN + (UC + 10 + q)))
                            hidden_pair(e + 1, q)
                    for q in range(2, 4):
                        sp.wait_ge(*at(p + "lo", e * UN + (UC + FT + 2 * q - 2)))
                        down_pair(e, q)

                for q in range(2):
                    sp.wait_ge(*ring_free[q])
                    hidden_pair(0, q)
                for signal in dring_free:
                    sp.wait_ge(*signal)
                over_experts(sp, E, body)

            ffn(0, [at("a_lo", 18), at("a_lo", 20)], [at("m_out", 1)])
            for g in range(IN1, GEND):
                if g < IN1 + 2:
                    sp.wait_ge(*at("f0_lo", UC + UN * (FE - 1) + FT - 1 + g - IN1))
                group(g)
            ffn(1, [at("b_lo", 18), at("b_lo", 18)], [at("l_out", 1), at("st_all", 16 * 19)])
            sp.wait_ge(*at("y_ev", 6))
            ytok = proj[:, 0:3072].rearrange("p (a b) -> p a b", a=3)
            for i, (a, n) in enumerate(TILES):
                sp.dma_start(O["y_all"][a:a + n], ytok[0:n, i, :]).then_inc(s("st_y"), 16)
            sp.wait_ge(*at("st_y", 48))

        @block.tensor
        def _(pe):
            mm = PEE.matmul

            def tr(out, in_, n):
                return PEE.transpose(out, in_, ident[0:n, 0:n])

            def row(h, n=4):
                return ident[0:n, h:h + 1].to_broadcast([n, 128])

            pe.wait_ge(*at("ld_x", 48))
            pe.wait_ge(*at("ld_v", 64))
            for k in range(KT):
                for i, (a, n) in enumerate(TILES):
                    last = tr(PS[:, k, a:a + n], xtok[0:n, i, 128 * k:128 * k + 128], n)
                last.then_inc(s("xt_pe"), 1)
            pe.wait_ge(*at("xT", KT))
            tr(PS[:, 0, 0:NVEC], vrows[0:NVEC, 0:128], NVEC)
            tr(PS[:, 0, 128:128 + NCONV], vrows[0:NCONV, 128:256], NCONV)
            tr(PS[:, 0, 256:288], nload[0:32, :], 32).then_inc(s("vec_pe"), 1)

            def narrow(layer, parts):
                pe.wait_ge(*at(("ld_wsm", "ld_l1")[layer], (16, 80)[layer]))
                for c, n, b in parts:
                    for k in range(KT):
                        last = mm(PS[0:n, b, 0:T], wsm[:, k, c:c + n], xT[:, k, :], start=k == 0, stop=k == KT - 1)
                last.then_inc(s("small_pe"), 1)

            narrow(0, [(0, 4, 6), (4, 4, 7)])

            def mm3(out, w, x, start, stop):
                mm(out, w[0], x[0], start=start, stop=False)
                mm(out, w[0], x[1], start=False, stop=False)
                return mm(out, w[1], x[0], start=False, stop=stop)

            def tile_mm(half, t, x):
                for k in range(KT):
                    w = [proj_parts(t // 2, part)[:, k, 128 * (t % 2):128 * (t % 2) + 128] for part in range(2)]
                    last = mm3(PS[:, 4 * half + t, 0:T], w, [x[0][:, k, :], x[1][:, k, :]], k == 0, k == KT - 1)
                last.then_inc(s("proj_pe"), 1)

            def units(g):
                return ("a_lo", 2 * g) if g < IN1 else ("b_lo", 2 * (g - IN1))

            def group(g, x, banks_free=True):
                name, before = units(g)
                for t in range(4):
                    if t % 2 == 0:
                        pe.wait_ge(*at(name, before + t // 2 + 1))
                    if not banks_free:
                        pe.wait_ge(*at("proj_ev", 4 * (g - 2) + t + 1))
                    tile_mm(g % 2, t, x)

            def group_pairs(lo, hi, x):
                name, before = units(2 * lo)
                with pe.Fori(lo, hi) as p:
                    for half in range(2):
                        for t in range(4):
                            if t % 2 == 0:
                                pe.wait_ge(*at(name, p * 4 + (before - 4 * lo + 2 * half + t // 2 + 1)))
                            pe.wait_ge(*at("proj_ev", p * 8 + (4 * half + t - 7)))
                            tile_mm(half, t, x)

            pe.wait_ge(*at("vec_ev", 1))
            pe.wait_ge(*at("xlo", 2))
            group(0, xsplit["in0"])
            pe.wait_ge(*at("small_ev", 1))
            group(1, xsplit["in0"])
            group_pairs(1, 4, xsplit["in0"])

            def state_mm(p, h, kt_, vdec, vblk, kcols, banks, pbank):
                for i in range(2):
                    mm(PS[:, pbank, 128 * h:128 * h + 128], kt_[:, i, kcols], vdec[:, i, h, :], start=i == 0, stop=False)
                mm(PS[:, pbank, 128 * h:128 * h + 128], kt_[0:R2, 2, kcols], vblk[0:R2, 0, :], start=False, stop=True)
                for j, b in enumerate(banks):
                    last = mm(PS[:, b, :], kt_[0:R2, 2, kcols], vblk[0:R2, 1 + 4 * j:5 + 4 * j, :].rearrange("p a b -> p (a b)"),
                              start=True, stop=True)
                last.then_inc(s(p + "state_pe"), 1)

            def out_mm(bank, lhs, h, final):
                mm(PS[:, bank, 0:TP], lhs[0], att[:, h, 0:A1], start=True, stop=False)
                mm(PS[:, bank, 128:TP], lhs[1], att[:, h, A1:A2], start=False, stop=False)
                mm(PS[:, bank, 256:TP], lhs[2], att[0:R2, h, A2:A2 + PR2], start=False, stop=False)
                mm(PS[:, bank, TP:T], lhs[2], att[0:R2, h, A2 + PR2:ATT], start=False, stop=False)
                for b in range(NB):
                    last = mm(PS[:, bank, TP + 4 * b:TP + 4 * b + 4], final(b), qs[:, h, 4 * b:4 * b + 4],
                              start=False, stop=b == NB - 1)
                return last

            def scores(bank, h, q0, k0):
                mm(PS[:, bank, 0:A1], P[:, k0 + h, 0:128], P[:, q0 + h, 0:TP], start=True, stop=True)
                mm(PS[:, bank, A1:A2], P[:, k0 + h, 128:256], P[:, q0 + h, 128:TP], start=True, stop=True)
                return mm(PS[0:R2, bank, A2:ATT], P[:, k0 + h, 256:T], P[:, q0 + h, 256:T], start=True, stop=True)

            def tokens(bank, i, m0_, n=4):
                a, r = TILES[i]
                for h in range(n):
                    last = tr(PS[0:r, bank, 128 * h:128 * h + 128], P[:, m0_ + h, a:a + r], 128)
                return last

            def norm(p, rms=False, mean_at=0, var_at=4):
                o = zT[:, 0:4, :]
                if not rms:
                    for h in range(H):
                        last = mm(PS[:, mean_at + h, 0:T], meanE, o[:, h, :], start=True, stop=True)
                    last.then_inc(s(p + "mean"), 1)
                pe.wait_ge(*at(p + "sq", 1))
                for h in range(H):
                    last = mm(PS[:, var_at + h, 0:T], meanE, zT[:, 4 + h, :], start=True, stop=True)
                last.then_inc(s(p + "var"), 1)

            pe.wait_ge(*at("proj_ev", 32))
            pe.wait_ge(*at("ld_c0", 16))
            for m in range(8):
                last = mm(PS[:, m, 0:T], const(C0, "rot"), P[:, m, :], start=True, stop=True)
            last.then_inc(s("rot"), 1)
            pe.wait_ge(*at("rotm", 1))
            for i in range(3):
                tokens(3 + i, i, 8).then_inc(s("r_vt"), 1)
            pe.wait_ge(*at("rope", 1))
            for i in range(3):
                tokens(i, i, 4).then_inc(s("r_kt"), 1)
            for h, b in enumerate([6, 7, 3, 4]):
                if h == 2:
                    pe.wait_ge(*at("r_vtok", 3))
                scores(b, h, 0, 4).then_inc(s("r_qk"), 1)
            pe.wait_ge(*at("r_ktok", 3))
            pe.wait_ge(*at("r_qs", 1))
            pe.wait_ge(*at("ld_stA", 16))
            for h, b in enumerate([0, 1, 2, 5]):
                pe.wait_ge(*at("r_att", h + 1))
                v = [vtok[:, 0, 128 * h:128 * h + 128], vtok[:, 1, 128 * h:128 * h + 128], vtok[0:R2, 2, 128 * h:128 * h + 128]]
                out_mm(b, v, h, lambda b_: stA[:, 4 * b_ + h, :]).then_inc(s("r_o"), 1)
            pe.wait_ge(*at("r_oev", 4))
            for h in range(H):
                if h == 0:
                    pe.wait_ge(*at("r_vd", 1))
                pe.wait_ge(*at("r_vb", h + 1))
                if h >= 2:
                    pe.wait_ge(*at("r_stu", h - 1))
                state_mm("r_", h, ktok, vd, vb[h % 2], slice(128 * h, 128 * h + 128), [(7, 3), (4, 5)][h % 2], 6)
            pe.wait_ge(*at("r_stu", 4))
            norm("r_", mean_at=0, var_at=0)

            pe.wait_ge(*at("r_out", 1))
            pe.wait_ge(*at("r_pst", 1))
            pe.wait_ge(*at("m_rows", 1))
            pe.wait_ge(*at("m_exp", 1))
            for i, (a, n) in enumerate(TILES):
                tr(PS[0:n, 7, 4 * i:4 * i + 4], ROW[3][:, a:a + n], 4)
                last = tr(PS[0:n, 7, 12 + 4 * i:16 + 4 * i], ROW[5][:, a:a + n], 4)
            last.then_inc(s("m_colpe"), 1)
            for h in range(H):
                mm(PS[:, h, 0:T], row(h), ROW[4][:, 0:T], start=True, stop=True)
                if h == 3:
                    pe.wait_ge(*at("m_col", 1))
                mm(PS[:, 4 + h, 0:344], row(h), ROW[6], start=True, stop=True).then_inc(s("m_bc"), 1)
            for h in range(H):
                pe.wait_ge(*at("m_ex", h + 1))
                scores(h, h, 16, 20).then_inc(s("m_qk"), 1)
            pe.wait_ge(*at("m_ebc", 1))
            for n_, (b, i, m_) in enumerate([(4, 0, 20), (5, 1, 20), (6, 2, 20), (7, 0, 24), (4, 1, 24), (5, 2, 24)]):
                if n_ >= 4:
                    pe.wait_ge(*at("m_tok", n_ - 3))
                tokens(b, i, m_).then_inc(s("m_tpe"), 1)
            pe.wait_ge(*at("m_tok", 6))
            pe.wait_ge(*at("m_qs", 1))
            pe.wait_ge(*at("ld_stB", 16))
            for h in range(H):
                pe.wait_ge(*at("m_att", h + 1))
                out_mm(4 + h, [ones, ones, ones[0:R2, :]], h, lambda b_: nT[:, 4 * b_ + h:4 * b_ + h + 1].to_broadcast([128, 128]))
                v = [vtok[:, 0, 128 * h:128 * h + 128], vtok[:, 1, 128 * h:128 * h + 128], vtok[0:R2, 2, 128 * h:128 * h + 128]]
                out_mm(h, v, h, lambda b_: stB[:, 4 * b_ + h, :]).then_inc(s("m_o"), 1)
            pe.wait_ge(*at("m_oev", 1))
            pe.wait_ge(*at("m_vd", 1))
            for h in range(H):
                kc = slice(128 * h, 128 * h + 128)
                mm(PS[:, 5, 9 * h:9 * h + 9], ktok[0:R2, 2, kc], wl2[0:R2, h, :], start=True, stop=False)
                for i in range(2):
                    mm(PS[:, 5, 9 * h:9 * h + 1], ktok[:, i, kc], mcol[:, 12 + 4 * i + h:13 + 4 * i + h], start=False, stop=i == 1)
            for h in range(H):
                pe.wait_ge(*at("m_vb", h + 1))
                if h >= 2:
                    pe.wait_ge(*at("m_stu", h - 1))
                kc = slice(128 * h, 128 * h + 128)
                state_mm("m_", h, ktok, vd, vb[h % 2], kc, [(7, 3), (4, 2)][h % 2], 6)
            pe.wait_ge(*at("m_stu", 4))
            pe.wait_ge(*at("m_nst", 1))
            tr(PS[0:36, 0, 0:128], nT[:, 0:36], 128).then_inc(s("m_npe"), 1)
            pe.wait_ge(*at("m_nrow", 1))
            norm("m_", mean_at=0, var_at=0)

            def layer_norm(p, ready, count):
                for k in range(KT):
                    pe.wait_ge(*at(ready, count - KT + k + 1))
                    last = mm(PS[:, LNB[p], 0:T], meanD, zT[:, k, :], start=k == 0, stop=k == KT - 1)
                last.then_inc(s(p + "mean"), 1)
                for k in range(KT):
                    if k % 4 == 0:
                        pe.wait_ge(*at(p + "sq", k // 4 + 1))
                    last = mm(PS[:, LNB[p] + 1, 0:T], meanD, mix[:, k, :], start=k == 0, stop=k == KT - 1)
                last.then_inc(s(p + "var"), 1)

            def ffn(layer):
                p, E = f"f{layer}_", (FE, NE)[layer]
                x = xsplit["out"]
                pe.sem_inc(s(p + "hid_pe"), 1)
                pe.sem_inc(s(p + "down_pe"), 1)

                def body(e, is_last):
                    for j in range(FT):
                        pe.wait_ge(*at(p + "lo", e * UN + (UC + j + 1)))
                        pe.wait_ge(*at(p + "hid_ev", e * FT + max(j, 1)))
                        for gu in range(2):
                            for k in range(KT):
                                w = [gu_parts(j, part)[:, gu, k, :] for part in range(2)]
                                last = mm3(PS[:, 2 * (j % 2) + gu, 0:T], w, [x[0][:, k, :], x[1][:, k, :]], k == 0, k == KT - 1)
                        last.then_inc(s(p + "hid_pe"), 1)
                    for d in range(KT):
                        pe.wait_ge(*at(p + "lo", e * UN + (UC + FT + d + 1)))
                        pe.wait_ge(*at(p + "down_ev", e * KT + d + 1))
                        for j in range(FT):
                            if d == 0 and j >= FT - 2:
                                pe.wait_ge(*at(p + "hid_ev", e * FT + j + 2))
                            w = [down_parts(d, part)[:, j, :] for part in range(2)]
                            last = mm3(PS[:, 4 + d % 4, 0:T], w, [hsplit[0][:, j, :], hsplit[1][:, j, :]], j == 0, j == FT - 1)
                        last.then_inc(s(p + "down_pe"), 1)

                with pe.Fori(0, E) as e:
                    body(e, False)

            pe.wait_ge(*at("xlo", 4))
            group(8, xsplit["out"])
            group(9, xsplit["out"])
            layer_norm("n0m_", "proj_ev", 40)
            pe.wait_ge(*at("xlo", 6))
            ffn(0)
            layer_norm("n0f_", "f0_down_ev", 4 + FE * KT)
            pe.wait_ge(*at("n0f_x", 2))

            narrow(1, [(0, 4, 5), (4, 4, 6), (8, 16, 7)])
            pe.wait_ge(*at("xlo", 8))
            group(10, xsplit["in1"])
            pe.wait_ge(*at("ld_halo", 16))
            for m in range(12):
                last = tr(PS[:, 4, 24 * m:24 * m + 24], halo[:, 128 * m:128 * m + 128], 24)
            last.then_inc(s("halo_pe"), 1)
            pe.wait_ge(*at("cin0", 1))
            pe.wait_ge(*at("small_ev", 2))
            group(11, xsplit["in1"])
            group_pairs(6, 8, xsplit["in1"])
            group(16, xsplit["in1"], banks_free=False)

            pe.wait_ge(*at("last", 12))
            pe.wait_ge(*at("proj_ev", 4 * OUT1))
            for m in range(12):
                last = tr(PS[0:27, m // 4, 128 * (m % 4):128 * (m % 4) + 128], lastT[:, m, :], 128)
            last.then_inc(s("last_pe"), 1)
            pe.wait_ge(*at("last_ev", 1))
            pe.wait_ge(*at("g_sqn", 1))
            for m in range(8):
                last = mm(PS[:, m, 0:T], ones, sqn[:, m, :], start=True, stop=True)
            last.then_inc(s("g_l2pe"), 1)
            pe.wait_ge(*at("g_l2a", 1))
            pe.wait_ge(*at("g_rows", 1))
            for r in range(4):
                for i, (a, n) in enumerate(TILES):
                    last = tr(PS[0:n, 0, 12 * r + 4 * i:12 * r + 4 * i + 4], [GROW[0], GROW[3], GROW[4], GROW[5]][r][:, a:a + n], 4)
            last.then_inc(s("g_colpe"), 1)
            pe.wait_ge(*at("g_col", 1))
            for h in range(H):
                mm(PS[:, h, 0:315], row(h), GROW[2], start=True, stop=True)
                last = mm(PS[:, 4 + h, 0:T], row(h), GROW[0][:, 0:T], start=True, stop=True)
            last.then_inc(s("g_bc"), 1)
            pe.wait_ge(*at("g_bcev", 1))
            pe.wait_ge(*at("g_kb", 1))
            for h in range(H):
                for a, n in TILES:
                    last = mm(PS[0:n, h, a:a + n], P[:, 4 + h, a:a + n], kb[:, h, a:a + n], start=True, stop=True)
                last.then_inc(s("g_aa"), 1)
            for h in range(H):
                for a, n in TILES:
                    last = mm(PS[0:n, 4 + h, a:a + n], P[:, 4 + h, a:a + n], P[:, h, a:a + n], start=True, stop=True)
                last.then_inc(s("g_qk"), 1)
            pe.wait_ge(*at("g_at", 1))
            for i in range(3):
                tokens(i, i, 4).then_inc(s("g_kt"), 1)
            pe.wait_ge(*at("g_att", 1))
            for i in range(3):
                tokens(4 + i, i, 8).then_inc(s("g_vt"), 1)
            pe.wait_ge(*at("g_tok_a", 3))
            pe.wait_ge(*at("g_tok_d", 6))

            for n_, (k, i) in enumerate(ORDER):
                what, out, lhs, rhs, _ = SOLVE[k]
                a, n = TILES[i]
                if solve_after(k, i):
                    pe.wait_ge(*at("sv_ev", solve_after(k, i)))
                if n_ >= 8:
                    pe.wait_ge(*at("sv_ev", n_ - 7))
                for h in range(H):
                    o = PS[0:n, n_ % 8, n * h:n * h + n]
                    if what in ("split", "transpose"):
                        last = tr(o, lhs[0:n, h, a:a + n], n)
                    else:
                        last = mm(o, lhs[0:n, h, a:a + n], rhs[0:n, h, a:a + n], start=True, stop=True)
                last.then_inc(s("sv_pe"), 1)
            pe.wait_ge(*at("sv_ev", len(ORDER)))

            for i, (a, n) in enumerate(TILES):
                for h in range(H):
                    last = mm(PS[:, i, n * h:n * h + n], rhsk[0:n, i, 128 * h:128 * h + 128], SRT[0:n, h, a:a + n], start=True, stop=True)
                last.then_inc(s("g_w"), 1)
            for i, (a, n) in enumerate(TILES):
                if i == 2:
                    pe.wait_ge(*at("g_wtm", 1))
                if i > 0:
                    pe.wait_ge(*at("g_s", i))
                    pe.wait_ge(*at("g_wev", 3))
                for h in range(H):
                    o = PS[0:n, 3, 128 * h:128 * h + 128]
                    last = mm(o, SRT[0:n, h, a:a + n], rhsv[0:n, i, 128 * h:128 * h + 128], start=True, stop=i == 0)
                    if i == 1:
                        last = mm(o, kb[:, h, a:a + n], sg[:, 0, h, :], start=False, stop=True)
                    if i == 2:
                        mm(o, wtm[:, h, 0, :], sg[:, 1, h, :], start=False, stop=False)
                        for b in range(NB):
                            last = mm(o, wtm[:, h, 1 + b, :], stA[:, 4 * b + h, :], start=False, stop=b == NB - 1)
                last.then_inc(s("g_upe"), 1)
                pe.wait_ge(*at("g_ua", i + 1))
                pe.wait_ge(*at("g_ue", i + 1))
                if i < 2:
                    for h in range(H):
                        last = mm(PS[:, 5, 128 * h:128 * h + 128], ktg[:, i, 128 * h:128 * h + 128], rhsk[:, i, 128 * h:128 * h + 128],
                                  start=True, stop=True)
                    last.then_inc(s("g_spe"), 1)
            pe.wait_ge(*at("g_wev", 3))
            for h, b in enumerate([0, 1, 2, 5]):
                for i, (a, n) in enumerate(TILES):
                    mm(PS[:, b, a:a + n], ug[0:n, i, 128 * h:128 * h + 128], attg[0:n, h, a:a + n], start=i == 0, stop=False)
                    if i == 1:
                        mm(PS[:, b, a:a + n], sg[:, 0, h, :], qe[:, h, a:a + n], start=False, stop=False)
                mm(PS[:, b, 256:TP], sg[:, 1, h, :], qe[:, h, 256:TP], start=False, stop=False)
                for b_ in range(NB):
                    last = mm(PS[:, b, TP + 4 * b_:TP + 4 * b_ + 4], stA[:, 4 * b_ + h, :], qe[:, h, TP + 4 * b_:TP + 4 * b_ + 4],
                              start=False, stop=b_ == NB - 1)
                last.then_inc(s("g_o"), 1)
            pe.wait_ge(*at("g_oev", 1))
            for h in range(H):
                pe.wait_ge(*at("g_vb", h + 1))
                if h >= 2:
                    pe.wait_ge(*at("g_stu", h - 1))
                kc = slice(128 * h, 128 * h + 128)
                mm(PS[:, 6, kc], ktg[0:R2, 2, kc], ub[h % 2][0:R2, 0, :], start=True, stop=True)
                for j, b in enumerate([(7, 3), (4, 5)][h % 2]):
                    last = mm(PS[:, b, :], ktg[0:R2, 2, kc], ub[h % 2][0:R2, 1 + 4 * j:5 + 4 * j, :].rearrange("p a b -> p (a b)"),
                              start=True, stop=True)
                last.then_inc(s("g_state_pe"), 1)
            pe.wait_ge(*at("g_stu", 4))
            norm("g_", rms=True, var_at=0)

            pe.wait_ge(*at("g_out", 1))
            pe.wait_ge(*at("g_pst", 1))
            for p in range(2):
                last = mm(PS[:, 6 + p, 0:T], walpha[:, 128 * p:128 * p + 128], lrT, start=True, stop=True)
            last.then_inc(s("l_alpha"), 1)
            for i in range(3):
                tokens(i, i, 20).then_inc(s("l_vt"), 1)
            pe.wait_ge(*at("l_dqk", 1))
            for i, (a, n) in enumerate(TILES):
                for p in range(2):
                    last = tr(PS[0:n, 3 + i // 2, 256 * (i % 2) + 128 * p:256 * (i % 2) + 128 * p + 128], k2[:, p, a:a + n], 128)
            last.then_inc(s("l_kt"), 1)
            pe.wait_ge(*at("l_tok", 6))
            for h, b in enumerate([5, 6, 7, 0]):
                r = slice(64 * (h % 2), 64 * (h % 2) + 64)
                for a, n in TILES:
                    last = mm(PS[0:n, b, a:a + n], k1[r, h // 2, a:a + n], q1[r, h // 2, a:a + n], start=True, stop=True)
                last.then_inc(s("l_qk"), 1)
            pe.wait_ge(*at("l_vb0", 1))
            for p in range(2):
                if p == 1:
                    pe.wait_ge(*at("l_sc", 1))
                for c in range(4):
                    r = slice(64 * (c % 2), 64 * (c % 2) + 64)
                    mm(PS[:, 1 + c % 2, 256 * (c // 2):256 * (c // 2) + 256], ktl[r, c // 2, 128 * p:128 * p + 128],
                       vtl[r, c // 2, 256 * p:256 * p + 256], start=True, stop=True)
                for q in range(2):
                    last = mm(PS[:, 3, 128 * q:128 * q + 128], ktl[0:R2, 2, 128 * p:128 * p + 128], lvp[0:R2, 2 * p + q, :],
                              start=True, stop=True)
                last.then_inc(s("l_upe"), 1)
            pe.wait_ge(*at("l_sc", 2))
            pe.wait_ge(*at("ld_stG", 32))
            pe.wait_ge(*at("l_att", 4))
            for h in range(H):
                r, p = slice(64 * (h % 2), 64 * (h % 2) + 64), h // 2
                for i in (2, 0, 1):
                    a, n = TILES[i]
                    mm(PS[:, h, a:a + n], vtl[0:n, i, 128 * h:128 * h + 128], attl[0:n, h, a:a + n], start=i == 2, stop=False)
                for c in range(1, 5):
                    n = 64 if c < 4 else PR2
                    mm(PS[:, h, 64 * c:64 * c + n], sc[:, c - 1, p, :], q2[:, h, 64 * c:64 * c + n], start=False, stop=False)
                for b in range(NB):
                    last = mm(PS[:, h, TP + 4 * b:TP + 4 * b + 4], stG[:, 2 * b + p, :], q2[:, h, TP + 4 * b:TP + 4 * b + 4],
                              start=False, stop=b == NB - 1)
                last.then_inc(s("l_o"), 1)
            for h in range(H):
                pe.wait_ge(*at("l_vb", h + 1))
                if h >= 2:
                    pe.wait_ge(*at("l_stu", h - 1))
                for j, b in enumerate([(4, 5), (6, 7)][h % 2]):
                    last = mm(PS[:, b, :], ktl[0:R2, 2, 128 * (h // 2):128 * (h // 2) + 128],
                              lb[h % 2][0:R2, 1 + 4 * j:5 + 4 * j, :].rearrange("p a b -> p (a b)"), start=True, stop=True)
                last.then_inc(s("l_state_pe"), 1)
            pe.wait_ge(*at("l_oev", 1))
            norm("l_", var_at=0)

            pe.wait_ge(*at("xlo", 10))
            group(17, xsplit["out"])
            group(18, xsplit["out"])
            layer_norm("n1m_", "proj_ev", 4 * GEND)
            pe.wait_ge(*at("n1m_x", 2))

            pe.wait_ge(*at("ld_router", 32))
            for i, (a, n) in enumerate(TILES):
                for k in range(KT):
                    mm(PS[0:n, 2, 8 * i:8 * i + 8], xT[:, k, a:a + n], wrt[:, k, :], start=k == 0, stop=False)
                last = mm(PS[0:n, 2, 8 * i:8 * i + 8], ones[0:1, 0:n], brt[0:1, :], start=False, stop=True)
            last.then_inc(s("x_log"), 1)
            pe.wait_ge(*at("x_gate", 1))
            for i, (a, n) in enumerate(TILES):
                last = tr(PS[0:8, 3, a:a + n], gate[0:n, i, :], n)
            last.then_inc(s("x_gt"), 1)
            pe.wait_ge(*at("x_gtev", 1))
            for e in range(NE):
                mm(PS[:, e, 0:T], row(e, 8), gT[0:8, :], start=True, stop=True).then_inc(s("x_bc"), 1)
            pe.wait_ge(*at("x_bcev", 2))
            pe.wait_ge(*at("xlo", 12))
            ffn(1)
            layer_norm("n1f_", "f1_down_ev", 4 + NE * KT)
            pe.wait_ge(*at("n1f_x", 2))
            for i, (a, n) in enumerate(TILES):
                for q in range(2):
                    for k in range(4):
                        last = tr(PS[0:n, 2 * i + q, 128 * k:128 * k + 128], xT[:, 4 * q + k, a:a + n], 128)
                    last.then_inc(s("y_pe"), 1)

        @block.scalar
        def _(act):
            A = S_.activation
            chain = [0]

            def link(ins):
                chain[0] += 1
                ins.then_inc(s("act_chain"), 1)
                act.wait_ge(*at("act_chain", chain[0]))

            act.dma_start(cc[:], I["c_common"]).then_inc(s("ld_v"), 16)
            act.dma_start(vrows[0:NVEC, 0:128], I["vec_rows"]).then_inc(s("ld_v"), 16)
            act.dma_start(vrows[0:NCONV, 128:256], I["conv_rows"]).then_inc(s("ld_v"), 16)
            act.dma_start(nload[0:32, :], I["state_mlstm_n"].rearrange("b h d -> (b h) d")).then_inc(s("ld_v"), 16)
            act.dma_start(wsm[:, :, 0:8], I["w_in0"][:, 4096:4104].rearrange("(k p) n -> p k n", p=128)).then_inc(s("ld_wsm"), 16)
            act.dma_start(gates0[0:4, :], I["gate_cols"][:, 0:2]).then_inc(s("ld_r"), 16)
            act.dma_start(m0[0:4, 0:8], I["m_rows"]).then_inc(s("ld_r"), 16)
            act.dma_start(r4[0:4, :], I["c_rows"]).then_inc(s("ld_r"), 16)
            act.dma_start(cst[:, 0:N0], I["c_layer0"]).then_inc(s("ld_c0"), 16)
            act.dma_start(stA[:], I["state_ret"].rearrange("b h d e -> d (b h) e")).then_inc(s("ld_stA"), 16)
            act.dma_start(stB[:], I["state_mlstm_c"].rearrange("b h d e -> d (b h) e")).then_inc(s("ld_stB"), 16)

            for k in range(1, KT, 2):
                act.wait_ge(*at("xt_pe", k + 1))
                A(xT[:, k, :], PS[:, k, 0:T], COPY).then_inc(s("xT"), 1)

            def x_hi(where, chunk, src, ready):
                act.wait_ge(*ready)
                k = slice(4 * chunk, 4 * chunk + 4)
                A(xsplit[where][0][:, k, :], src[:, k, :], COPY).then_inc(s("xhi"), 1)

            def proj_hi(layer, i):
                g = (0, IN1)[layer] + i // 2
                act.wait_ge(*at(f"ring{g % 2}", 16 * (g // 2 + 1)))
                if i >= 2:
                    act.wait_ge(*at("proj_pe", (0, 4 * IN1)[layer] + 2 * (i - 1)))
                elif layer == 1:
                    act.wait_ge(*at(*[("f0_hid_pe", FE * FT + 1), ("f0_down_pe", FE * KT + 1)][i]))
                A(proj_parts(i, 0), raw_proj(g, i % 2), COPY).then_inc(s("ab"[layer] + "_hi"), 1)

            for c in range(2):
                x_hi("in0", c, xT, at("xT", KT))
            proj_hi(0, 0)
            proj_hi(0, 1)

            act.wait_ge(*at("m_abs", 1))
            link(A(ROW[5][:, 0:T], ROW[7][:, 0:T], EXP, scale=-1.0))
            A(ROW[5][:, 0:T], ROW[5][:, 0:T], LN, bias=1.0).then_inc(s("m_lse"), 1)

            for g, q in [(g, q) for g in range(8) for q in range(2)]:
                f = [COPY, COPY, COPY, SILU, COPY, COPY, COPY, SIGM][g]
                if 2 * g + q + 2 < 16:
                    proj_hi(0, 2 * g + q + 2)
                for t in (2 * q, 2 * q + 1):
                    act.wait_ge(*at("proj_pe", 4 * g + t + 1))
                    A(P[:, 4 * g + t, :], PS[:, 4 * (g % 2) + t, 0:T], f, scale=128 ** -0.5 if g == 5 else 1.0).then_inc(s("proj_ev"), 1)

            def norm(p, prepare=lambda: None):
                act.wait_ge(*at(p + "cent", 1))
                A(zT[:, 4:8, :], zT[:, 0:4, :], SQR).then_inc(s(p + "sq"), 1)
                prepare()
                act.wait_ge(*at(p + "var", 1))
                link(A(zT[:, 4:8, :], bank4(0), LN, bias=EPS))
                A(zT[:, 4:8, :], zT[:, 4:8, :], EXP, scale=-0.5).then_inc(s(p + "rstd"), 1)

            for i in range(3):
                n = TILES[i][1]
                act.wait_ge(*at("r_vt", i + 1))
                A(vtok[0:n, i, :], PS[0:n, 3 + i, :], COPY).then_inc(s("r_vtok"), 1)
            for i in range(3):
                n = TILES[i][1]
                act.wait_ge(*at("r_kt", i + 1))
                A(ktok[0:n, i, :], PS[0:n, i, :], COPY).then_inc(s("r_ktok"), 1)
            for h, b in enumerate([0, 1, 2, 5]):
                act.wait_ge(*at("r_o", h + 1))
                A(zT[:, h, :], PS[:, b, 0:T], COPY).then_inc(s("r_oev"), 1)
            act.wait_ge(*at("r_state_pe", 4))
            A(pst[:], PS[:, 6, :].rearrange("p (a b) -> p a b", a=4), COPY).then_inc(s("r_pst"), 1)
            norm("r_")

            act.wait_ge(*at("m_rows", 1))
            A(ROW[6], ROW[6], EXP)
            A(ROW[5][:, 0:T], ROW[5][:, 0:T], EXP).then_inc(s("m_exp"), 1)
            act.wait_ge(*at("m_bc", 4))
            A(ebc, PS[:, 4:8, 0:344], COPY).then_inc(s("m_ebc"), 1)
            act.wait_ge(*at("m_col", 1))
            for h in range(H):
                act.wait_ge(*at("m_ex", h + 1))
                A(att[:, h, 0:A1], att[:, h, 0:A1], EXP, bias=mcol[:, h:h + 1])
                A(att[:, h, A1:A2], att[:, h, A1:A2], EXP, bias=mcol[:, 4 + h:5 + h])
                A(att[0:R2, h, A2:ATT], att[0:R2, h, A2:ATT], EXP, bias=mcol[0:R2, 8 + h:9 + h]).then_inc(s("m_w"), 1)
            for n_, (b, i, dst) in enumerate([(4, 0, ktok), (5, 1, ktok), (6, 2, ktok), (7, 0, vtok), (4, 1, vtok), (5, 2, vtok)]):
                n = TILES[i][1]
                act.wait_ge(*at("m_tpe", n_ + 1))
                A(dst[0:n, i, :], PS[0:n, b, :], COPY).then_inc(s("m_tok"), 1)
            x_hi("out", 0, mix, at("r_out", 1))
            act.wait_ge(*at("m_state_pe", 4))
            act.wait_ge(*at("st_rp", 16))
            A(pst[:], PS[:, 6, :].rearrange("p (a b) -> p a b", a=4), COPY).then_inc(s("m_pst"), 1)
            act.wait_ge(*at("m_npe", 1))
            A(nrow[0:36, :], PS[0:36, 0, 0:128], COPY).then_inc(s("m_nrow"), 1)
            norm("m_", lambda: proj_hi(0, 16))
            act.wait_ge(*at("st_mp", 16))
            proj_hi(0, 17)
            x_hi("out", 1, mix, at("m_out", 1))

            def layer_norm(p, scaled, where=None):
                for c in range(2):
                    act.wait_ge(*at(p + "cent", c + 1))
                    A(mix[:, 4 * c:4 * c + 4, :], zT[:, 4 * c:4 * c + 4, :], SQR).then_inc(s(p + "sq"), 1)
                act.wait_ge(*at(p + "var", 1))
                link(A(mix[:, 1, :], PS[:, LNB[p] + 1, 0:T], LN, bias=LN_EPS))
                A(mix[:, 0, :], mix[:, 1, :], EXP, scale=-0.5).then_inc(s(p + "rstd"), 1)
                if where:
                    for c in range(2):
                        x_hi(where, c, xT, at(p + "x", c + 1))
                if scaled:
                    A(zT[:], xT[:], COPY, scale=ALPHA).then_inc(s(p + "z"), 1)

            def hidden_hi(p, e, j, free):
                act.wait_ge(*at(p + f"w{j // 2 % 2}", e * 96 + 32 * (j // 4 + 1)))
                act.wait_ge(*free)
                A(gu_parts(j, 0), raw_gu(j), COPY).then_inc(s(p + "hi"), 1)

            def ffn_first(layer):
                last_unit = 4 * (OUT0 + 2 if layer == 0 else GEND)
                for j in range(2):
                    hidden_hi(f"f{layer}_", 0, j, at("proj_pe", last_unit - 2 + 2 * j))

            def ffn(layer):
                p, E = f"f{layer}_", (FE, NE)[layer]

                def body(e, is_last):
                    for n in range(2, UN):
                        if n < FT:
                            hidden_hi(p, e, n, at(p + "hid_pe", e * FT + n))
                        else:
                            d = n - FT
                            act.wait_ge(*at(p + f"d{d // 2 % 2}", e * 32 + 16 * (d // 4 + 1)))
                            if d == 1:
                                act.wait_ge(*at(p + "hid_pe", e * FT + FT))
                            elif d >= 2:
                                act.wait_ge(*at(p + "down_pe", e * KT + d))
                            A(down_parts(d, 0), raw_down(d), COPY).then_inc(s(p + "hi"), 1)
                        j = n - 2
                        if j < FT:
                            act.wait_ge(*at(p + "hid_pe", e * FT + (j + 2)))
                            A(gact[:, j % 2, :], PS[:, 2 * (j % 2), 0:T], SILU).then_inc(s(p + "silu"), 1)
                    if not is_last:
                        hidden_hi(p, e + 1, 0, at(p + "hid_pe", e * FT + (FT + 1)))
                        hidden_hi(p, e + 1, 1, at(p + "down_pe", e * KT + (KT + 1)))

                over_experts(act, E, body)

            for i in (18, 19):
                proj_hi(0, i)
            ffn_first(0)
            layer_norm("n0m_", True, "out")
            ffn(0)
            proj_hi(1, 0)
            proj_hi(1, 1)
            layer_norm("n0f_", False, "in1")

            act.wait_ge(*at("small_pe", 2))
            A(GROW[0][:, 0:T], PS[0:4, 5, 0:T], SIGM).then_inc(s("g_beta"), 1)
            act.wait_ge(*at("g_abs", 1))
            A(gates0[0:4, 0:1], gates0[0:4, 0:1], EXP)
            link(A(GROW[6][:, 0:T], GROW[6][:, 0:T], EXP, scale=-1.0))
            A(GROW[6][:, 0:T], GROW[6][:, 0:T], LN, bias=1.0).then_inc(s("g_lse"), 1)
            act.wait_ge(*at("g_gc", 1))
            A(GROW[3][:, 0:T], GROW[2][:, 0:T], EXP)
            A(GROW[5][:, 0:T], GROW[5][:, 0:T], EXP)
            A(GROW[1][:, 0:11], GROW[2][:, T:T + 11], EXP).then_inc(s("g_eg"), 1)

            proj_hi(1, 2)
            act.wait_ge(*at("cin0", 1))

            def conv_out(m):
                act.wait_ge(*at("conv", m + 1))
                A(P[:, m, 0:TP], cacc[:, m % 2, 0:TP], SILU)
                A(smp(P[:, m, :]), cconv(m), SILU).then_inc(s("convs"), 1)

            for g, q in [(g, q) for g in range(IN1, OUT1) for q in range(2)]:
                if 2 * (g - IN1) + q + 3 < 14:
                    proj_hi(1, 2 * (g - IN1) + q + 3)
                for t in (2 * q, 2 * q + 1):
                    m = 4 * (g - IN1) + t
                    act.wait_ge(*at("proj_pe", 4 * g + t + 1))
                    ps = PS[:, 4 * (g % 2) + t, 0:T]
                    if m < 12:
                        if m >= 4:
                            act.wait_ge(*at("conv", m - 3))
                            act.wait_ge(*at("last", m - 3))
                        A(cin[:, m % 4, 3:3 + TP], ps[:, 0:TP], COPY)
                        A(cins(m)[:, :, 3:7], smp(ps), COPY).then_inc(s("cin"), 1)
                        act.wait_ge(*at("cin", m + 1))
                        act.sem_inc(s("proj_ev"), 1)
                        if m:
                            conv_out(m - 1)
                    else:
                        if m == 12:
                            conv_out(11)
                        f = SILU if m < 16 or m >= 24 else COPY
                        A(P[:, m, :], ps, f, scale=64 ** -0.5 if m in (16, 17) else 1.0).then_inc(s("proj_ev"), 1)

            act.wait_ge(*at("convs", 12))
            A(sqn, P[:, 0:8, :], SQR).then_inc(s("g_sqn"), 1)
            act.wait_ge(*at("last_pe", 1))
            A(lastrow[0:27, :], PS[0:27, 0:3, :], COPY).then_inc(s("last_ev"), 1)
            act.wait_ge(*at("g_l2pe", 1))
            A(sqn, PS[:, 0:8, 0:T], LN, bias=EPS).then_inc(s("g_l2a"), 1)
            act.wait_ge(*at("g_l2a", 1))
            A(sqn[:, 0:4, :], sqn[:, 0:4, :], EXP, scale=-0.5, bias=-0.5 * math.log(128))
            A(sqn[:, 4:8, :], sqn[:, 4:8, :], EXP, scale=-0.5).then_inc(s("g_l2r"), 1)
            act.wait_ge(*at("g_bc", 1))
            A(dbc, PS[:, 0:4, T:T + 11], COPY)
            A(qe, bank4(0), EXP).then_inc(s("g_eq"), 1)
            for h in range(H):
                act.wait_ge(*at("g_dx", h + 1))
                for i, (a, n) in enumerate(TILES):
                    last = A(decI[0:n, h, a:a + n], decI[0:n, h, a:a + n], EXP, bias=gcol[0:n, 2, i, h:h + 1])
                last.then_inc(s("g_dec"), 1)
            for i, (a, n) in enumerate(TILES):
                act.wait_ge(*at("g_kt", i + 1))
                A(ktg[0:n, i, :], PS[0:n, i, :], COPY).then_inc(s("g_tok_a"), 1)
            for i, (a, n) in enumerate(TILES):
                act.wait_ge(*at("g_w", i + 1))
                A(kb[:, :, a:a + n], PS[:, i, 0:4 * n].rearrange("p (a b) -> p a b", a=4), COPY, scale=-1.0).then_inc(s("g_wev"), 1)
            act.wait_ge(*at("st_conv", 32))
            for i, (a, n) in enumerate(TILES):
                act.wait_ge(*at("g_upe", i + 1))
                A(ug[0:n, i, :], PS[0:n, 3, :], COPY).then_inc(s("g_ua"), 1)
            act.wait_ge(*at("g_o", 4))
            A(zT[:, 0:3, :], PS[:, 0:3, 0:T], COPY)
            A(zT[:, 3, :], PS[:, 5, 0:T], COPY).then_inc(s("g_oev"), 1)
            act.wait_ge(*at("g_oev", 1))
            A(zT[:, 4:8, :], zT[:, 0:4, :], SQR).then_inc(s("g_sq"), 1)
            act.wait_ge(*at("g_var", 1))
            link(A(zT[:, 4:8, :], bank4(0), LN, bias=EPS))
            A(zT[:, 4:8, :], zT[:, 4:8, :], EXP, scale=-0.5).then_inc(s("g_rstd"), 1)

            act.wait_ge(*at("l_abs", 1))
            link(A(cb_, cb_, EXP, scale=-1.0))
            A(cb_, cb_, LN, bias=1.0).then_inc(s("l_lse"), 1)
            for i, (a, n) in enumerate(TILES):
                act.wait_ge(*at("l_vt", i + 1))
                A(vtl[0:n, i, :], PS[0:n, i, :], COPY).then_inc(s("l_tok"), 1)
            act.wait_ge(*at("l_x", 1))
            A(e1, cb_, EXP)
            A(e2, cb_, EXP, scale=-1.0)
            A(e3, bc_, EXP)
            A(kx_, kx_, EXP).then_inc(s("l_e"), 1)
            act.wait_ge(*at("l_kt", 1))
            for i in range(3):
                n = TILES[i][1]
                A(ktl[0:n, i, :], PS[0:n, 3 + i // 2, 256 * (i % 2):256 * (i % 2) + 256], COPY).then_inc(s("l_tok"), 1)
            x_hi("out", 0, mix, at("g_out", 1))
            act.wait_ge(*at("l_o", 4))
            A(zT[:, 0:4, :], bank4(0), COPY).then_inc(s("l_oev"), 1)
            norm("l_", lambda: proj_hi(1, 14))
            proj_hi(1, 15)
            x_hi("out", 1, mix, at("l_out", 1))
            proj_hi(1, 16)
            proj_hi(1, 17)
            ffn_first(1)
            layer_norm("n1m_", True, "out")
            act.wait_ge(*at("x_lm", 1))
            A(lt, lt, EXP).then_inc(s("x_exp"), 1)
            act.wait_ge(*at("x_bc", 8))
            A(gbc[:, 0:4, :], bank4(0), COPY).then_inc(s("x_bcev"), 1)
            ffn(1)
            layer_norm("n1f_", False)
            for n_ in range(1, 6, 2):
                i, q = n_ // 2, n_ % 2
                n = TILES[i][1]
                act.wait_ge(*at("y_pe", n_ + 1))
                A(proj[0:n, 1024 * i + 512 * q:1024 * i + 512 * q + 512], PS[0:n, n_, :], COPY).then_inc(s("y_ev"), 1)

        @block.gpsimd
        def _(pool):
            pool.wait_ge(*at("ld_c0", 16))
            pool.wait_ge(*at("rot", 1))
            cos = const(C0, "cos").rearrange("p (a b) -> p a b", a=2)
            for a in range(2):
                q = P[:, 4 * a:4 * a + 4, :]
                G.tensor_tensor(q, q, cos[:, a:a + 1, :].to_broadcast([128, 4, T]), MUL).then_inc(s("ropec"), 1)

            def out_state(p, st, dram_s, dram_p):
                for h in range(H):
                    pool.wait_ge(*at(p + "stu", h + 1))
                    pool.dma_start(dram_s[:, h].rearrange("b d e -> d b e"), st[:, h::4, :]).then_inc(s("st_all"), 16)
                pool.wait_ge(*at(p + "pst", 1))
                pool.dma_start(dram_p.rearrange("h d e -> d h e"), pst[:]).then_inc(s("st_" + p[0] + "p"), 16)

            pool.wait_ge(*at("r_vtok", 3))
            gk = const(C0, "gk").rearrange("p (a b) -> p a b", a=2)
            gk2 = const(C0, "gk2").rearrange("p (a b) -> p a b", a=4)
            for i in range(2):
                last = G.tensor_tensor(vd[:, i], vtok[:, i, :].rearrange("p (a b) -> p a b", a=4),
                                       gk[:, i, :].unsqueeze(2).to_broadcast([128, 4, 128]), MUL)
            last.then_inc(s("r_vd"), 1)
            for h in range(H):
                if h >= 2:
                    pool.wait_ge(*at("r_state_pe", h - 1))
                G.tensor_tensor(vb[h % 2][0:R2], vtok[0:R2, 2, 128 * h:128 * h + 128].unsqueeze(1).to_broadcast([R2, SEGS, 128]),
                                gk2[0:R2, h, :].unsqueeze(2).to_broadcast([R2, SEGS, 128]), MUL).then_inc(s("r_vb"), 1)
            out_state("r_", stA, O["sample_ret"], O["prompt_ret"][0])

            pool.wait_ge(*at("m_wl2", 1))
            pool.wait_ge(*at("m_tok", 6))
            for i in range(2):
                last = G.tensor_tensor(vd[:, i], vtok[:, i, :].rearrange("p (a b) -> p a b", a=4),
                                       mcol[:, 12 + 4 * i:16 + 4 * i].unsqueeze(2).to_broadcast([128, 4, 128]), MUL)
            last.then_inc(s("m_vd"), 1)
            for h in range(H):
                if h >= 2:
                    pool.wait_ge(*at("m_state_pe", h - 1))
                G.tensor_tensor(vb[h % 2][0:R2], vtok[0:R2, 2, 128 * h:128 * h + 128].unsqueeze(1).to_broadcast([R2, SEGS, 128]),
                                wl2[0:R2, h, :].unsqueeze(2).to_broadcast([R2, SEGS, 128]), MUL).then_inc(s("m_vb"), 1)
            out_state("m_", stB, O["sample_c"], O["prompt_c"][0])
            pool.wait_ge(*at("m_nrow", 1))
            pool.dma_start(O["sample_n"].rearrange("b h d -> (b h) d"), nrow[0:32, :]).then_inc(s("st_all"), 16)
            pool.dma_start(O["prompt_n"].rearrange("b h d -> (b h) d"), nrow[32:36, :]).then_inc(s("st_all"), 16)
            pool.wait_ge(*at("m_mt", 1))
            pool.dma_start(O["m_rows"], m0[0:4, 0:9]).then_inc(s("st_all"), 16)

            pool.wait_ge(*at("m_out", 1))
            pool.dma_start(cst[:, 0:N1], I["c_layer1"]).then_inc(s("ld_l1"), 16)
            pool.dma_start(gates0[0:4, :], I["gate_cols"][:, 2:4]).then_inc(s("ld_l1"), 16)
            pool.dma_start(wsm[:, :, 0:8], I["w_in1"][:, 2048:2056].rearrange("(k p) n -> p k n", p=128)).then_inc(s("ld_l1"), 16)
            pool.dma_start(wsm[:, :, 8:24], I["w_in1"][:, 3592:3608].rearrange("(k p) n -> p k n", p=128)).then_inc(s("ld_l1"), 16)
            pool.dma_start(walpha, I["gla_w_alpha"]).then_inc(s("ld_l1"), 16)
            pool.wait_ge(*at("st_all", 16 * 11))
            pool.wait_ge(*at("st_rp", 16))
            pool.wait_ge(*at("st_mp", 16))
            pool.wait_ge(*at("f0_down_pe", 1 + FE * KT))
            pool.dma_start(r4b[0:4, :], I["c_rows"]).then_inc(s("ld_gdn"), 16)
            pool.dma_start(stA[:], I["state_gdn"].rearrange("b h d e -> d (b h) e")).then_inc(s("ld_gdn"), 16)
            pool.wait_ge(*at("n0f_x", 2))
            pool.dma_start(halo, I["state_gdn_conv"].rearrange("b w c -> (b w) c")).then_inc(s("ld_halo"), 16)

            for m in range(12):
                pool.wait_ge(*at("cin", m + 1))
                G.tensor_copy(lastT[:, m, 0:3], cin[:, m % 4, TP:TP + 3])
                G.tensor_copy(lastT[:, m, 3:27].rearrange("p (b t) -> p b t", b=NB), cins(m)[:, :, 4:7]).then_inc(s("last"), 1)
            pool.wait_ge(*at("last_ev", 1))
            pool.dma_start(O["prompt_conv"][0], lastrow[0:3, :]).then_inc(s("st_conv"), 16)
            pool.dma_start(O["sample_conv"].rearrange("b w c -> (b w) c"), lastrow[3:27, :]).then_inc(s("st_conv"), 16)

            pool.wait_ge(*at("g_ue", 3))
            blk = const(C1, "blk")
            for h in range(H):
                if h >= 2:
                    pool.wait_ge(*at("g_state_pe", h - 1))
                G.tensor_tensor(ub[h % 2][0:R2], rhsk[0:R2, 2, 128 * h:128 * h + 128].unsqueeze(1).to_broadcast([R2, SEGS, 128]),
                                blk[0:R2].unsqueeze(2).to_broadcast([R2, SEGS, 128]), MUL).then_inc(s("g_vb"), 1)
            pool.wait_ge(*at("g_upe", 3))
            for r in range(2):
                pool.dma_start(stG[64 * r:64 * r + 64], I["state_gla"][:, r::2].rearrange("b p d e -> d b p e")).then_inc(s("ld_stG"), 16)
            for h in range(H):
                pool.wait_ge(*at("g_stu", h + 1))
                pool.dma_start(O["sample_gdn"][:, h].rearrange("b d e -> d b e"), stA[:, h::4, :]).then_inc(s("st_all"), 16)
            pool.wait_ge(*at("g_pst", 1))
            pool.dma_start(O["prompt_gdn"][0].rearrange("h d e -> d h e"), sg[:, 2]).then_inc(s("st_gp"), 16)

            pool.wait_ge(*at("l_tok", 3))
            last = G.tensor_tensor(lvp[0:R2], vtl[0:R2, 2, :].rearrange("p (a b) -> p a b", a=4),
                                   blk[0:R2, 0:1].unsqueeze(2).to_broadcast([R2, 4, 128]), MUL)
            last.then_inc(s("l_vb0"), 1)
            for h in range(H):
                if h >= 2:
                    pool.wait_ge(*at("l_state_pe", h - 1))
                G.tensor_tensor(lb[h % 2][0:R2], vtl[0:R2, 2, 128 * h:128 * h + 128].unsqueeze(1).to_broadcast([R2, SEGS, 128]),
                                blk[0:R2].unsqueeze(2).to_broadcast([R2, SEGS, 128]), MUL).then_inc(s("l_vb"), 1)
            pool.wait_ge(*at("l_sc", 2))
            for r in range(2):
                pool.dma_start(O["prompt_gla"][0, r::2].rearrange("p d e -> d p e"), sc[64 * r:64 * r + 64, 4]).then_inc(s("st_all"), 16)
            pool.wait_ge(*at("l_stu", 4))
            for r in range(2):
                pool.dma_start(O["sample_gla"][:, r::2].rearrange("b p d e -> d b p e"), stG[64 * r:64 * r + 64]).then_inc(s("st_all"), 16)
            pool.wait_ge(*at("l_out", 1))
            pool.dma_start(wrt, I["moe_w_router"].rearrange("(k p) n -> p k n", p=128)).then_inc(s("ld_router"), 16)
            pool.dma_start(brt[0:1, :], I["moe_b_router"].rearrange("(a n) -> a n", a=1)).then_inc(s("ld_router"), 16)
            pool.wait_ge(*at("st_all", 16 * 19))
            pool.wait_ge(*at("st_gp", 16))
            pool.wait_ge(*at("st_conv", 32))

        @block.vector
        def _(dve):
            TT, TSC, STT, CP = V.tensor_tensor, V.tensor_scalar, V.scalar_tensor_tensor, V.tensor_copy
            chain = [0]

            def link(ins):
                chain[0] += 1
                ins.then_inc(s("dve_chain"), 1)
                dve.wait_ge(*at("dve_chain", chain[0]))

            for k in range(0, KT, 2):
                dve.wait_ge(*at("xt_pe", k + 1))
                CP(xT[:, k, :], PS[:, k, 0:T]).then_inc(s("xT"), 1)
            dve.wait_ge(*at("vec_pe", 1))
            CP(vec[:, 0:NVEC], PS[:, 0, 0:NVEC])
            CP(vec[:, NVEC:NVEC + NCONV], PS[:, 0, 128:128 + NCONV])
            CP(nT[:, 0:32], PS[:, 0, 256:288]).then_inc(s("vec_ev"), 1)

            def x_lo(where, chunk, src, n):
                dve.wait_ge(*at("xhi", n))
                k = slice(4 * chunk, 4 * chunk + 4)
                TT(xsplit[where][1][:, k, :], src[:, k, :], xsplit[where][0][:, k, :].bitcast(F32), SUB).then_inc(s("xlo"), 1)

            def proj_lo(layer, i):
                dve.wait_ge(*at("ab"[layer] + "_hi", i + 1))
                g = (0, IN1)[layer] + i // 2
                TT(proj_parts(i, 1), raw_proj(g, i % 2), proj_parts(i, 0).bitcast(F32), SUB).then_inc(s("ab"[layer] + "_lo"), 1)

            for c in range(2):
                x_lo("in0", c, xT, c + 1)
            proj_lo(0, 0)
            proj_lo(0, 1)

            f, i_, b_, a_, M = ROW[1][:, 0:T], ROW[0][:, 0:T], ROW[2][:, 0:T], ROW[3][:, 0:T], ROW[4][:, 0:T]
            ab, l_, pk = ROW[7][:, 0:T], ROW[5][:, 0:T], ROW[6]
            dve.wait_ge(*at("small_pe", 1))
            dve.wait_ge(*at("ld_r", 48))
            TSC(i_, PS[0:4, 6, 0:T], gates0[0:4, 0:1], None, ADD)
            link(TSC(f, PS[0:4, 7, 0:T], gates0[0:4, 1:2], None, ADD))
            STT(ab, f, -1.0, f, MUL, MAX).then_inc(s("m_abs"), 1)
            dve.sem_inc(s("small_ev"), 1)
            dve.wait_ge(*at("m_lse", 1))
            link(STT(f, f, 0.0, l_, MIN, SUB))
            link(V.tensor_tensor_scan(b_, r4[0:4, 0:T], f, 0.0, MUL, ADD))
            link(TT(a_, i_, b_, SUB))
            link(CP(ab, a_))
            link(TSC(ab[:, 0:1], ab[:, 0:1], 0.0, None, MAX))
            link(TT(smp(ab)[:, :, 0], smp(ab)[:, :, 0], m0[0:4, 0:8], MAX))
            link(V.tensor_tensor_scan(M, r4[0:4, T:2 * T], ab, 0.0, ADD, MAX))
            STT(pk[:, 0:T], b_, -1.0, M, MUL, SUB)
            TT(pk[:, T:T + TS].rearrange("p (b t) -> p b t", b=NB), m0[0:4, 0:8].unsqueeze(2).to_broadcast([4, NB, NS]), smp(M), SUB)
            TT(pk[:, T + TS:T + TS + NB], m0[0:4, 0:8], smp(M)[:, :, NS - 1], SUB)
            TSC(l_[:, 0:TP], a_[:, 0:TP], M[:, TP - 1:TP], None, SUB)
            link(TT(smp(l_), smp(a_), smp(M)[:, :, NS - 1:NS].to_broadcast([4, NB, NS]), SUB))
            link(STT(m0[0:4, 0:8], smp(b_)[:, :, NS - 1], 0.0, smp(M)[:, :, NS - 1], ADD, ADD))
            TT(m0[0:4, 8:9], b_[:, TP - 1:TP], M[:, TP - 1:TP], ADD).then_inc(s("m_mt"), 1)
            dve.sem_inc(s("m_rows"), 1)

            for i in range(2, 2 * OUT0):
                proj_lo(0, i)

            def norm(p, dst, gate0, gain, rms=False, prepare=lambda: None):
                if not rms:
                    dve.wait_ge(*at(p + "mean", 1))
                    TT(zT[:, 0:4, :], zT[:, 0:4, :], bank4(0), SUB).then_inc(s(p + "cent"), 1)
                prepare()
                dve.wait_ge(*at(p + "rstd", 1))
                link(TT(zT[:, 0:4, :], zT[:, 0:4, :], zT[:, 4:8, :], MUL))
                for h in range(H):
                    g = vec[:, VEC[gain] + h:VEC[gain] + h + 1]
                    if gate0 is None:
                        last = TSC(mix[:, dst + h, :], zT[:, h, :], g, None, MUL)
                    else:
                        last = STT(mix[:, dst + h, :], zT[:, h, :], g, P[:, gate0 + h, :], MUL, MUL)
                last.then_inc(s(p + "out"), 1)

            def state_update(p, st, h, banks, decay):
                v = st[:, h::4, :]
                if decay is None:
                    for j, b in enumerate(banks):
                        last = STT(v[:, 4 * j:4 * j + 4, :], v[:, 4 * j:4 * j + 4, :], math.exp(4 * math.log(1 - 2.0 ** (-5 - h))),
                                   PS[:, b, :].rearrange("p (a b) -> p a b", a=4), MUL, ADD)
                else:
                    link(TT(v, v, decay.unsqueeze(2).to_broadcast([128, NB, 128]), MUL))
                    for j, b in enumerate(banks):
                        last = TT(v[:, 4 * j:4 * j + 4, :], v[:, 4 * j:4 * j + 4, :], PS[:, b, :].rearrange("p (a b) -> p a b", a=4), ADD)
                last.then_inc(s(p + "stu"), 1)

            dve.wait_ge(*at("ld_c0", 16))
            dve.wait_ge(*at("rot", 1))
            sin = const(C0, "sin").rearrange("p (a b) -> p a b", a=2)
            for a in range(2):
                last = TT(zT[:, 4 * a:4 * a + 4, :], bank4(4 * a), sin[:, a:a + 1, :].to_broadcast([128, 4, T]), MUL)
            link(last)
            dve.sem_inc(s("rotm"), 1)
            dve.wait_ge(*at("ropec", 2))
            link(TT(P[:, 0:8, :], P[:, 0:8, :], zT[:], ADD))
            dve.sem_inc(s("rope"), 1)
            TT(qs, P[:, 0:4, TP:T], const(C0, "gq").rearrange("p (a b) -> p a b", a=4), MUL).then_inc(s("r_qs"), 1)
            dec = const(C0, "dec").rearrange("p (a b) -> p a b", a=4)
            for h, b in enumerate([6, 7, 3, 4]):
                dve.wait_ge(*at("r_qk", h + 1))
                TT(att[:, h, 0:A2], PS[:, b, 0:A2], dec[:, h, 0:A2], MUL)
                TT(att[0:R2, h, A2:ATT], PS[0:R2, b, A2:ATT], dec[0:R2, h, A2:ATT], MUL).then_inc(s("r_att"), 1)
            for h in range(H):
                dve.wait_ge(*at("r_state_pe", h + 1))
                state_update("r_", stA, h, [(7, 3), (4, 5)][h % 2], None)
            norm("r_", 0, 12, "ret")

            mask = const(C0, "mask")
            dve.wait_ge(*at("m_colpe", 1))
            CP(mcol[:, 0:8], PS[:, 7, 0:8])
            CP(mcol[0:R2, 8:12], PS[0:R2, 7, 8:12])
            CP(mcol[:, 12:20], PS[:, 7, 12:20])
            link(CP(mcol[0:R2, 20:24], PS[0:R2, 7, 20:24]))
            dve.sem_inc(s("m_col"), 1)
            TT(wl2[0:R2], mcol[0:R2, 20:24].unsqueeze(2).to_broadcast([R2, 4, 9]), const(C0, "blk")[0:R2].unsqueeze(1).to_broadcast([R2, 4, 9]),
               MUL).then_inc(s("m_wl2"), 1)
            for h in range(H):
                dve.wait_ge(*at("m_bc", h + 1))
                TT(att[:, h, 0:A1], mask[:, 0:A1], PS[:, h, 0:TP], SUB)
                TT(att[:, h, A1:A2], mask[:, A1:A2], PS[:, h, 128:TP], SUB)
                TT(att[0:R2, h, A2:ATT], mask[0:R2, A2:ATT], PS[0:R2, h, 256:T], SUB).then_inc(s("m_ex"), 1)
            dve.wait_ge(*at("m_ebc", 1))
            TT(qs, P[:, 16:20, TP:T], ebc[:, :, T:T + TS], MUL).then_inc(s("m_qs"), 1)
            for h in range(H):
                dve.wait_ge(*at("m_qk", h + 1))
                dve.wait_ge(*at("m_w", h + 1))
                TT(att[:, h, 0:A2], PS[:, h, 0:A2], att[:, h, 0:A2], MUL)
                TT(att[0:R2, h, A2:ATT], PS[0:R2, h, A2:ATT], att[0:R2, h, A2:ATT], MUL).then_inc(s("m_att"), 1)
            x_lo("out", 0, mix, 3)
            dve.wait_ge(*at("m_o", 4))
            o, d = zT[:, 0:4, :], zT[:, 4:8, :]
            link(TT(d, bank4(4), ebc[:, :, 0:T], MAX))
            link(STT(d, bank4(4), -1.0, d, MUL, MAX))
            link(V.reciprocal(d, d))
            link(TT(d, d, P[:, 28:32, :], MUL))
            TT(o, bank4(0), d, MUL).then_inc(s("m_oev"), 1)
            for h in range(H):
                dve.wait_ge(*at("m_state_pe", h + 1))
                state_update("m_", stB, h, [(7, 3), (4, 2)][h % 2], ebc[:, h, T + TS:T + TS + NB])
                n = nT[:, h:32:4]
                link(TT(n, n, ebc[:, h, T + TS:T + TS + NB], MUL))
                TT(n, n, PS[:, 5, 9 * h + 1:9 * h + 9], ADD)
                last = CP(nT[:, 32 + h:33 + h], PS[:, 5, 9 * h:9 * h + 1])
            last.then_inc(s("m_nst"), 1)
            norm("m_", 4, None, "mlstm", prepare=lambda: proj_lo(0, 16))
            x_lo("out", 1, mix, 4)
            proj_lo(0, 17)

            def residual(layer):
                g0, i0 = ((OUT0, 2 * OUT0), (OUT1, 2 * (OUT1 - IN1)))[layer]
                for u in range(4):
                    if u < 2:
                        proj_lo(layer, i0 + 2 + u)
                    for k in (2 * u, 2 * u + 1):
                        g = g0 + k // 4
                        dve.wait_ge(*at("proj_pe", 4 * g + k % 4 + 1))
                        STT(zT[:, k, :], xT[:, k, :], ALPHA, PS[:, 4 * (g % 2) + k % 4, 0:T], MUL, ADD).then_inc(s("proj_ev"), 1)

            def layer_norm(p, gain, prepare=lambda: None):
                dve.wait_ge(*at(p + "mean", 1))
                for c in range(2):
                    z = zT[:, 4 * c:4 * c + 4, :]
                    TT(z, z, PS[:, LNB[p]:LNB[p] + 1, 0:T].to_broadcast([128, 4, T]), SUB).then_inc(s(p + "cent"), 1)
                prepare()
                dve.wait_ge(*at(p + "rstd", 1))
                for c in range(2):
                    z = zT[:, 4 * c:4 * c + 4, :]
                    link(TT(z, z, mix[:, 0:1, :].to_broadcast([128, 4, T]), MUL))
                    for k in range(4 * c, 4 * c + 4):
                        g = VEC[gain + "_g"] + k
                        last = TSC(xT[:, k, :], zT[:, k, :], vec[:, g:g + 1], vec[:, g + 8:g + 9], MUL, ADD)
                    last.then_inc(s(p + "x"), 1)

            def hidden_lo(p, e, j):
                dve.wait_ge(*at(p + "hi", e * UN + (j + 1)))
                TT(gu_parts(j, 1), raw_gu(j), gu_parts(j, 0).bitcast(F32), SUB).then_inc(s(p + "lo"), 1)

            def ffn_first(layer):
                p = f"f{layer}_"
                dve.sem_inc(s(p + "lo"), UC)
                hidden_lo(p, 0, 0)
                hidden_lo(p, 0, 1)

            def ffn(layer):
                p, E = f"f{layer}_", (FE, NE)[layer]
                steps = 1 + layer
                dve.sem_inc(s(p + "hid_ev"), 1)
                dve.sem_inc(s(p + "down_ev"), 4)

                def hidden(e, j):
                    dve.wait_ge(*at(p + "silu", e * FT + (j + 1)))
                    a, b, n = gact[:, j % 2, :], PS[:, 2 * (j % 2) + 1, 0:T], e * (steps * FT) + (steps * j + 1)
                    if layer == 1:
                        TT(gu_raw, a, b, MUL).then_inc(s(p + "gu"), 1)
                        dve.wait_ge(*at(p + "gu", n))
                        a, b, n = gu_raw, gbc[:, e, :], n + 1
                    TT(hraw[:, j % 2, :], a, b, MUL)
                    TT(hsplit[0][:, j, :], a, b, MUL).then_inc(s(p + "gu"), 1)
                    dve.wait_ge(*at(p + "gu", n))
                    TT(hsplit[1][:, j, :], hraw[:, j % 2, :], hsplit[0][:, j, :].bitcast(F32), SUB).then_inc(s(p + "hid_ev"), 1)

                def add(e, d):
                    dve.wait_ge(*at(p + "down_pe", e * KT + (d + 2)))
                    TT(zT[:, d, :], zT[:, d, :], PS[:, 4 + d % 4, 0:T], ADD).then_inc(s(p + "down_ev"), 1)

                def body(e, is_last):
                    for n in range(2, UN):
                        if n < FT:
                            hidden_lo(p, e, n)
                        else:
                            dve.wait_ge(*at(p + "hi", e * UN + (n + 1)))
                            d = n - FT
                            TT(down_parts(d, 1), raw_down(d), down_parts(d, 0).bitcast(F32), SUB).then_inc(s(p + "lo"), 1)
                        if n - 2 < FT:
                            hidden(e, n - 2)
                        else:
                            add(e, n - 2 - FT)
                    for j in range(2):
                        if not is_last:
                            hidden_lo(p, e + 1, j)
                        add(e, KT - 2 + j)

                over_experts(dve, E, body)

            residual(0)
            layer_norm("n0m_", "mix0", lambda: ffn_first(0))
            for c in range(2):
                x_lo("out", c, xT, 5 + c)
            dve.wait_ge(*at("n0m_z", 1))
            dve.wait_ge(*at("st_all", 16 * 11))
            ffn(0)

            def first_lo():
                proj_lo(1, 0)
                proj_lo(1, 1)

            layer_norm("n0f_", "ffn0", first_lo)
            for c in range(2):
                x_lo("in1", c, xT, 7 + c)

            V.memset(cin[:, :, 0:3], 0.0)
            x_, tmp, gc = GROW[1][:, 0:T], GROW[6][:, 0:T], GROW[2]
            dve.wait_ge(*at("small_pe", 2))
            dve.wait_ge(*at("ld_l1", 80))
            dve.wait_ge(*at("ld_gdn", 32))
            CP(lrT, PS[0:16, 7, 0:T])
            link(TSC(x_, PS[0:4, 6, 0:T], gates0[0:4, 1:2], None, ADD))
            STT(tmp, x_, -1.0, x_, MUL, MAX).then_inc(s("g_abs"), 1)
            dve.wait_ge(*at("g_beta", 1))
            dve.sem_inc(s("small_ev"), 1)
            dve.wait_ge(*at("g_lse", 1))
            link(STT(x_, x_, 0.0, tmp, MAX, ADD))
            link(TSC(x_, x_, gates0[0:4, 0:1], -1.0, MUL, MUL))
            link(V.tensor_tensor_scan(gc[:, 0:T], r4b[0:4, 2 * T:3 * T], x_, 0.0, MUL, ADD))
            CP(gc[:, T:T + 2], gc[:, 127:256:128])
            CP(gc[:, T + 2:T + 3], gc[:, TP - 1:TP])
            CP(gc[:, T + 3:T + 11], smp(gc)[:, :, NS - 1])
            TSC(GROW[4][:, 0:T], gc[:, 0:T], -1.0, None, MUL)
            for a, n in [(0, 128), (128, 128), (256, PR2)]:
                TSC(GROW[5][:, a:a + n], gc[:, a:a + n], -1.0, gc[:, a + n - 1:a + n], MUL, ADD)
            TT(smp(GROW[5]), smp(gc)[:, :, NS - 1:NS].to_broadcast([4, NB, NS]), smp(gc), SUB).then_inc(s("g_gc"), 1)
            dve.wait_ge(*at("g_eg", 1))
            TT(GROW[3][:, 0:T], GROW[3][:, 0:T], GROW[0][:, 0:T], MUL)
            CP(gc[:, T:T + 11], GROW[1][:, 0:11]).then_inc(s("g_rows"), 1)

            proj_lo(1, 2)
            dve.wait_ge(*at("halo_pe", 1))
            link(CP(convT, PS[:, 4, 0:288].rearrange("p (a b) -> p a b", a=12)))
            dve.sem_inc(s("cin0"), 1)

            n_ = CONVW - 3
            for m in range(12):
                if m % 2 == 0:
                    proj_lo(1, m // 2 + 3)
                if m >= 4:
                    dve.wait_ge(*at("conv", m - 3))
                    dve.wait_ge(*at("last", m - 3))
                dve.wait_ge(*at("cin", m + 1))
                link(CP(cins(m)[:, :, 0:3], convT[:, m, :].rearrange("p (b t) -> p b t", b=NB)))
                if m >= 2:
                    dve.wait_ge(*at("convs", m - 1))
                w = [vec[:, NVEC + 12 * j + m:NVEC + 12 * j + m + 1] for j in range(4)]
                acc, src = cacc[:, m % 2, 0:n_], cin[:, m % 4, :]
                link(TSC(acc, src[:, 0:n_], w[0], None, MUL))
                link(STT(acc, src[:, 1:1 + n_], w[1], acc, MUL, ADD))
                link(STT(acc, src[:, 2:2 + n_], w[2], acc, MUL, ADD))
                STT(acc, src[:, 3:3 + n_], w[3], acc, MUL, ADD).then_inc(s("conv"), 1)

            for i in range(9, 14):
                proj_lo(1, i)

            dve.wait_ge(*at("g_l2r", 1))
            link(TT(P[:, 0:8, :], P[:, 0:8, :], sqn, MUL))
            dve.wait_ge(*at("g_colpe", 1))
            CP(gcol[:, :, 0:2, :], PS[:, 0, 0:48].rearrange("p (a b c) -> p a b c", a=4, b=3)[:, :, 0:2, :])
            CP(gcol[0:R2, :, 2, :], PS[0:R2, 0, 0:48].rearrange("p (a b c) -> p a b c", a=4, b=3)[:, :, 2, :]).then_inc(s("g_col"), 1)
            dve.wait_ge(*at("g_bc", 1))
            dve.wait_ge(*at("g_eq", 1))
            incl, strict = const(C1, "incl"), const(C1, "strict")
            for h in range(H):
                TT(decI[:, h, 0:256], PS[:, h, 0:256], incl[:, 0:256], ADD)
                TT(decI[0:R2, h, 256:T], PS[0:R2, h, 256:T], incl[0:R2, 256:T], ADD).then_inc(s("g_dx"), 1)
            dve.wait_ge(*at("g_dx", 4))
            dve.sem_inc(s("g_bcev"), 1)
            TT(kb, P[:, 4:8, :], bank4(4), MUL).then_inc(s("g_kb"), 1)
            TT(qe, qe, P[:, 0:4, :], MUL)

            def parts(v):
                return [v[:, :, 0:256], v[0:R2, :, 256:T]]

            def maskb(name):
                v = const(C1, name)
                return [v[:, 0:256].unsqueeze(1).to_broadcast([128, H, 256]), v[0:R2, 256:T].unsqueeze(1).to_broadcast([R2, H, R2])]

            dve.wait_ge(*at("g_aa", 4))
            dve.wait_ge(*at("g_dec", 4))
            for v, p_, d_ in zip(parts(SDT), parts(bank4(0)), parts(decI)):
                last = TT(v, p_, d_, MUL)
            link(last)
            for v, m_ in zip(parts(SDT), maskb("strict")):
                last = TT(v, v, m_, MUL)
            last.then_inc(s("g_at"), 1)
            dve.wait_ge(*at("g_qk", 4))
            for v, p_, d_ in zip(parts(attg), parts(bank4(4)), parts(decI)):
                last = TT(v, p_, d_, MUL)
            last.then_inc(s("g_att"), 1)

            def scaled_tokens(dst, i, bank, col):
                n = TILES[i][1]
                return TT(dst[0:n, i, :].rearrange("p (a b) -> p a b", a=4), PS[0:n, bank, :].rearrange("p (a b) -> p a b", a=4),
                          gcol[0:n, col, i, :].unsqueeze(2).to_broadcast([n, 4, 128]), MUL)

            dve.wait_ge(*at("g_tok_a", 3))
            for i in range(3):
                scaled_tokens(rhsk, i, i, 1).then_inc(s("g_tok_d"), 1)
            for i in range(3):
                dve.wait_ge(*at("g_vt", i + 1))
                scaled_tokens(rhsv, i, 4 + i, 0).then_inc(s("g_tok_d"), 1)

            def tile(v, i):
                a, n = TILES[i]
                return v[0:n, :, a:a + n]

            def tmask(name, i):
                a, n = TILES[i]
                return const(C1, name)[0:n, a:a + n].unsqueeze(1).to_broadcast([n, H, n])

            for n_, (k, i) in enumerate(ORDER):
                what, out, lhs, rhs, _ = SOLVE[k]
                n = TILES[i][1]
                dve.wait_ge(*at("sv_pe", n_ + 1))
                ps = PS[0:n, n_ % 8, 0:4 * n].rearrange("p (a b) -> p a b", a=4)
                if what == "split":
                    TT(tile(SD, i), ps, tmask("same8", i), MUL)
                    link(TT(tile(SDT, i), tile(SDT, i), tmask("same8", i), MUL))
                    TT(tile(SO, i), ps, tile(SD, i), SUB)
                    TT(tile(SRT, i), tmask("eye", i), tile(SDT, i), SUB).then_inc(s("sv_ev"), 1)
                elif what == "add":
                    TT(tile(out, i), tile(out, i), ps, ADD).then_inc(s("sv_ev"), 1)
                else:
                    last = CP(tile(out, i), ps)
                    if what == "copyz":
                        last = TT(tile(SO, i), tmask("eye", i), ps, SUB)
                    last.then_inc(s("sv_ev"), 1)

            dve.wait_ge(*at("g_wev", 3))
            for h in range(H):
                last = TT(wtm[:, h], kb[:, h:h + 1, 256:T].to_broadcast([128, SEGS, R2]),
                          const(C1, "seg9").rearrange("p (a b) -> p a b", a=SEGS), MUL)
            last.then_inc(s("g_wtm"), 1)
            for i in range(3):
                dve.wait_ge(*at("g_upe", i + 1))
                dve.wait_ge(*at("g_ua", i + 1))
                scaled_tokens(rhsk, i, 3, 3).then_inc(s("g_ue"), 1)
                if i == 0:
                    dve.wait_ge(*at("g_spe", 1))
                    CP(sg[:, 0], PS[:, 5, :].rearrange("p (a b) -> p a b", a=4)).then_inc(s("g_s"), 1)
                if i == 1:
                    dve.wait_ge(*at("g_spe", 2))
                    for h in range(H):
                        last = STT(sg[:, 1, h, :], sg[:, 0, h, :], dbc[:, h, 1:2], PS[:, 5, 128 * h:128 * h + 128], MUL, ADD)
                    last.then_inc(s("g_s"), 1)
            for h in range(H):
                dve.wait_ge(*at("g_state_pe", h + 1))
                state_update("g_", stA, h, [(7, 3), (4, 5)][h % 2], dbc[:, h, 3:11])
            for h in range(H):
                last = STT(sg[:, 2, h, :], sg[:, 1, h, :], dbc[:, h, 2:3], PS[:, 6, 128 * h:128 * h + 128], MUL, ADD)
            last.then_inc(s("g_pst"), 1)
            norm("g_", 0, 12, "gdn", rms=True)

            dve.wait_ge(*at("l_alpha", 1))
            dve.wait_ge(*at("g_stu", 4))
            for p in range(2):
                last = TSC(bc_[:, p, :], PS[:, 6 + p, 0:T], vec[:, VEC["balpha"] + p:VEC["balpha"] + p + 1], None, ADD)
            link(last)
            STT(cb_, bc_, -1.0, bc_, MUL, MAX).then_inc(s("l_abs"), 1)
            dve.wait_ge(*at("l_lse", 1))
            link(STT(bc_, bc_, 0.0, cb_, MIN, SUB))
            link(TSC(kx_, bc_, 1.0 / 16.0, None, MUL))
            for p in range(2):
                last = V.tensor_tensor_scan(bc_[:, p, :], const(C1, "rst"), kx_[:, p, :], 0.0, MUL, ADD)
            link(last)
            for p in range(2):
                for v, n, k, mid in ((slice(0, 256), 64, 4, 31), (slice(256, TP), PR2, 1, 7), (slice(TP, T), NS, NB, 1)):
                    x4 = bc_[:, p, v].rearrange("p (c t) -> p c t", t=n)
                    TT(cb_[:, p, v].rearrange("p (c t) -> p c t", t=n), x4, x4[:, :, mid:mid + 1].to_broadcast([128, k, n]), SUB)
                    last = TT(kx_[:, p, v].rearrange("p (c t) -> p c t", t=n), x4[:, :, n - 1:n].to_broadcast([128, k, n]), x4, SUB)
            last.then_inc(s("l_x"), 1)
            dve.wait_ge(*at("l_e", 1))
            TT(q1, P[:, 16:18, :], e1, MUL)
            TT(k1, P[:, 18:20, :], e2, MUL)
            link(TT(k2, P[:, 18:20, :], kx_, MUL))
            V.memset(q2[64:128, 0:4:2, :], 0.0)
            link(V.memset(q2[0:64, 1:4:2, :], 0.0))
            for h in range(H):
                r = slice(64 * (h % 2), 64 * (h % 2) + 64)
                last = TT(q2[r, h, :], P[r, 16 + h // 2, :], e3[r, h // 2, :], MUL)
            last.then_inc(s("l_dqk"), 1)
            for h, b in enumerate([5, 6, 7, 0]):
                dve.wait_ge(*at("l_qk", h + 1))
                if h == 0:
                    dve.wait_ge(*at("st_gp", 16))
                gm = const(C1, "gla")
                TT(attl[:, h, 0:256], PS[:, b, 0:256], gm[:, 0:256], MUL)
                TT(attl[0:R2, h, 256:T], PS[0:R2, b, 256:T], gm[0:R2, 256:T], MUL).then_inc(s("l_att"), 1)
            for p in range(2):
                dve.wait_ge(*at("l_upe", p + 1))
                for c in range(5):
                    for q in range(2):
                        r = slice(64 * q, 64 * q + 64)
                        u = PS[r, 3, 128 * q:128 * q + 128] if c == 4 else PS[r, 1 + c % 2, 256 * (c // 2) + 128 * q:256 * (c // 2) + 128 * q + 128]
                        end = 64 * c + 63 if c < 4 else TP - 1
                        if c == 0:
                            last = CP(sc[r, 0, p, :], u)
                        else:
                            last = STT(sc[r, c, p, :], sc[r, c - 1, p, :], e3[r, p, end:end + 1], u, MUL, ADD)
                    link(last)
                dve.sem_inc(s("l_sc"), 1)
            for h in range(H):
                r, p = slice(64 * (h % 2), 64 * (h % 2) + 64), h // 2
                dve.wait_ge(*at("l_state_pe", h + 1))
                v = stG[r, p::2, :]
                link(TT(v, v, smp(e3[r, p, :])[:, :, NS - 1:NS].to_broadcast([64, NB, 128]), MUL))
                for j, b in enumerate([(4, 5), (6, 7)][h % 2]):
                    last = TT(v[:, 4 * j:4 * j + 4, :], v[:, 4 * j:4 * j + 4, :], PS[r, b, :].rearrange("p (a b) -> p a b", a=4), ADD)
                last.then_inc(s("l_stu"), 1)
            x_lo("out", 0, mix, 9)
            norm("l_", 4, 24, "gla", prepare=lambda: proj_lo(1, 14))
            x_lo("out", 1, mix, 10)
            proj_lo(1, 15)

            residual(1)
            layer_norm("n1m_", "mix1", lambda: ffn_first(1))
            for c in range(2):
                x_lo("out", c, xT, 11 + c)

            link(V.memset(lt, 0.0))
            dve.wait_ge(*at("x_log", 1))
            CP(lt[:, 0:2, :], PS[:, 2, 0:16].rearrange("p (a b) -> p a b", a=2))
            link(CP(lt[0:R2, 2, :], PS[0:R2, 2, 16:24]))
            link(V.tensor_reduce(st3[:, :, 0], lt, AX.X, MAX))
            TT(lt, lt, st3[:, :, 0:1].to_broadcast([128, 3, NE]), SUB).then_inc(s("x_lm"), 1)
            dve.wait_ge(*at("x_exp", 1))
            link(V.tensor_reduce(st3[:, :, 1], lt, AX.X, ADD))
            link(V.reciprocal(st3[:, :, 2], st3[:, :, 1]))
            link(TT(lt, lt, st3[:, :, 2:3].to_broadcast([128, 3, NE]), MUL))
            for i in range(3):
                other = lt[:, i:i + 1, :].to_broadcast([128, NE, NE])
                own = lt[:, i, :].unsqueeze(2).to_broadcast([128, NE, NE])
                TT(gcmp[:, i, :].rearrange("p (a b) -> p a b", a=NE), other, own, ALU.is_gt)
                last = TT(geq[:, i, :].rearrange("p (a b) -> p a b", a=NE), other, own, ALU.is_equal)
            link(last)
            link(TT(geq, geq, const(C1, "tri").unsqueeze(1).to_broadcast([128, 3, 64]), MUL))
            link(TT(gcmp, gcmp, geq, ADD))
            link(V.tensor_reduce(lm, gcmp.rearrange("p a (b c) -> p a b c", b=NE), AX.X, ADD))
            link(TSC(lm, lm, 1.5, None, ALU.is_lt))
            link(TT(gate, lm, lt, MUL))
            link(V.tensor_reduce(st3[:, :, 3], gate, AX.X, ADD))
            link(V.reciprocal(st3[:, :, 4], st3[:, :, 3]))
            TT(gate, gate, st3[:, :, 4:5].to_broadcast([128, 3, NE]), MUL).then_inc(s("x_gate"), 1)
            dve.wait_ge(*at("x_gt", 1))
            CP(gT[0:8, :], PS[0:8, 3, 0:T]).then_inc(s("x_gtev"), 1)
            dve.wait_ge(*at("x_bc", 8))
            CP(gbc[:, 4:8, :], bank4(4)).then_inc(s("x_bcev"), 1)
            dve.wait_ge(*at("n1m_z", 1))
            dve.wait_ge(*at("st_all", 16 * 19))
            dve.wait_ge(*at("st_conv", 32))
            ffn(1)
            layer_norm("n1f_", "ffn1")
            for n_ in range(0, 6, 2):
                i, q = n_ // 2, n_ % 2
                n = TILES[i][1]
                dve.wait_ge(*at("y_pe", n_ + 1))
                CP(proj[0:n, 1024 * i:1024 * i + 512], PS[0:n, n_, :]).then_inc(s("y_ev"), 1)


def _constants(np):
    f = np.float32
    cc = np.zeros((128, 512), f)
    cc[:, 0:128] = np.eye(128)
    cc[:, 128:256] = 1.0 / D
    cc[:, 256:384] = 1.0 / 128
    cc[:, 384:512] = 1.0
    c0 = np.zeros((128, N0), f)

    def put(c, table, name, v):
        a, n = table[name]
        v = np.asarray(v, np.float64).reshape(v.shape[0], n)
        c[:v.shape[0], a:a + n] = v

    rot = np.zeros((128, 128))
    for j in range(64):
        rot[64 + j, j] = -1.0
        rot[j, 64 + j] = 1.0
    put(c0, C0, "rot", rot)
    pos = np.concatenate([np.arange(TP), np.tile(2048 + np.arange(NS), NB)]).astype(f)
    inv = (10000.0 ** (-np.arange(64, dtype=f) / f(64))).astype(f)
    ang = np.tile((pos[None, :] * inv[:, None]).astype(f), (2, 1)).astype(np.float64)
    for name, v in (("cos", np.cos(ang)), ("sin", np.sin(ang))):
        put(c0, C0, name, np.stack([v, v * 128 ** -0.5], 1))
    seq = np.concatenate([np.zeros(TP, int), 1 + np.arange(TS) // NS])
    idx = np.concatenate([np.arange(TP), np.arange(TS) % NS])
    ln = np.concatenate([np.full(TP, TP), np.full(TS, NS)])
    gam = 1.0 - 2.0 ** (-5.0 - np.arange(H))
    ok = (seq[:, None] == seq[None, :]) & (idx[None, :] >= idx[:, None])
    diff = np.where(ok, idx[None, :] - idx[:, None], 0)
    dec = np.zeros((128, H, ATT))
    mask = np.full((128, ATT), -1e30)
    for (a, n), (lo, hi), at in zip(TILES, ((0, TP), (128, TP), (256, T)), (0, A1, A2)):
        w = hi - lo
        mask[:n, at:at + w] = np.where(ok[a:a + n, lo:hi], 0.0, -1e30)
        for h in range(H):
            dec[:n, h, at:at + w] = np.where(ok[a:a + n, lo:hi], gam[h] ** diff[a:a + n, lo:hi], 0.0)
    put(c0, C0, "dec", dec)
    put(c0, C0, "mask", mask)
    put(c0, C0, "gq", np.broadcast_to((gam[:, None] ** (idx[TP:] + 1.0)[None, :])[None], (128, H, TS)))
    gk = gam[None, :] ** (ln - 1 - idx)[:, None]
    put(c0, C0, "gk", np.stack([gk[0:128], gk[128:256]], 1))
    blk = (seq[256:, None] == np.arange(SEGS)[None, :]).astype(f)
    put(c0, C0, "gk2", gk[256:, :, None] * blk[:, None, :])
    put(c0, C0, "blk", blk)
    c1 = np.zeros((128, N1), f)
    chunk = np.concatenate([np.arange(256) // 64, np.full(PR2, 4), 5 + np.arange(TS) // NS])
    tabs = {n: np.zeros((128, T)) for n in ("strict", "same8", "eye", "gla")}
    incl = np.full((128, T), -1e30)
    for a, n in TILES:
        q = ok[a:a + n, a:a + n]
        r = np.arange(n)
        incl[:n, a:a + n] = np.where(q, 0.0, -1e30)
        tabs["strict"][:n, a:a + n] = q & (r[None, :] > r[:, None])
        tabs["same8"][:n, a:a + n] = (r[None, :] // 8) == (r[:, None] // 8)
        tabs["eye"][:n, a:a + n] = np.eye(n)
        tabs["gla"][:n, a:a + n] = q & (chunk[a:a + n, None] == chunk[None, a:a + n])
    put(c1, C1, "incl", incl)
    for n_, v in tabs.items():
        put(c1, C1, n_, v)
    start = np.ones(T)
    start[[0, 64, 128, 192, 256, *range(TP, T, NS)]] = 0
    put(c1, C1, "rst", np.broadcast_to(start, (128, T)))
    put(c1, C1, "seg9", np.broadcast_to(blk.T[None], (128, SEGS, R2)))
    put(c1, C1, "blk", blk)
    put(c1, C1, "tri", np.broadcast_to(np.tril(np.ones((NE, NE)), -1)[None], (128, NE, NE)))
    r4 = np.zeros((4, N4), f)
    first = idx == 0
    r4[:, 0:T] = np.where(first, 0.0, 1.0)
    r4[:, T:2 * T] = np.where(first, -3e38, 0.0)
    g = np.where(first, 0.0, 1.0)
    g[[128, 256]] = 0.0
    r4[:, 2 * T:3 * T] = g
    return {"c_common": cc, "c_layer0": c0, "c_layer1": c1, "c_rows": r4}


_DIRECT = ["state_ret", "state_mlstm_c", "state_mlstm_n", "state_gdn", "state_gdn_conv", "state_gla", "w_in0", "w_out0",
           "ffn0_w_gate", "ffn0_w_up", "ffn0_w_down", "w_in1", "gla_w_alpha", "w_out1", "moe_w_router", "moe_b_router",
           "moe_w_gate", "moe_w_up", "moe_w_down"]
_OUTS = {"y_all": (T, D), "prompt_ret": (1, 4, 128, 128), "prompt_c": (1, 4, 128, 128), "prompt_n": (1, 4, 128), "m_rows": (4, 9),
         "prompt_gdn": (1, 4, 128, 128), "prompt_conv": (1, 3, QKV), "prompt_gla": (1, 4, 64, 128), "sample_ret": (NB, 4, 128, 128),
         "sample_c": (NB, 4, 128, 128), "sample_n": (NB, 4, 128), "sample_gdn": (NB, 4, 128, 128), "sample_conv": (NB, 3, QKV),
         "sample_gla": (NB, 4, 64, 128)}


def kernel(**inputs):
    import numpy as np
    import concourse.bacc as bacc
    from concourse.bass_utils import run_bass_kernel_spmd

    x = {k: np.asarray(v) for k, v in inputs.items()}
    arrays = {n: np.ascontiguousarray(x[n]) for n in _DIRECT}
    arrays["x_all"] = np.concatenate([x["meta_tokens"], x["x_prompt"].reshape(SEQ, D), x["x_sample"].reshape(TS, D)])
    norms = [x[n] for n in ("ln0_mix_g", "ln0_mix_b", "ln0_ffn_g", "ln0_ffn_b", "ln1_mix_g", "ln1_mix_b", "ln1_ffn_g", "ln1_ffn_b",
                            "ret_norm_g", "mlstm_norm_g", "gdn_norm_g", "gla_norm_g", "gla_b_alpha")]
    arrays["vec_rows"] = np.concatenate([v.reshape(-1, 128) for v in norms])
    arrays["conv_rows"] = np.ascontiguousarray(x["gdn_conv_w"]).reshape(NCONV, 128)
    arrays["gate_cols"] = np.stack([x["mlstm_gate_bias"][0:4], x["mlstm_gate_bias"][4:8], x["gdn_a_log"], x["gdn_dt_bias"]], 1)
    arrays["m_rows"] = np.ascontiguousarray(x["state_mlstm_m"].T)
    arrays |= _constants(np)
    nc = bacc.Bacc("TRN2", target_bir_lowering=False, num_devices=1)
    I = {n: nc.dram_tensor("in_" + n, a.shape, mybir.dt.float32, kind="ExternalInput").ap() for n, a in arrays.items()}
    O = {n: nc.dram_tensor("out_" + n, shape, mybir.dt.float32, kind="ExternalOutput").ap() for n, shape in _OUTS.items()}
    build(nc, I, O)
    r = run_bass_kernel_spmd(nc, [{"in_" + n: a for n, a in arrays.items()}], core_ids=[0]).results[0]
    o = {n: r["out_" + n] for n in _OUTS}
    y, m = o["y_all"], o["m_rows"]
    return (y[NMETA:TP].reshape(1, SEQ, D), y[TP:].reshape(NB, NS, D),
            o["prompt_ret"], o["prompt_c"], o["prompt_n"], np.ascontiguousarray(m[:, 8:9].T), o["prompt_gdn"], o["prompt_conv"], o["prompt_gla"],
            o["sample_ret"], o["sample_c"], o["sample_n"], np.ascontiguousarray(m[:, 0:8].T), o["sample_gdn"], o["sample_conv"], o["sample_gla"])
```

```python
import math
from contextlib import ExitStack

import concourse.bass as bass
from concourse import mybir

D, KT = 1024, 8
NMETA, SEQ, NB, NS = 16, 256, 8, 4
TP, TS = NMETA + SEQ, NB * NS
T = TP + TS
TILES = [(0, 128), (128, 128), (256, T - 256)]
R2 = T - 256
PR2 = TP - 256
H = 4
HT = H * T
FT = 11
NE = 8
FE = 2
UN = FT + KT
UC = UN - FT + 1
QKV = 1536
LN_EPS, EPS = 1e-5, 1e-6
ALPHA = 4 ** 0.25
ATT = 464
A1, A2 = TP, TP + (TP - 128)
SEGS = 1 + NB
NVEC, NCONV = 82, 48
CONVW = 3 + TP + NB * (3 + NS)
CC = dict(ident=(0, 128), meanD=(128, 128), meanE=(256, 128), ones=(384, 128))
C0 = dict(rot=(0, 128), cos=(128, 2 * T), sin=(128 + 2 * T, 2 * T), dec=(128 + 4 * T, 4 * ATT),
          mask=(128 + 4 * T + 4 * ATT, ATT), gq=(128 + 4 * T + 5 * ATT, 128),
          gk=(256 + 4 * T + 5 * ATT, 8), gk2=(264 + 4 * T + 5 * ATT, 36), blk=(300 + 4 * T + 5 * ATT, 9))
C1 = dict(incl=(0, T), strict=(T, T), same8=(2 * T, T), eye=(3 * T, T), gla=(4 * T, T), rst=(5 * T, T),
          seg9=(6 * T, SEGS * R2), blk=(6 * T + SEGS * R2, 9), tri=(6 * T + SEGS * R2 + 9, 64))
N0, N1 = 309 + 4 * T + 5 * ATT, 6 * T + SEGS * R2 + 73
C4 = dict(rst0=(0, T), rneg=(T, T), rstg=(2 * T, T))
N4 = 3 * T


def build(nc, I, O):
    SBUF0 = -(-nc.sbuf_base // 32) * 32
    F32 = mybir.dt.float32
    ALU, ACT, AX = mybir.AluOpType, mybir.ActivationFunctionType, mybir.AxisListType
    MUL, ADD, SUB, MAX, MIN = ALU.mult, ALU.add, ALU.subtract, ALU.max, ALU.min
    EXP, LN, COPY, IDN, SQR, SILU, SIGM = ACT.Exp, ACT.Ln, ACT.Copy, ACT.Identity, ACT.Square, ACT.Silu, ACT.Sigmoid
    V, S_, G, PEE = nc.vector, nc.scalar, nc.gpsimd, nc.tensor
    ctx = ExitStack()
    sems = {}

    SHARED = {
        "mean": [("r_", 1), ("m_", 1), ("l_", 1)], "cent": [("r_", 1), ("m_", 1), ("l_", 1)],
        "sq": [("r_", 1), ("m_", 1), ("g_", 1), ("l_", 1)], "var": [("r_", 1), ("m_", 1), ("g_", 1), ("l_", 1)],
        "rstd": [("r_", 1), ("m_", 1), ("g_", 1), ("l_", 1)], "out": [("r_", 1), ("m_", 1), ("g_", 1), ("l_", 1)],
        "state_pe": [("r_", 4), ("m_", 4), ("g_", 4), ("l_", 4)], "stu": [("r_", 4), ("m_", 4), ("g_", 4), ("l_", 4)],
        "vb": [("r_", 4), ("m_", 4), ("g_", 4), ("l_", 4)], "vd": [("r_", 1), ("m_", 1)], "pst": [("r_", 1), ("m_", 1)],
        "o": [("r_", 4), ("m_", 4), ("g_", 4), ("l_", 4)], "att": [("r_", 4), ("m_", 4), ("g_", 1), ("l_", 4)],
        "qk": [("r_", 4), ("m_", 4), ("g_", 4), ("l_", 4)], "qs": [("r_", 1), ("m_", 1)],
        "bc": [("m_", 4), ("g_", 1)], "colpe": [("m_", 1), ("g_", 1)], "col": [("m_", 1), ("g_", 1)],
        "abs": [("m_", 1), ("g_", 1), ("l_", 1)], "lse": [("m_", 1), ("g_", 1), ("l_", 1)], "rows": [("m_", 1), ("g_", 1)],
        "kt": [("r_", 3), ("g_", 3), ("l_", 1)], "vt": [("r_", 3), ("g_", 3), ("l_", 3)],
        "normmean": [("n0m_", 1), ("n0f_", 1), ("n1m_", 1), ("n1f_", 1)], "normcent": [("n0m_", 4), ("n0f_", 4), ("n1m_", 4), ("n1f_", 4)],
        "normsq": [("n0m_", 4), ("n0f_", 4), ("n1m_", 4), ("n1f_", 4)], "normvar": [("n0m_", 1), ("n0f_", 1), ("n1m_", 1), ("n1f_", 1)],
        "normrstd": [("n0m_", 1), ("n0f_", 1), ("n1m_", 1), ("n1f_", 1)], "normx": [("n0m_", 2), ("n0f_", 2), ("n1m_", 2), ("n1f_", 2)],
        "normz": [("n0m_", 1), ("n1m_", 1)], "normzn": [("n0m_", 2), ("n0f_", 2), ("n1m_", 2), ("n1f_", 2)],
        "w0": [("f0_", 96 * FE), ("f1_", 0)], "w1": [("f0_", 96 * FE), ("f1_", 0)],
        "d0": [("f0_", 32 * FE), ("f1_", 0)], "d1": [("f0_", 32 * FE), ("f1_", 0)],
        "hi": [("a_", 2 * 10), ("f0_", UN * FE), ("b_", 2 * 9), ("f1_", 0)],
        "lo": [("a_", 2 * 10), ("f0_", UN * FE + UC), ("b_", 2 * 9), ("f1_", 0)],
    }
    CHAINS = {
        "router_pe": [("x_log", 1), ("x_gt", 1), ("x_bc", 8)], "router_dve": [("x_lm", 1), ("x_gate", 1), ("x_gtev", 1)],
        "tok_act": [("r_vtok", 3), ("r_ktok", 3), ("m_tok", 6), ("g_tok_a", 3), ("l_tok", 6)],
        "oev_act": [("r_oev", 4), ("g_oev", 1), ("l_oev", 4)],
        "late_load": [("ld_halo", 16), ("ld_stG", 32), ("ld_router", 32)], "silu": [("f0_silu", FE * FT), ("f1_silu", 0)],
        "rope_pe": [("vec_pe", 1), ("rot", 1)], "rows_exp": [("m_exp", 1), ("g_eg", 1)],
    }
    WHERE = {}
    for kind, users in CHAINS.items():
        base = 0
        for name, count in users:
            WHERE[name] = (kind, base)
            base += count
    for kind, users in SHARED.items():
        base = 0
        for prefix, count in users:
            WHERE[prefix + kind.removeprefix("norm")] = (kind, base)
            base += count

    def s(name):
        kind = WHERE.get(name, (name, 0))[0]
        if kind not in sems:
            sems[kind] = ctx.enter_context(nc.semaphore(kind))
        return sems[kind]

    def at(name, n):
        return s(name), n + WHERE.get(name, (name, 0))[1]

    with ctx:
        F32R = mybir.dt.float32r
        words = [0]

        def sb(name, shape):
            n = 8 * -(-math.prod(shape[1:]) // 8)
            t = nc.alloc_sbuf_tensor_at(name, shape, F32, offset=SBUF0 + 4 * words[0])
            words[0] += n
            return t

        def split(name, at_, shape):
            return nc.alloc_sbuf_tensor_at(name, shape, F32R, offset=SBUF0 + 4 * at_)

        xT = sb("xT", [128, KT, T])
        wring = sb("wring", [128, 8192])
        cst = sb("cst", [128, max(N0, N1)])
        cc = sb("cc", [128, 512])
        vec = sb("vec", [128, NVEC + NCONV])
        zT_at = words[0]
        zT = sb("zT", [128, KT, T])
        d_at = words[0]
        dring = sb("dring", [128, 4 * FT * 128])
        st_at = words[0]
        stA = sb("stA", [128, 32, 128])
        stB = sb("stB", [128, 32, 128])
        mix_at = words[0]
        mix = sb("mix", [128, KT, T])
        p_at = words[0]
        proj = sb("proj", [128, 32 * T])
        a_at = words[0]
        arena = sb("arena", [128, 9600])
        xsplit = {n: [split(f"x_{n}_{part}", where[i], [128, KT, T]) for i, part in enumerate(("hi", "lo"))]
                  for n, where in {"in0": (zT_at, mix_at), "in1": (d_at, d_at + KT * T), "out": (p_at, p_at + KT * T)}.items()}
        hsplit = [split(f"hid_{part}", st_at + FT * T * i, [128, FT, T]) for i, part in enumerate(("hi", "lo"))]
        wc = split("w_parts", a_at, [128, 2, 2, 2048])
        we = split("w_early", p_at + 2 * KT * T, [128, 2, 2048])
        dc = split("d_parts", st_at + 2 * FT * T, [128, 2, FT, 128])
        PS = ctx.enter_context(nc.psum_tensor("PS", [128, 8, 512], F32))

        def const(table, name):
            a, n = table[name]
            return (cc if table is CC else cst)[:, a:a + n]

        ident, meanD, meanE, ones = (const(CC, n) for n in ("ident", "meanD", "meanE", "ones"))
        halves = [wring[:, 4096 * i:4096 * (i + 1)].rearrange("p (k n) -> p k n", k=KT) for i in range(2)]
        slots = [wring[:, 4096 * i:4096 * (i + 1)].rearrange("p (g k n) -> p g k n", g=2, k=KT) for i in range(2)]
        dslots = [dring[:, 2816 * i:2816 * (i + 1)].rearrange("p (k n) -> p k n", k=FT) for i in range(2)]

        def proj_parts(layer, i, part):
            if layer == 0 and i >= 16:
                v = we[:, part] if i % 2 == 0 else wc[:, i // 2 % 2, part]
            else:
                v = wc[:, i % 2, part]
            return v.rearrange("p (k n) -> p k n", k=KT)

        def gu_parts(j, part):
            return wc[:, j % 2, part].rearrange("p (g k n) -> p g k n", g=2, k=KT)

        def down_parts(d, part):
            if d % 2:
                return wc[:, 1, part, 0:FT * 128].rearrange("p (k n) -> p k n", k=FT)
            return dc[:, part]

        def raw_proj(g, q):
            return halves[g % 2][:, :, 256 * q:256 * q + 256]

        def raw_gu(j):
            return slots[j // 2 % 2][:, :, :, 128 * (j % 2):128 * (j % 2) + 128]

        def raw_down(d):
            return dslots[d // 2 % 2][:, :, 128 * (d % 2):128 * (d % 2) + 128]

        P = proj[:].rearrange("p (m t) -> p m t", t=T)

        VEC = {n: 8 * i for i, n in enumerate(["mix0_g", "mix0_b", "ffn0_g", "ffn0_b", "mix1_g", "mix1_b", "ffn1_g", "ffn1_b"])}
        VEC |= {"ret": 64, "mlstm": 68, "gdn": 72, "gla": 76, "balpha": 80}

        def carve(base, at, n, *shape):
            v = base[:, at:at + n]
            if len(shape) == 2:
                v = v.rearrange("p (a b) -> p a b", a=shape[0])
            if len(shape) == 3:
                v = v.rearrange("p (a b c) -> p a b c", a=shape[0], b=shape[1])
            return v

        ktok = carve(arena, 0, 1536, 3, 512)
        vtok = carve(arena, 1536, 1536, 3, 512)
        att = carve(arena, 3072, 1856, 4, ATT)
        vd = carve(arena, 4928, 1024, 2, 4, 128)
        pst = carve(arena, 8192, 512, 4, 128)
        qn = carve(arena, 8704, 128, 4, 32)
        ebc = carve(arena, 6464, 1376, 4, 344)
        qs = carve(arena, 7840, 128, 4, 32)
        mcol = carve(arena, 9008, 24)
        wl2 = carve(arena, 9032, 36, 4, 9)
        nT = carve(arena, 9072, 36)
        nrow = carve(arena, 9108, 128)
        gates0 = carve(arena, 9236, 2)
        m0 = carve(arena, 9238, 9)
        wsm = [carve(proj, 9120, KT * 36, KT, 36), carve(proj, 8960, KT * 80, KT, 80)]
        nload = carve(arena, 9440, 128)
        r4 = carve(dring, 0, N4)
        ROW = [dring[0:4, N4 + 344 * i:N4 + 344 * (i + 1)] for i in range(8)]
        vb = [carve(dring, 4480, 1152, SEGS, 128), carve(dring, 0, 1152, SEGS, 128)]
        xtok = proj[:, 0:3072].rearrange("p (a b) -> p a b", a=3)
        vrows = proj[:, 3072:3328]

        mixf, zf = mix[:].rearrange("p a b -> p (a b)"), zT[:].rearrange("p a b -> p (a b)")
        stBf = stB[:].rearrange("p a b -> p (a b)")
        cin = carve(mixf, 0, 4 * CONVW, 4, CONVW)
        cacc = carve(mixf, 4 * CONVW, 2 * CONVW, 2, CONVW)
        convT = carve(zf, 0, 288, 12, 24)
        halo = zf[0:24, 612:612 + QKV]
        lastT = carve(zf, 288, 324, 12, 27)
        lastrow = carve(dring, 3968, 1536)
        sqn = carve(arena, 4864, 2432, 8, T)
        decI = carve(arena, 0, HT, 4, T)
        attg = carve(arena, HT, HT, 4, T)
        kb = carve(arena, 2 * HT, HT, 4, T)
        qe = carve(arena, 3 * HT, HT, 4, T)
        ktg = carve(arena, 4864, 1536, 3, 512)
        ug = carve(arena, 6400, 1536, 3, 512)
        sg = carve(arena, 7936, 1536, 3, 4, 128)
        gcol = carve(arena, 9472, 48, 4, 3, 4)
        dbc = carve(arena, 9520, 44, 4, 11)
        SDT, SD = carve(zf, 0, HT, 4, T), carve(zf, HT, HT, 4, T)
        SRT, SO = carve(mixf, 0, HT, 4, T), carve(mixf, HT, HT, 4, T)
        SP_, SPT = carve(dring, 0, HT, 4, T), carve(dring, HT, HT, 4, T)
        rhsk = carve(dring, 2432, 1536, 3, 512)
        rhsv = carve(dring, 3968, 1536, 3, 512)
        ub = [carve(dring, 0, 1152, SEGS, 128), carve(dring, HT, 1152, SEGS, 128)]
        r4b = carve(stBf, 0, N4)
        GROW = [stBf[0:4, N4 + 315 * i:N4 + 315 * (i + 1)] for i in range(7)]
        wtm = carve(stBf, 2368, 4 * SEGS * R2, 4, SEGS, R2)
        lrT, walpha = P[0:16, 28, :], arena[0:16, 8704:8960]
        bc_, cb_, kx_, q1, k1, k2 = (carve(wring, 4096 + 608 * i, 608, 2, T) for i in range(6))
        e1, e2 = (carve(wring, 608 * i, 608, 2, T) for i in range(2))
        e3 = P[:, 29:31, :]
        q2 = carve(wring, 0, HT, 4, T)
        ktl = carve(arena, 6080, 768, 3, 256)
        vtl = carve(arena, 6848, 1536, 3, 512)
        attl = carve(arena, 8384, HT, 4, T)
        sc = carve(dring, 0, 1280, 5, 2, 128)
        lb = [carve(dring, 1280, 1152, SEGS, 128), carve(dring, 2432, 1152, SEGS, 128)]
        lvp = carve(dring, 3584, 512, 4, 128)
        stG = stB[:, 0:16, :]

        SOLVE = [("split", None, SDT, None, None),
                 ("copy", SP_, SDT, SD, 0),
                 ("copy", SPT, SD, SDT, 0),
                 ("add", SRT, SP_, SRT, 1),
                 ("copy", SD, SPT, SP_, 2),
                 ("add", SRT, SD, SRT, 4),
                 ("copy", SP_, SRT, SO, 5),
                 ("copyz", SPT, SO, SRT, 5),
                 ("transpose", SDT, SRT, None, 5),
                 ("copy", SD, SPT, SP_, 7),
                 ("copy", SRT, SP_, SPT, 8),
                 ("add", SO, SD, SO, 9),
                 ("copy", SP_, SRT, SD, 10),
                 ("copy", SPT, SD, SRT, 10),
                 ("add", SO, SP_, SO, 12),
                 ("copy", SD, SPT, SP_, 13),
                 ("add", SO, SD, SO, 15),
                 ("copy", SRT, SDT, SO, 16)]
        ORDER = [(k, i) for k in range(len(SOLVE)) for i in range(3) if i < 2 or k <= 8 or k == 17]
        AT = {ki: n for n, ki in enumerate(ORDER)}

        def solve_after(k, i):
            w = SOLVE[k][4]
            if i == 2 and k == 17:
                w = 8
            return 0 if w is None else AT[(w, i)] + 1

        gact = P[:, 16:18, :]
        gu_raw = P[:, 18, :]
        hraw = mix[:, 6:8, :]
        gbc = P[:, 20:28, :]
        rt = proj[:, 28 * T:32 * T]
        lt, lm, gate = (carve(rt, 24 * i, 24, 3, 8) for i in range(3))
        gcmp, geq = (carve(rt, 72 + 192 * i, 192, 3, 64) for i in range(2))
        st3 = carve(rt, 456, 24, 3, 8)
        gT = rt[:, 480:480 + T]
        brt = rt[:, 800:808]
        wrt = carve(rt, 832, 64, KT, 8)

        NARROW = 6
        RPAIRS = GPAIRS = [(4, 7), (5, 7), (0, 1), (2, 3)]
        MPAIRS = [(4, 7), (4, 7), (0, 1), (2, 3)]
        LCHUNK = [(1, 2, 3), (4, 5, 6)]
        LPAIRS = [(4, 5), (6, 7), (0, 1), (2, 3)]
        LNB = {"n0m_": 0, "n0f_": 0, "n1m_": 4, "n1f_": 0}

        def bank4(a):
            return PS[:, a:a + 4, 0:T]

        def smp(ap):
            return ap[:, TP:T].rearrange("p (b t) -> p b t", b=NB)

        def cins(m):
            return cin[:, m % 4, 3 + TP:CONVW].rearrange("p (b t) -> p b t", b=NB)

        def cconv(m):
            return cacc[:, m % 2, 3 + TP:CONVW].rearrange("p (b t) -> p b t", b=NB)[:, :, 0:NS]

        in0 = [512 * g for g in range(8)]
        in1 = [0, 512, 1024, 1536, 2056, 2568, 3080]
        groups = [(I["w_in0"], c) for c in in0] + [(I["w_out0"], c) for c in (0, 512)] \
            + [(I["w_in1"], c) for c in in1] + [(I["w_out1"], c) for c in (0, 512)]
        OUT0, IN1, OUT1, GEND = 8, 10, 17, 19

        def ffn_weights(layer):
            if layer == 0:
                g, u = (I[n].rearrange("(k p) (e f) -> e p k f", p=128, e=FE) for n in ("ffn0_w_gate", "ffn0_w_up"))
                d = I["ffn0_w_down"].rearrange("(e j p) d -> e p j d", p=128, e=FE)
            else:
                g, u = (I[n].rearrange("e (k p) f -> e p k f", p=128) for n in ("moe_w_gate", "moe_w_up"))
                d = I["moe_w_down"].rearrange("e (j p) d -> e p j d", p=128)
            return g, u, d

        def over_experts(engine, E, body):
            first = 1 if E == NE else 0
            if first:
                body(0, False, True)
            with engine.Fori(first, E - 1) as e:
                body(e, False, False)
            body(E - 1, True, False)

        block = ctx.enter_context(nc.Block())

        @block.sync
        def _(sp):
            def group(g):
                w, c = groups[g]
                if 2 <= g < IN1:
                    sp.wait_ge(*at("a_lo", 2 * (g - 1)))
                elif g >= IN1 + 2:
                    sp.wait_ge(*at("b_lo", 2 * (g - 1 - IN1)))
                if g == OUT1:
                    sp.wait_ge(*at("l_qk", 4))
                if g == OUT1 + 1:
                    sp.wait_ge(*at("l_o", 4))
                sp.dma_start(halves[g % 2], w[:, c:c + 512].rearrange("(k p) n -> p k n", p=128)).then_inc(s(f"ring{g % 2}"), 16)

            for i, (a, n) in enumerate(TILES):
                sp.dma_start(xtok[0:n, i, :], I["x_all"][a:a + n]).then_inc(s("ld_x"), 16)
            group(0)
            group(1)
            for g in range(2, OUT0 + 2):
                group(g)

            def ffn(layer, ring_free, dring_free):
                wg, wu, wd = ffn_weights(layer)
                p, E = f"f{layer}_", (FE, NE)[layer]

                def hidden_pair(e, q):
                    n = min(256, FT * 128 - 256 * q)
                    for gu, w in enumerate((wg, wu)):
                        sp.dma_start(slots[q % 2][:, gu, :, 0:n], w[e, :, :, 256 * q:256 * q + n]).then_inc(s(p + f"w{q % 2}"), 16)

                def down_pair(e, q):
                    sp.dma_start(dslots[q % 2], wd[e, :, :, 256 * q:256 * q + 256]).then_inc(s(p + f"d{q % 2}"), 16)

                def body(e, is_last, with_router):
                    sp.wait_ge(*at(p + "lo", e * UN + (UC - 2)))
                    down_pair(e, 0)
                    sp.wait_ge(*at(p + "lo", e * UN + UC))
                    down_pair(e, 1)
                    for q in range(2, 6):
                        sp.wait_ge(*at(p + "lo", e * UN + (UC + 2 * q - 2)))
                        hidden_pair(e, q)
                    if not is_last:
                        for q in range(2):
                            sp.wait_ge(*at(p + "lo", e * UN + (UC + 10 + q)))
                            hidden_pair(e + 1, q)
                    for q in range(2, 4):
                        sp.wait_ge(*at(p + "lo", e * UN + (UC + FT + 2 * q - 2)))
                        down_pair(e, q)

                for q in range(2):
                    sp.wait_ge(*ring_free[q])
                    hidden_pair(0, q)
                for signal in dring_free:
                    sp.wait_ge(*signal)
                over_experts(sp, E, body)

            ffn(0, [at("a_lo", 18), at("a_lo", 20)], [at("m_out", 1), at("m_state_pe", 4)])
            for g in range(IN1, GEND):
                if g < IN1 + 2:
                    sp.wait_ge(*at("f0_lo", UC + UN * (FE - 1) + FT - 1 + g - IN1))
                group(g)
            ffn(1, [at("b_lo", 18), at("b_lo", 18)], [at("l_out", 1), at("st_all", 16 * 19)])
            sp.wait_ge(*at("y_ev", 6))
            ytok = proj[:, 0:3072].rearrange("p (a b) -> p a b", a=3)
            for i, (a, n) in enumerate(TILES):
                sp.dma_start(O["y_all"][a:a + n], ytok[0:n, i, :]).then_inc(s("st_y"), 16)
            sp.wait_ge(*at("st_y", 48))

        @block.tensor
        def _(pe):
            mm = PEE.matmul

            def tr(out, in_, n):
                return PEE.transpose(out, in_, ident[0:n, 0:n])

            def row(h, n=4):
                return ident[0:n, h:h + 1].to_broadcast([n, 128])

            pe.wait_ge(*at("ld_x", 48))
            pe.wait_ge(*at("ld_cc", 16))
            for k in range(KT):
                for i, (a, n) in enumerate(TILES):
                    last = tr(PS[:, k, a:a + n], xtok[0:n, i, 128 * k:128 * k + 128], n)
                last.then_inc(s("xt_pe"), 1)
            pe.wait_ge(*at("xhi", 2))
            pe.wait_ge(*at("ld_v", 48))
            tr(PS[:, 0, 0:NVEC], vrows[0:NVEC, 0:128], NVEC)
            tr(PS[:, 0, 128:128 + NCONV], vrows[0:NCONV, 128:256], NCONV)
            tr(PS[:, 0, 256:288], nload[0:32, :], 32).then_inc(s("vec_pe"), 1)

            def narrow(layer):
                pe.wait_ge(*at(("ld_wsm", "ld_l1")[layer], (32, 96)[layer]))
                n = (36, 80)[layer]
                for k in range(KT):
                    if layer == 1 and k % 4 == 0:
                        pe.wait_ge(*at("n0f_x", k // 4 + 1))
                    last = mm(PS[0:n, NARROW, 0:T], wsm[layer][:, k, :], xT[:, k, :], start=k == 0, stop=k == KT - 1)
                last.then_inc(s("small_pe"), 1)


            def mm3(out, w, x, start, stop):
                mm(out, w[0], x[0], start=start, stop=False)
                mm(out, w[0], x[1], start=False, stop=False)
                return mm(out, w[1], x[0], start=False, stop=stop)

            def tile_mm(half, t, x, unit=(1, None)):
                for k in range(KT):
                    w = [proj_parts(unit[0], t // 2 if unit[1] is None else unit[1], part)[:, k, 128 * (t % 2):128 * (t % 2) + 128] for part in range(2)]
                    last = mm3(PS[:, 4 * half + t, 0:T], w, [x[0][:, k, :], x[1][:, k, :]], k == 0, k == KT - 1)
                last.then_inc(s("proj_pe"), 1)

            def units(g):
                return ("a_lo", 2 * g) if g < IN1 else ("b_lo", 2 * (g - IN1))

            def group(g, x, banks_free=lambda t: [], between=lambda t: None):
                name, before = units(g)
                for t in range(4):
                    if t % 2 == 0:
                        pe.wait_ge(*at(name, before + t // 2 + 1))
                    for signal in banks_free(t):
                        pe.wait_ge(*signal)
                    tile_mm(g % 2, t, x, (int(g >= IN1), before + t // 2))
                    between(t)

            def group_pairs(lo, hi, x):
                name, before = units(2 * lo)
                with pe.Fori(lo, hi) as p:
                    for half in range(2):
                        for t in range(4):
                            if t % 2 == 0:
                                pe.wait_ge(*at(name, p * 4 + (before - 4 * lo + 2 * half + t // 2 + 1)))
                            pe.wait_ge(*at("proj_ev", p * 8 + (4 * half + t - 7)))
                            tile_mm(half, t, x)

            pe.wait_ge(*at("vec_ev", 1))
            pe.wait_ge(*at("xlo", 2))
            group(0, xsplit["in0"])
            narrow(0)
            group(1, xsplit["in0"], lambda t: [at("small_ev", 1)] if 4 + t == NARROW else [])
            group_pairs(1, 2, xsplit["in0"])
            pe.wait_ge(*at("ld_c0", 16))
            for m in range(8):
                pe.wait_ge(*at("proj_ev", 9 + m))
                last = mm(PS[:, m, 0:T], const(C0, "rot"), P[:, m, :], start=True, stop=True)
            last.then_inc(s("rot"), 1)
            pe.wait_ge(*at("rotm", 1))
            group_pairs(2, 4, xsplit["in0"])

            def state_mm(p, h, kt_, vdec, vblk, kcols, banks, pbank):
                for i in range(2):
                    mm(PS[:, pbank, 128 * h:128 * h + 128], kt_[:, i, kcols], vdec[:, i, h, :], start=i == 0, stop=False)
                mm(PS[:, pbank, 128 * h:128 * h + 128], kt_[0:R2, 2, kcols], vblk[0:R2, 0, :], start=False, stop=True)
                for j, b in enumerate(banks):
                    last = mm(PS[:, b, :], kt_[0:R2, 2, kcols], vblk[0:R2, 1 + 4 * j:5 + 4 * j, :].rearrange("p a b -> p (a b)"),
                              start=True, stop=True)
                last.then_inc(s(p + "state_pe"), 1)

            def out_mm(bank, lhs, h, final):
                mm(PS[:, bank, 0:TP], lhs[0], att[:, h, 0:A1], start=True, stop=False)
                mm(PS[:, bank, 128:TP], lhs[1], att[:, h, A1:A2], start=False, stop=False)
                mm(PS[:, bank, 256:TP], lhs[2], att[0:R2, h, A2:A2 + PR2], start=False, stop=False)
                mm(PS[:, bank, TP:T], lhs[2], att[0:R2, h, A2 + PR2:ATT], start=False, stop=False)
                if final is None:
                    return mm(PS[:, bank, TP:T], ones, qn[:, h, :], start=False, stop=True)
                for b in range(NB):
                    last = mm(PS[:, bank, TP + 4 * b:TP + 4 * b + 4], final(b), qs[:, h, 4 * b:4 * b + 4],
                              start=False, stop=b == NB - 1)
                return last

            def scores(bank, h, q0, k0):
                mm(PS[:, bank, 0:A1], P[:, k0 + h, 0:128], P[:, q0 + h, 0:TP], start=True, stop=True)
                mm(PS[:, bank, A1:A2], P[:, k0 + h, 128:256], P[:, q0 + h, 128:TP], start=True, stop=True)
                return mm(PS[0:R2, bank, A2:ATT], P[:, k0 + h, 256:T], P[:, q0 + h, 256:T], start=True, stop=True)

            def tokens(bank, i, m0_, n=4):
                a, r = TILES[i]
                for h in range(n):
                    last = tr(PS[0:r, bank, 128 * h:128 * h + 128], P[:, m0_ + h, a:a + r], 128)
                return last

            def head_means(p, heads=range(H)):
                for h in heads:
                    pe.wait_ge(*at(p + "oev", h + 1))
                    last = mm(PS[:, h, 0:T], meanE, zT[:, h, :], start=True, stop=True)
                if heads[-1] == H - 1:
                    last.then_inc(s(p + "mean"), 1)

            def head_vars(p):
                pe.wait_ge(*at(p + "sq", 1))
                for h in range(H):
                    last = mm(PS[:, h, 0:T], meanE, zT[:, 4 + h, :], start=True, stop=True)
                last.then_inc(s(p + "var"), 1)

            pe.wait_ge(*at("proj_ev", 32))
            for i in range(3):
                tokens(3 + i, i, 8).then_inc(s("r_vt"), 1)
            pe.wait_ge(*at("rope", 1))
            for i in range(3):
                tokens(i, i, 4).then_inc(s("r_kt"), 1)
            for h, b in enumerate([6, 7, 3, 4]):
                if h == 2:
                    pe.wait_ge(*at("r_vtok", 3))
                scores(b, h, 0, 4).then_inc(s("r_qk"), 1)
            pe.wait_ge(*at("r_ktok", 3))
            pe.wait_ge(*at("r_qs", 1))
            pe.wait_ge(*at("ld_stA", 16))
            for h in range(H):
                pe.wait_ge(*at("r_att", h + 1))
                v = [vtok[:, 0, 128 * h:128 * h + 128], vtok[:, 1, 128 * h:128 * h + 128], vtok[0:R2, 2, 128 * h:128 * h + 128]]
                out_mm(h, v, h, lambda b_: stA[:, 4 * b_ + h, :]).then_inc(s("r_o"), 1)
            head_means("r_")
            for h in range(H):
                if h == 0:
                    pe.wait_ge(*at("r_vd", 1))
                if h == 1:
                    head_vars("r_")
                    pe.wait_ge(*at("r_stu", 1))
                if h == 2:
                    pe.wait_ge(*at("r_rstd", 1))
                pe.wait_ge(*at("r_vb", h + 1))
                state_mm("r_", h, ktok, vd, vb[h % 2], slice(128 * h, 128 * h + 128), RPAIRS[h], 6)

            pe.wait_ge(*at("r_stu", 2))
            pe.wait_ge(*at("m_rows", 1))
            pe.wait_ge(*at("m_exp", 1))
            for i, (a, n) in enumerate(TILES):
                tr(PS[0:n, 7, 4 * i:4 * i + 4], ROW[3][:, a:a + n], 4)
                last = tr(PS[0:n, 7, 12 + 4 * i:16 + 4 * i], ROW[5][:, a:a + n], 4)
            last.then_inc(s("m_colpe"), 1)
            pe.wait_ge(*at("r_stu", 4))
            for h in range(H):
                if h == 2:
                    pe.wait_ge(*at("r_pst", 1))
                mm(PS[:, h, 0:T], row(h), ROW[4][:, 0:T], start=True, stop=True)
                if h == 3:
                    pe.wait_ge(*at("m_col", 1))
                mm(PS[:, 4 + h, 0:344], row(h), ROW[6], start=True, stop=True).then_inc(s("m_bc"), 1)
            for h in range(H):
                pe.wait_ge(*at("m_ex", h + 1))
                scores(h, h, 16, 20).then_inc(s("m_qk"), 1)
            pe.wait_ge(*at("m_ebc", 1))
            for n_, (b, i, m_) in enumerate([(4, 0, 20), (5, 1, 20), (6, 2, 20), (7, 0, 24), (4, 1, 24), (5, 2, 24)]):
                if n_ >= 4:
                    pe.wait_ge(*at("m_tok", n_ - 3))
                tokens(b, i, m_).then_inc(s("m_tpe"), 1)
            pe.wait_ge(*at("m_tok", 6))
            pe.wait_ge(*at("m_qs", 1))
            pe.wait_ge(*at("ld_stB", 16))
            for h in range(H):
                pe.wait_ge(*at("m_att", h + 1))
                out_mm(4 + h, [ones, ones, ones[0:R2, :]], h, None)
                v = [vtok[:, 0, 128 * h:128 * h + 128], vtok[:, 1, 128 * h:128 * h + 128], vtok[0:R2, 2, 128 * h:128 * h + 128]]
                out_mm(h, v, h, lambda b_: stB[:, 4 * b_ + h, :]).then_inc(s("m_o"), 1)
            head_means("m_", range(3))
            pe.wait_ge(*at("m_vd", 1))
            for h in range(H):
                kc = slice(128 * h, 128 * h + 128)
                mm(PS[:, 5, 9 * h:9 * h + 9], ktok[0:R2, 2, kc], wl2[0:R2, h, :], start=True, stop=False)
                for i in range(2):
                    mm(PS[:, 5, 9 * h:9 * h + 1], ktok[:, i, kc], mcol[:, 12 + 4 * i + h:13 + 4 * i + h], start=False, stop=i == 1)
            head_means("m_", range(3, 4))
            for h in range(H):
                if h == 1:
                    head_vars("m_")
                if h == 2:
                    pe.wait_ge(*at("m_rstd", 1))
                if h == 1:
                    pe.wait_ge(*at("m_stu", 1))
                pe.wait_ge(*at("m_vb", h + 1))
                kc = slice(128 * h, 128 * h + 128)
                state_mm("m_", h, ktok, vd, vb[h % 2], kc, MPAIRS[h], 6)

            def ln_sum(p, ks, ready, count):
                for k in ks:
                    pe.wait_ge(*at(ready, count - KT + k + 1))
                    last = mm(PS[:, LNB[p], 0:T], meanD, zT[:, k, :], start=k == 0, stop=k == KT - 1)
                if KT - 1 in ks:
                    last.then_inc(s(p + "mean"), 1)

            def ln_var(p):
                for k in range(KT):
                    if k % 2 == 0:
                        pe.wait_ge(*at(p + "sq", k // 2 + 1))
                    last = mm(PS[:, LNB[p] + 1, 0:T], meanD, mix[:, k, :], start=k == 0, stop=k == KT - 1)
                last.then_inc(s(p + "var"), 1)

            def ffn(layer):
                p, E = f"f{layer}_", (FE, NE)[layer]
                x = xsplit["out"]
                pe.sem_inc(s(p + "hid_pe"), 1)
                pe.sem_inc(s(p + "down_pe"), 1)

                def body(e, is_last, with_router):
                    for j in range(FT):
                        pe.wait_ge(*at(p + "lo", e * UN + (UC + j + 1)))
                        pe.wait_ge(*at(p + "hid_ev", e * FT + max(j, 1)))
                        for gu in range(2):
                            for k in range(KT):
                                if (j, gu, k) == (0, 0, 4):
                                    pe.wait_ge(*at("xlo", 6 + 6 * layer))
                                w = [gu_parts(j, part)[:, gu, k, :] for part in range(2)]
                                last = mm3(PS[:, 2 * (j % 2) + gu, 0:T], w, [x[0][:, k, :], x[1][:, k, :]], k == 0, k == KT - 1)
                        last.then_inc(s(p + "hid_pe"), 1)
                        if with_router and j < 2:
                            spread_gates(j)
                    if with_router:
                        pe.wait_ge(*at("x_bcev", 2))
                    for d in range(KT):
                        pe.wait_ge(*at(p + "lo", e * UN + (UC + FT + d + 1)))
                        pe.wait_ge(*at(p + "down_ev", e * KT + d + 1))
                        for j in range(FT):
                            if d == 0 and j >= FT - 2:
                                pe.wait_ge(*at(p + "hid_ev", e * FT + j + 2))
                            w = [down_parts(d, part)[:, j, :] for part in range(2)]
                            last = mm3(PS[:, 4 + d % 4, 0:T], w, [hsplit[0][:, j, :], hsplit[1][:, j, :]], j == 0, j == FT - 1)
                        last.then_inc(s(p + "down_pe"), 1)
                        if is_last and d >= 2:
                            ln_sum(f"n{layer}f_", [d - 2], p + "down_ev", 4 + E * KT)

                def spread_gates(part):
                    if part == 0:
                        pe.wait_ge(*at("x_gate", 1))
                        for i, (a, n) in enumerate(TILES):
                            last = tr(PS[0:8, 7, a:a + n], gate[0:n, i, :], n)
                        last.then_inc(s("x_gt"), 1)
                        pe.wait_ge(*at("x_gtev", 1))
                    else:
                        pe.wait_ge(*at("x_bcev", 1))
                    for e in range(4 * part, 4 * part + 4):
                        mm(PS[:, 4 + e % 4, 0:T], row(e, 8), gT[0:8, :], start=True, stop=True).then_inc(s("x_bc"), 1)

                over_experts(pe, E, body)
                ln_sum(f"n{layer}f_", [6, 7], p + "down_ev", 4 + E * KT)
                ln_var(f"n{layer}f_")

            pe.wait_ge(*at("xlo", 4))
            group(8, xsplit["out"], lambda t: [at("m_stu", 3 + t // 2)])
            pe.wait_ge(*at("m_nst", 1))
            tr(PS[0:36, 5, 0:128], nT[:, 0:36], 128).then_inc(s("m_npe"), 1)
            def mean_between(p, count):
                return lambda t: ln_sum(p, {1: range(4), 3: range(4, 6)}.get(t, ()), "proj_ev", count)

            group(9, xsplit["out"], lambda t: [[], [at("m_nrow", 1)], [at("m_pst", 1)], []][t], mean_between("n0m_", 40))
            ln_sum("n0m_", [6, 7], "proj_ev", 40)
            ln_var("n0m_")
            pe.wait_ge(*at("xlo", 5))
            ffn(0)

            narrow(1)
            pe.wait_ge(*at("xlo", 8))
            group(10, xsplit["in1"])
            pe.wait_ge(*at("ld_halo", 16))
            for m in range(12):
                last = tr(PS[:, 4, 24 * m:24 * m + 24], halo[:, 128 * m:128 * m + 128], 24)
            last.then_inc(s("halo_pe"), 1)
            pe.wait_ge(*at("cin0", 1))
            pe.wait_ge(*at("small_ev", 2))
            group(11, xsplit["in1"])
            group_pairs(6, 8, xsplit["in1"])
            group(16, xsplit["in1"], lambda t: [at("proj_ev", 4 * 14 + t + 1)])

            pe.wait_ge(*at("proj_ev", 4 * OUT1))
            pe.wait_ge(*at("g_rows", 1))
            for r in range(4):
                for i, (a, n) in enumerate(TILES):
                    last = tr(PS[0:n, 0, 12 * r + 4 * i:12 * r + 4 * i + 4], [GROW[0], GROW[3], GROW[4], GROW[5]][r][:, a:a + n], 4)
            last.then_inc(s("g_colpe"), 1)
            pe.wait_ge(*at("g_col", 1))
            for h in range(H):
                mm(PS[:, h, 0:315], row(h), GROW[2], start=True, stop=True)
                last = mm(PS[:, 4 + h, 0:T], row(h), GROW[0][:, 0:T], start=True, stop=True)
            last.then_inc(s("g_bc"), 1)
            pe.wait_ge(*at("g_sqn", 1))
            pe.wait_ge(*at("g_bcev", 1))
            for m in range(8):
                last = mm(PS[:, m, 0:T], ones, sqn[:, m, :], start=True, stop=True)
            last.then_inc(s("g_l2pe"), 1)
            pe.wait_ge(*at("g_l2a", 1))
            pe.wait_ge(*at("last", 12))
            for m in range(12):
                last = tr(PS[0:27, 5 + m // 4, 128 * (m % 4):128 * (m % 4) + 128], lastT[:, m, :], 128)
            last.then_inc(s("last_pe"), 1)
            pe.wait_ge(*at("g_kb", 1))
            for h in range(H):
                for a, n in TILES:
                    last = mm(PS[0:n, h, a:a + n], P[:, 4 + h, a:a + n], kb[:, h, a:a + n], start=True, stop=True)
                last.then_inc(s("g_aa"), 1)
            pe.wait_ge(*at("g_kb", 2))
            pe.wait_ge(*at("last_ev", 1))
            for h in range(H):
                for a, n in TILES:
                    last = mm(PS[0:n, 4 + h, a:a + n], P[:, 4 + h, a:a + n], P[:, h, a:a + n], start=True, stop=True)
                last.then_inc(s("g_qk"), 1)
            pe.wait_ge(*at("g_at", 1))
            for i in range(3):
                tokens(i, i, 4).then_inc(s("g_kt"), 1)
            pe.wait_ge(*at("g_att", 1))
            for i in range(3):
                tokens(4 + i, i, 8).then_inc(s("g_vt"), 1)
            pe.wait_ge(*at("g_tok_a", 3))
            pe.wait_ge(*at("g_tok_d", 6))

            for n_, (k, i) in enumerate(ORDER):
                what, out, lhs, rhs, _ = SOLVE[k]
                a, n = TILES[i]
                if solve_after(k, i):
                    pe.wait_ge(*at("sv_ev", solve_after(k, i)))
                if n_ >= 8:
                    pe.wait_ge(*at("sv_ev", n_ - 7))
                for h in range(H):
                    o = PS[0:n, n_ % 8, n * h:n * h + n]
                    if what in ("split", "transpose"):
                        last = tr(o, lhs[0:n, h, a:a + n], n)
                    else:
                        last = mm(o, lhs[0:n, h, a:a + n], rhs[0:n, h, a:a + n], start=True, stop=True)
                last.then_inc(s("sv_pe"), 1)
            pe.wait_ge(*at("sv_ev", len(ORDER)))
            for p in range(2):
                last = mm(PS[:, 6 + p, 0:T], walpha[:, 128 * p:128 * p + 128], lrT, start=True, stop=True)
            last.then_inc(s("l_alpha"), 1)

            for i, (a, n) in enumerate(TILES):
                for h in range(H):
                    last = mm(PS[:, i, n * h:n * h + n], rhsk[0:n, i, 128 * h:128 * h + 128], SRT[0:n, h, a:a + n], start=True, stop=True)
                last.then_inc(s("g_w"), 1)
            for i, (a, n) in enumerate(TILES):
                if i == 2:
                    pe.wait_ge(*at("g_wtm", 1))
                if i > 0:
                    pe.wait_ge(*at("g_s", i))
                    pe.wait_ge(*at("g_wev", 3))
                for h in range(H):
                    o = PS[0:n, 3, 128 * h:128 * h + 128]
                    last = mm(o, SRT[0:n, h, a:a + n], rhsv[0:n, i, 128 * h:128 * h + 128], start=True, stop=i == 0)
                    if i == 1:
                        last = mm(o, kb[:, h, a:a + n], sg[:, 0, h, :], start=False, stop=True)
                    if i == 2:
                        mm(o, wtm[:, h, 0, :], sg[:, 1, h, :], start=False, stop=False)
                        for b in range(NB):
                            last = mm(o, wtm[:, h, 1 + b, :], stA[:, 4 * b + h, :], start=False, stop=b == NB - 1)
                last.then_inc(s("g_upe"), 1)
                pe.wait_ge(*at("g_ua", i + 1))
                pe.wait_ge(*at("g_ue", i + 1))
                if i < 2:
                    for h in range(H):
                        last = mm(PS[:, 5, 128 * h:128 * h + 128], ktg[:, i, 128 * h:128 * h + 128], rhsk[:, i, 128 * h:128 * h + 128],
                                  start=True, stop=True)
                    last.then_inc(s("g_spe"), 1)
            pe.wait_ge(*at("g_wev", 3))
            for b, h in enumerate(range(H)):
                for i, (a, n) in enumerate(TILES):
                    mm(PS[:, b, a:a + n], ug[0:n, i, 128 * h:128 * h + 128], attg[0:n, h, a:a + n], start=i == 0, stop=False)
                    if i == 1:
                        mm(PS[:, b, a:a + n], sg[:, 0, h, :], qe[:, h, a:a + n], start=False, stop=False)
                mm(PS[:, b, 256:TP], sg[:, 1, h, :], qe[:, h, 256:TP], start=False, stop=False)
                for b_ in range(NB):
                    last = mm(PS[:, b, TP + 4 * b_:TP + 4 * b_ + 4], stA[:, 4 * b_ + h, :], qe[:, h, TP + 4 * b_:TP + 4 * b_ + 4],
                              start=False, stop=b_ == NB - 1)
                last.then_inc(s("g_o"), 1)
            for h in range(H):
                if h == 1:
                    head_vars("g_")
                    pe.wait_ge(*at("g_stu", 1))
                if h == 2:
                    pe.wait_ge(*at("g_rstd", 1))
                pe.wait_ge(*at("g_vb", h + 1))
                kc = slice(128 * h, 128 * h + 128)
                mm(PS[:, 6, kc], ktg[0:R2, 2, kc], ub[h % 2][0:R2, 0, :], start=True, stop=True)
                for j, b in enumerate(GPAIRS[h]):
                    last = mm(PS[:, b, :], ktg[0:R2, 2, kc], ub[h % 2][0:R2, 1 + 4 * j:5 + 4 * j, :].rearrange("p a b -> p (a b)"),
                              start=True, stop=True)
                last.then_inc(s("g_state_pe"), 1)

            pe.wait_ge(*at("g_stu", 2))
            for i, b in enumerate((4, 5, 7)):
                tokens(b, i, 20).then_inc(s("l_vt"), 1)
            pe.wait_ge(*at("g_stu", 4))
            pe.wait_ge(*at("l_tok", 1))
            pe.wait_ge(*at("l_dqk", 1))
            for i, (a, n) in enumerate(TILES):
                for p in range(2):
                    last = tr(PS[0:n, 3 + i // 2, 256 * (i % 2) + 128 * p:256 * (i % 2) + 128 * p + 128], k2[:, p, a:a + n], 128)
            last.then_inc(s("l_kt"), 1)
            pe.wait_ge(*at("l_tok", 6))
            for h, b in enumerate([5, 6, 7, 0]):
                if h == 1:
                    pe.wait_ge(*at("g_pst", 1))
                r = slice(64 * (h % 2), 64 * (h % 2) + 64)
                for a, n in TILES:
                    last = mm(PS[0:n, b, a:a + n], k1[r, h // 2, a:a + n], q1[r, h // 2, a:a + n], start=True, stop=True)
                last.then_inc(s("l_qk"), 1)
            pe.wait_ge(*at("l_vb0", 1))
            for p in range(2):
                if p == 1:
                    pe.wait_ge(*at("l_att", 2))
                for c in range(4):
                    r = slice(64 * (c % 2), 64 * (c % 2) + 64)
                    mm(PS[:, LCHUNK[p][c % 2], 256 * (c // 2):256 * (c // 2) + 256], ktl[r, c // 2, 128 * p:128 * p + 128],
                       vtl[r, c // 2, 256 * p:256 * p + 256], start=True, stop=True)
                for q in range(2):
                    last = mm(PS[:, LCHUNK[p][2], 128 * q:128 * q + 128], ktl[0:R2, 2, 128 * p:128 * p + 128],
                              lvp[0:R2, 2 * p + q, :], start=True, stop=True)
                last.then_inc(s("l_upe"), 1)
            pe.wait_ge(*at("ld_stG", 32))
            pe.wait_ge(*at("l_att", 4))
            for h in range(H):
                if h % 2 == 0:
                    pe.wait_ge(*at("l_sc", h // 2 + 1))
                r, p = slice(64 * (h % 2), 64 * (h % 2) + 64), h // 2
                for i in (2, 0, 1):
                    a, n = TILES[i]
                    mm(PS[:, h, a:a + n], vtl[0:n, i, 128 * h:128 * h + 128], attl[0:n, h, a:a + n], start=i == 2, stop=False)
                for c in range(1, 5):
                    n = 64 if c < 4 else PR2
                    mm(PS[:, h, 64 * c:64 * c + n], sc[:, c - 1, p, :], q2[:, h, 64 * c:64 * c + n], start=False, stop=False)
                for b in range(NB):
                    last = mm(PS[:, h, TP + 4 * b:TP + 4 * b + 4], stG[:, 2 * b + p, :], q2[:, h, TP + 4 * b:TP + 4 * b + 4],
                              start=False, stop=b == NB - 1)
                last.then_inc(s("l_o"), 1)
            head_means("l_")
            for h in range(H):
                if h == 1:
                    head_vars("l_")
                pe.wait_ge(*at("l_vb", h + 1))
                if h == 2:
                    pe.wait_ge(*at("l_rstd", 1))
                for j, b in enumerate(LPAIRS[h]):
                    last = mm(PS[:, b, :], ktl[0:R2, 2, 128 * (h // 2):128 * (h // 2) + 128],
                              lb[h % 2][0:R2, 1 + 4 * j:5 + 4 * j, :].rearrange("p a b -> p (a b)"), start=True, stop=True)
                last.then_inc(s("l_state_pe"), 1)

            pe.wait_ge(*at("xlo", 10))
            group(17, xsplit["out"], lambda t: [at("l_stu", 2)])
            group(18, xsplit["out"], lambda t: [at("l_stu", 4)], between=mean_between("n1m_", 4 * GEND))
            ln_sum("n1m_", [6, 7], "proj_ev", 4 * GEND)
            ln_var("n1m_")

            pe.wait_ge(*at("ld_router", 32))
            for half in range(2):
                pe.wait_ge(*at("n1m_x", half + 1))
                for i, (a, n) in enumerate(TILES):
                    for k in range(4 * half, 4 * half + 4):
                        mm(PS[0:n, 5 + i, 0:8], xT[:, k, a:a + n], wrt[:, k, :], start=k == 0, stop=False)
                    if half == 1:
                        last = mm(PS[0:n, 5 + i, 0:8], ones[0:1, 0:n], brt[0:1, :], start=False, stop=True)
            last.then_inc(s("x_log"), 1)
            pe.wait_ge(*at("xlo", 11))
            ffn(1)
            for q in range(2):
                pe.wait_ge(*at("n1f_x", q + 1))
                for i, (a, n) in enumerate(TILES):
                    for k in range(4):
                        last = tr(PS[0:n, 2 * i + q, 128 * k:128 * k + 128], xT[:, 4 * q + k, a:a + n], 128)
                    last.then_inc(s("y_pe"), 1)

        @block.scalar
        def _(act):
            A = S_.activation
            chain = [0]

            def link(ins):
                chain[0] += 1
                ins.then_inc(s("act_chain"), 1)
                act.wait_ge(*at("act_chain", chain[0]))

            act.dma_start(cc[:], I["c_common"]).then_inc(s("ld_cc"), 16)
            act.dma_start(vrows[0:NVEC, 0:128], I["vec_rows"]).then_inc(s("ld_v"), 16)
            act.dma_start(vrows[0:NCONV, 128:256], I["conv_rows"]).then_inc(s("ld_v"), 16)
            act.dma_start(nload[0:32, :], I["state_mlstm_n"].rearrange("b h d -> (b h) d")).then_inc(s("ld_v"), 16)
            for r in range(2):
                act.dma_start(wsm[0][:, :, 32 * r:32 * r + 4], I["w_in0"][:, 4096 + 4 * r:4100 + 4 * r].rearrange("(k p) n -> p k n", p=128)).then_inc(s("ld_wsm"), 16)
            act.dma_start(gates0[0:4, :], I["gate_cols"][:, 0:2]).then_inc(s("ld_r"), 16)
            act.dma_start(m0[0:4, 0:8], I["m_rows"]).then_inc(s("ld_r"), 16)
            act.dma_start(r4[0:4, :], I["c_rows"]).then_inc(s("ld_r"), 16)
            act.dma_start(cst[:, 0:N0], I["c_layer0"]).then_inc(s("ld_c0"), 16)
            act.dma_start(stA[:], I["state_ret"].rearrange("b h d e -> d (b h) e")).then_inc(s("ld_stA"), 16)
            act.dma_start(stB[:], I["state_mlstm_c"].rearrange("b h d e -> d (b h) e")).then_inc(s("ld_stB"), 16)

            def x_hi(where, chunk, src, ready):
                act.wait_ge(*ready)
                k = slice(4 * chunk, 4 * chunk + 4)
                A(xsplit[where][0][:, k, :], src[:, k, :], COPY).then_inc(s("xhi"), 1)

            def proj_hi(layer, i):
                g = (0, IN1)[layer] + i // 2
                act.wait_ge(*at(f"ring{g % 2}", 16 * (g // 2 + 1)))
                if i >= 2:
                    act.wait_ge(*at("proj_pe", (0, 4 * IN1)[layer] + 2 * (i - 1)))
                elif layer == 1:
                    act.wait_ge(*at(*[("f0_hid_pe", FE * FT + 1), ("f0_down_pe", FE * KT + 1)][i]))
                A(proj_parts(layer, i, 0), raw_proj(g, i % 2), COPY).then_inc(s("ab"[layer] + "_hi"), 1)

            for c in range(2):
                for k in range(4 * c, 4 * c + 4):
                    act.wait_ge(*at("xT", k + 1))
                    last = A(xsplit["in0"][0][:, k, :], PS[:, k, 0:T], COPY)
                last.then_inc(s("xhi"), 1)
            proj_hi(0, 0)
            proj_hi(0, 1)

            for g, q in [(g, q) for g in range(8) for q in range(2)]:
                f = [COPY, COPY, COPY, SILU, COPY, COPY, COPY, SIGM][g]
                if 2 * g + q + 2 < 16:
                    proj_hi(0, 2 * g + q + 2)
                if (g, q) == (6, 0):
                    act.wait_ge(*at("rope", 1))
                for t in (2 * q, 2 * q + 1):
                    act.wait_ge(*at("proj_pe", 4 * g + t + 1))
                    A(P[:, 4 * g + t, :], PS[:, 4 * (g % 2) + t, 0:T], f, scale=128 ** -0.5 if g == 5 else 1.0).then_inc(s("proj_ev"), 1)
                if (g, q) == (0, 1):
                    act.wait_ge(*at("m_abs", 1))
                    link(A(ROW[5][:, 0:T], ROW[7][:, 0:T], EXP, scale=-1.0))
                    A(ROW[5][:, 0:T], ROW[5][:, 0:T], LN, bias=1.0).then_inc(s("m_lse"), 1)


            def norm(p, prepare=lambda: None):
                act.wait_ge(*at(p + "cent", 1))
                A(zT[:, 4:8, :], zT[:, 0:4, :], SQR).then_inc(s(p + "sq"), 1)
                prepare()
                act.wait_ge(*at(p + "var", 1))
                link(A(zT[:, 4:8, :], bank4(0), LN, bias=EPS))
                A(zT[:, 4:8, :], zT[:, 4:8, :], EXP, scale=-0.5).then_inc(s(p + "rstd"), 1)

            for i in range(3):
                n = TILES[i][1]
                act.wait_ge(*at("r_vt", i + 1))
                A(vtok[0:n, i, :], PS[0:n, 3 + i, :], COPY).then_inc(s("r_vtok"), 1)
            for i in range(3):
                n = TILES[i][1]
                act.wait_ge(*at("r_kt", i + 1))
                A(ktok[0:n, i, :], PS[0:n, i, :], COPY).then_inc(s("r_ktok"), 1)
            for h in range(H):
                act.wait_ge(*at("r_o", h + 1))
                A(zT[:, h, :], PS[:, h, 0:T], COPY).then_inc(s("r_oev"), 1)
            norm("r_")

            act.wait_ge(*at("m_rows", 1))
            A(ROW[6], ROW[6], EXP)
            A(ROW[5][:, 0:T], ROW[5][:, 0:T], EXP).then_inc(s("m_exp"), 1)
            act.wait_ge(*at("r_state_pe", 4))
            A(pst[:], PS[:, 6, :].rearrange("p (a b) -> p a b", a=4), COPY).then_inc(s("r_pst"), 1)
            act.wait_ge(*at("m_bc", 4))
            A(ebc, PS[:, 4:8, 0:344], COPY).then_inc(s("m_ebc"), 1)
            act.wait_ge(*at("m_col", 1))
            for h in range(H):
                act.wait_ge(*at("m_ex", h + 1))
                A(att[:, h, 0:A1], att[:, h, 0:A1], EXP, bias=mcol[:, h:h + 1])
                A(att[:, h, A1:A2], att[:, h, A1:A2], EXP, bias=mcol[:, 4 + h:5 + h])
                A(att[0:R2, h, A2:ATT], att[0:R2, h, A2:ATT], EXP, bias=mcol[0:R2, 8 + h:9 + h]).then_inc(s("m_w"), 1)
            for n_, (b, i, dst) in enumerate([(4, 0, ktok), (5, 1, ktok), (6, 2, ktok), (7, 0, vtok), (4, 1, vtok), (5, 2, vtok)]):
                n = TILES[i][1]
                act.wait_ge(*at("m_tpe", n_ + 1))
                A(dst[0:n, i, :], PS[0:n, b, :], COPY).then_inc(s("m_tok"), 1)
            x_hi("out", 0, mix, at("r_out", 1))
            act.wait_ge(*at("m_oev", 4))
            norm("m_", lambda: proj_hi(0, 16))
            x_hi("out", 1, mix, at("m_out", 1))
            act.wait_ge(*at("m_state_pe", 4))
            act.wait_ge(*at("st_rp", 16))
            A(pst[:], PS[:, 6, :].rearrange("p (a b) -> p a b", a=4), COPY).then_inc(s("m_pst"), 1)
            proj_hi(0, 17)
            def layer_norm(p, scaled, where=None, gain=None):
                for c in range(4):
                    act.wait_ge(*at(p + "cent", c + 1))
                    A(mix[:, 2 * c:2 * c + 2, :], zT[:, 2 * c:2 * c + 2, :], SQR).then_inc(s(p + "sq"), 1)
                act.wait_ge(*at(p + "var", 1))
                link(A(mix[:, 1, :], PS[:, LNB[p] + 1, 0:T], LN, bias=LN_EPS))
                A(mix[:, 0, :], mix[:, 1, :], EXP, scale=-0.5).then_inc(s(p + "rstd"), 1)
                if where:
                    for c in range(2):
                        act.wait_ge(*at(p + "zn", c + 1))
                        for k in range(4 * c, 4 * c + 4):
                            g = VEC[gain + "_g"] + k
                            last = A(xsplit[where][0][:, k, :], zT[:, k, :], IDN, scale=vec[:, g:g + 1], bias=vec[:, g + 8:g + 9])
                        last.then_inc(s("xhi"), 1)
                if scaled:
                    act.wait_ge(*at(p + "x", 2))
                    act.wait_ge(*at("xhi", {"n0m_": 6, "n1m_": 12}[p]))
                    A(zT[:], xT[:], COPY, scale=ALPHA).then_inc(s(p + "z"), 1)

            def hidden_hi(p, e, j, free):
                act.wait_ge(*at(p + f"w{j // 2 % 2}", e * 96 + 32 * (j // 4 + 1)))
                act.wait_ge(*free)
                A(gu_parts(j, 0), raw_gu(j), COPY).then_inc(s(p + "hi"), 1)

            def ffn_first(layer):
                last_unit = 4 * (OUT0 + 2 if layer == 0 else GEND)
                for j in range(2):
                    hidden_hi(f"f{layer}_", 0, j, at("proj_pe", last_unit - 2 + 2 * j))

            def ffn(layer):
                p, E = f"f{layer}_", (FE, NE)[layer]

                def body(e, is_last, with_router):
                    for n in range(2, UN):
                        if with_router and n < 4:
                            act.wait_ge(*at("x_bc", 4 * (n - 1)))
                            A(gbc[:, 4 * n - 8:4 * n - 4, :], bank4(4), COPY).then_inc(s("x_bcev"), 1)
                        if n < FT:
                            hidden_hi(p, e, n, at(p + "hid_pe", e * FT + n))
                        else:
                            d = n - FT
                            act.wait_ge(*at(p + f"d{d // 2 % 2}", e * 32 + 16 * (d // 4 + 1)))
                            if d == 1:
                                act.wait_ge(*at(p + "hid_pe", e * FT + FT))
                            elif d >= 2:
                                act.wait_ge(*at(p + "down_pe", e * KT + d))
                            A(down_parts(d, 0), raw_down(d), COPY).then_inc(s(p + "hi"), 1)
                        j = n - 2
                        if j < FT:
                            act.wait_ge(*at(p + "hid_pe", e * FT + (j + 2)))
                            A(gact[:, j % 2, :], PS[:, 2 * (j % 2), 0:T], SILU).then_inc(s(p + "silu"), 1)
                    if not is_last:
                        hidden_hi(p, e + 1, 0, at(p + "hid_pe", e * FT + (FT + 1)))
                        hidden_hi(p, e + 1, 1, at(p + "down_pe", e * KT + (KT + 1)))

                over_experts(act, E, body)

            proj_hi(0, 18)
            act.wait_ge(*at("m_npe", 1))
            A(nrow[0:36, :], PS[0:36, 5, 0:128], COPY).then_inc(s("m_nrow"), 1)
            act.wait_ge(*at("m_stu", 4))
            proj_hi(0, 19)
            ffn_first(0)
            layer_norm("n0m_", True, "out", "mix0")
            ffn(0)
            proj_hi(1, 0)
            proj_hi(1, 1)
            layer_norm("n0f_", False, "in1", "ffn0")

            act.wait_ge(*at("small_pe", 2))
            A(GROW[0][:, 0:T], PS[0:4, NARROW, 0:T], SIGM).then_inc(s("g_beta"), 1)
            act.wait_ge(*at("g_abs", 1))
            A(gates0[0:4, 0:1], gates0[0:4, 0:1], EXP)
            link(A(GROW[6][:, 0:T], GROW[6][:, 0:T], EXP, scale=-1.0))
            A(GROW[6][:, 0:T], GROW[6][:, 0:T], LN, bias=1.0).then_inc(s("g_lse"), 1)
            act.wait_ge(*at("g_gc", 1))
            A(GROW[3][:, 0:T], GROW[2][:, 0:T], EXP)
            A(GROW[5][:, 0:T], GROW[5][:, 0:T], EXP)
            A(GROW[1][:, 0:11], GROW[2][:, T:T + 11], EXP).then_inc(s("g_eg"), 1)

            proj_hi(1, 2)
            act.wait_ge(*at("cin0", 1))

            def conv_out(m):
                act.wait_ge(*at("conv", m + 1))
                A(P[:, m, 0:TP], cacc[:, m % 2, 0:TP], SILU)
                A(smp(P[:, m, :]), cconv(m), SILU).then_inc(s("convs"), 1)

            for g, q in [(g, q) for g in range(IN1, OUT1) for q in range(2)]:
                if 2 * (g - IN1) + q + 3 < 14:
                    proj_hi(1, 2 * (g - IN1) + q + 3)
                for t in (2 * q, 2 * q + 1):
                    m = 4 * (g - IN1) + t
                    act.wait_ge(*at("proj_pe", 4 * g + t + 1))
                    ps = PS[:, 4 * (g % 2) + t, 0:T]
                    if m < 12:
                        if m >= 4:
                            act.wait_ge(*at("conv", m - 3))
                            act.wait_ge(*at("last", m - 3))
                        A(cin[:, m % 4, 3:3 + TP], ps[:, 0:TP], COPY)
                        A(cins(m)[:, :, 3:7], smp(ps), COPY).then_inc(s("cin"), 1)
                        act.wait_ge(*at("cin", m + 1))
                        act.sem_inc(s("proj_ev"), 1)
                        if m:
                            conv_out(m - 1)
                    else:
                        if m == 12:
                            conv_out(11)
                        f = SILU if m < 16 or m >= 24 else COPY
                        A(P[:, m, :], ps, f, scale=64 ** -0.5 if m in (16, 17) else 1.0).then_inc(s("proj_ev"), 1)

            act.wait_ge(*at("convs", 12))
            A(sqn, P[:, 0:8, :], SQR).then_inc(s("g_sqn"), 1)
            act.wait_ge(*at("g_bc", 1))
            A(dbc, PS[:, 0:4, T:T + 11], COPY)
            A(qe, bank4(0), EXP).then_inc(s("g_eq"), 1)
            for h in range(H):
                act.wait_ge(*at("g_dx", h + 1))
                for i, (a, n) in enumerate(TILES):
                    last = A(decI[0:n, h, a:a + n], decI[0:n, h, a:a + n], EXP, bias=gcol[0:n, 2, i, h:h + 1])
                last.then_inc(s("g_dec"), 1)
            act.wait_ge(*at("g_l2pe", 1))
            A(sqn, PS[:, 0:8, 0:T], LN, bias=EPS).then_inc(s("g_l2a"), 1)
            act.wait_ge(*at("g_l2a", 1))
            A(sqn[:, 4:8, :], sqn[:, 4:8, :], EXP, scale=-0.5).then_inc(s("g_l2r"), 1)
            A(sqn[:, 0:4, :], sqn[:, 0:4, :], EXP, scale=-0.5, bias=-0.5 * math.log(128)).then_inc(s("g_l2r"), 1)
            act.wait_ge(*at("last_pe", 1))
            A(lastrow[0:27, :], PS[0:27, 5:8, :], COPY).then_inc(s("last_ev"), 1)
            for i, (a, n) in enumerate(TILES):
                act.wait_ge(*at("g_kt", i + 1))
                A(ktg[0:n, i, :], PS[0:n, i, :], COPY).then_inc(s("g_tok_a"), 1)
            for i, (a, n) in enumerate(TILES):
                act.wait_ge(*at("g_w", i + 1))
                A(kb[:, :, a:a + n], PS[:, i, 0:4 * n].rearrange("p (a b) -> p a b", a=4), COPY, scale=-1.0).then_inc(s("g_wev"), 1)
            for i, (a, n) in enumerate(TILES):
                act.wait_ge(*at("g_upe", i + 1))
                A(ug[0:n, i, :], PS[0:n, 3, :], COPY).then_inc(s("g_ua"), 1)
            act.wait_ge(*at("l_abs", 1))
            link(A(cb_, cb_, EXP, scale=-1.0))
            A(cb_, cb_, LN, bias=1.0).then_inc(s("l_lse"), 1)
            act.wait_ge(*at("l_x", 1))
            A(e1, cb_, EXP)
            A(e2, cb_, EXP, scale=-1.0)
            A(e3, bc_, EXP)
            A(kx_, kx_, EXP).then_inc(s("l_e"), 1)
            act.wait_ge(*at("g_o", 4))
            A(zT[:, 0:4, :], bank4(0), COPY).then_inc(s("g_oev"), 1)
            act.wait_ge(*at("g_oev", 1))
            A(zT[:, 4:8, :], zT[:, 0:4, :], SQR).then_inc(s("g_sq"), 1)
            act.wait_ge(*at("g_var", 1))
            link(A(zT[:, 4:8, :], bank4(0), LN, bias=EPS))
            A(zT[:, 4:8, :], zT[:, 4:8, :], EXP, scale=-0.5).then_inc(s("g_rstd"), 1)

            for i, (a, n) in enumerate(TILES):
                act.wait_ge(*at("l_vt", i + 1))
                A(vtl[0:n, i, :], PS[0:n, (4, 5, 7)[i], :], COPY).then_inc(s("l_tok"), 1)
            act.wait_ge(*at("l_kt", 1))
            for i in range(3):
                n = TILES[i][1]
                A(ktl[0:n, i, :], PS[0:n, 3 + i // 2, 256 * (i % 2):256 * (i % 2) + 256], COPY).then_inc(s("l_tok"), 1)
            x_hi("out", 0, mix, at("g_out", 1))
            for h in range(H):
                act.wait_ge(*at("l_o", h + 1))
                A(zT[:, h, :], PS[:, h, 0:T], COPY).then_inc(s("l_oev"), 1)
            norm("l_", lambda: proj_hi(1, 14))
            x_hi("out", 1, mix, at("l_out", 1))
            act.wait_ge(*at("l_state_pe", 4))
            proj_hi(1, 15)
            proj_hi(1, 16)
            proj_hi(1, 17)
            ffn_first(1)
            layer_norm("n1m_", True, "out", "mix1")
            act.wait_ge(*at("x_lm", 1))
            A(lt, lt, EXP).then_inc(s("x_exp"), 1)
            ffn(1)
            layer_norm("n1f_", False)
            for q, i in ((0, 0), (0, 1), (0, 2), (1, 1)):
                n = TILES[i][1]
                act.wait_ge(*at("y_pe", 3 * q + i + 1))
                A(proj[0:n, 1024 * i + 512 * q:1024 * i + 512 * q + 512], PS[0:n, 2 * i + q, :], COPY).then_inc(s("y_ev"), 1)

        @block.gpsimd
        def _(pool):
            pool.wait_ge(*at("ld_c0", 16))
            pool.wait_ge(*at("rot", 1))
            cos = const(C0, "cos").rearrange("p (a b) -> p a b", a=2)
            for a in range(2):
                q = P[:, 4 * a:4 * a + 4, :]
                G.tensor_tensor(q, q, cos[:, a:a + 1, :].to_broadcast([128, 4, T]), MUL).then_inc(s("ropec"), 1)

            def out_state(p, st, dram_s, dram_p):
                for h in range(H):
                    pool.wait_ge(*at(p + "stu", h + 1))
                    pool.dma_start(dram_s[:, h].rearrange("b d e -> d b e"), st[:, h::4, :]).then_inc(s("st_all"), 16)
                pool.wait_ge(*at(p + "pst", 1))
                pool.dma_start(dram_p.rearrange("h d e -> d h e"), pst[:]).then_inc(s("st_" + p[0] + "p"), 16)

            pool.wait_ge(*at("r_vtok", 3))
            gk = const(C0, "gk").rearrange("p (a b) -> p a b", a=2)
            gk2 = const(C0, "gk2").rearrange("p (a b) -> p a b", a=4)
            for i in range(2):
                last = G.tensor_tensor(vd[:, i], vtok[:, i, :].rearrange("p (a b) -> p a b", a=4),
                                       gk[:, i, :].unsqueeze(2).to_broadcast([128, 4, 128]), MUL)
            last.then_inc(s("r_vd"), 1)
            pool.wait_ge(*at("m_rows", 1))
            for h in range(H):
                if h >= 2:
                    pool.wait_ge(*at("r_state_pe", h - 1))
                G.tensor_tensor(vb[h % 2][0:R2], vtok[0:R2, 2, 128 * h:128 * h + 128].unsqueeze(1).to_broadcast([R2, SEGS, 128]),
                                gk2[0:R2, h, :].unsqueeze(2).to_broadcast([R2, SEGS, 128]), MUL).then_inc(s("r_vb"), 1)
            out_state("r_", stA, O["sample_ret"], O["prompt_ret"][0])

            pool.wait_ge(*at("m_wl2", 1))
            pool.wait_ge(*at("m_tok", 6))
            for i in range(2):
                last = G.tensor_tensor(vd[:, i], vtok[:, i, :].rearrange("p (a b) -> p a b", a=4),
                                       mcol[:, 12 + 4 * i:16 + 4 * i].unsqueeze(2).to_broadcast([128, 4, 128]), MUL)
            last.then_inc(s("m_vd"), 1)
            for h in range(H):
                if h >= 2:
                    pool.wait_ge(*at("m_state_pe", h - 1))
                G.tensor_tensor(vb[h % 2][0:R2], vtok[0:R2, 2, 128 * h:128 * h + 128].unsqueeze(1).to_broadcast([R2, SEGS, 128]),
                                wl2[0:R2, h, :].unsqueeze(2).to_broadcast([R2, SEGS, 128]), MUL).then_inc(s("m_vb"), 1)
            out_state("m_", stB, O["sample_c"], O["prompt_c"][0])
            pool.wait_ge(*at("m_nrow", 1))
            pool.dma_start(O["sample_n"].rearrange("b h d -> (b h) d"), nrow[0:32, :]).then_inc(s("st_all"), 16)
            pool.dma_start(O["prompt_n"].rearrange("b h d -> (b h) d"), nrow[32:36, :]).then_inc(s("st_all"), 16)
            pool.wait_ge(*at("m_mt", 1))
            pool.dma_start(O["m_rows"], m0[0:4, 0:9]).then_inc(s("st_all"), 16)

            pool.wait_ge(*at("m_out", 1))
            pool.dma_start(cst[:, 0:N1], I["c_layer1"]).then_inc(s("ld_l1"), 16)
            pool.dma_start(gates0[0:4, :], I["gate_cols"][:, 2:4]).then_inc(s("ld_l1"), 16)
            for r in range(2):
                pool.dma_start(wsm[1][:, :, 32 * r:32 * r + 4], I["w_in1"][:, 2048 + 4 * r:2052 + 4 * r].rearrange("(k p) n -> p k n", p=128)).then_inc(s("ld_l1"), 16)
            pool.dma_start(wsm[1][:, :, 64:80], I["w_in1"][:, 3592:3608].rearrange("(k p) n -> p k n", p=128)).then_inc(s("ld_l1"), 16)
            pool.dma_start(walpha, I["gla_w_alpha"]).then_inc(s("ld_l1"), 16)
            pool.wait_ge(*at("st_all", 16 * 11))
            pool.wait_ge(*at("st_rp", 16))
            pool.wait_ge(*at("st_mp", 16))
            pool.wait_ge(*at("f0_down_pe", 1 + FE * KT))
            pool.dma_start(r4b[0:4, :], I["c_rows"]).then_inc(s("ld_gdn"), 16)
            pool.dma_start(stA[:], I["state_gdn"].rearrange("b h d e -> d (b h) e")).then_inc(s("ld_gdn"), 16)
            pool.wait_ge(*at("n0f_x", 2))
            pool.wait_ge(*at("xhi", 8))
            pool.dma_start(halo, I["state_gdn_conv"].rearrange("b w c -> (b w) c")).then_inc(s("ld_halo"), 16)

            for m in range(12):
                pool.wait_ge(*at("cin", m + 1))
                G.tensor_copy(lastT[:, m, 0:3], cin[:, m % 4, TP:TP + 3])
                G.tensor_copy(lastT[:, m, 3:27].rearrange("p (b t) -> p b t", b=NB), cins(m)[:, :, 4:7]).then_inc(s("last"), 1)
            pool.wait_ge(*at("last_ev", 1))
            pool.dma_start(O["prompt_conv"][0], lastrow[0:3, :]).then_inc(s("st_conv"), 16)
            pool.dma_start(O["sample_conv"].rearrange("b w c -> (b w) c"), lastrow[3:27, :]).then_inc(s("st_conv"), 16)

            pool.wait_ge(*at("g_ue", 3))
            blk = const(C1, "blk")
            for h in range(H):
                if h >= 2:
                    pool.wait_ge(*at("g_state_pe", h - 1))
                G.tensor_tensor(ub[h % 2][0:R2], rhsk[0:R2, 2, 128 * h:128 * h + 128].unsqueeze(1).to_broadcast([R2, SEGS, 128]),
                                blk[0:R2].unsqueeze(2).to_broadcast([R2, SEGS, 128]), MUL).then_inc(s("g_vb"), 1)
            pool.wait_ge(*at("g_upe", 3))
            for r in range(2):
                pool.dma_start(stG[64 * r:64 * r + 64], I["state_gla"][:, r::2].rearrange("b p d e -> d b p e")).then_inc(s("ld_stG"), 16)
            for h in range(H):
                pool.wait_ge(*at("g_stu", h + 1))
                pool.dma_start(O["sample_gdn"][:, h].rearrange("b d e -> d b e"), stA[:, h::4, :]).then_inc(s("st_all"), 16)
            pool.wait_ge(*at("g_pst", 1))
            pool.dma_start(O["prompt_gdn"][0].rearrange("h d e -> d h e"), sg[:, 2]).then_inc(s("st_gp"), 16)

            pool.wait_ge(*at("l_tok", 3))
            last = G.tensor_tensor(lvp[0:R2], vtl[0:R2, 2, :].rearrange("p (a b) -> p a b", a=4),
                                   blk[0:R2, 0:1].unsqueeze(2).to_broadcast([R2, 4, 128]), MUL)
            last.then_inc(s("l_vb0"), 1)
            for h in range(H):
                if h >= 2:
                    pool.wait_ge(*at("l_state_pe", h - 1))
                G.tensor_tensor(lb[h % 2][0:R2], vtl[0:R2, 2, 128 * h:128 * h + 128].unsqueeze(1).to_broadcast([R2, SEGS, 128]),
                                blk[0:R2].unsqueeze(2).to_broadcast([R2, SEGS, 128]), MUL).then_inc(s("l_vb"), 1)
            pool.wait_ge(*at("l_sc", 2))
            for r in range(2):
                pool.dma_start(O["prompt_gla"][0, r::2].rearrange("p d e -> d p e"), sc[64 * r:64 * r + 64, 4]).then_inc(s("st_all"), 16)
            pool.wait_ge(*at("l_stu", 4))
            for r in range(2):
                pool.dma_start(O["sample_gla"][:, r::2].rearrange("b p d e -> d b p e"), stG[64 * r:64 * r + 64]).then_inc(s("st_all"), 16)
            pool.wait_ge(*at("l_out", 1))
            pool.dma_start(wrt, I["moe_w_router"].rearrange("(k p) n -> p k n", p=128)).then_inc(s("ld_router"), 16)
            pool.dma_start(brt[0:1, :], I["moe_b_router"].rearrange("(a n) -> a n", a=1)).then_inc(s("ld_router"), 16)
            pool.wait_ge(*at("st_all", 16 * 19))
            pool.wait_ge(*at("st_gp", 16))
            pool.wait_ge(*at("st_conv", 32))

        @block.vector
        def _(dve):
            TT, TSC, STT, CP = V.tensor_tensor, V.tensor_scalar, V.scalar_tensor_tensor, V.tensor_copy
            chain = [0]

            def link(ins):
                chain[0] += 1
                ins.then_inc(s("dve_chain"), 1)
                dve.wait_ge(*at("dve_chain", chain[0]))

            V.memset(wsm[0][:, :, 4:32], 0.0)
            for k in range(KT):
                dve.wait_ge(*at("xt_pe", k + 1))
                CP(xT[:, k, :], PS[:, k, 0:T]).then_inc(s("xT"), 1)

            def x_lo(where, chunk, src, n):
                dve.wait_ge(*at("xhi", n))
                k = slice(4 * chunk, 4 * chunk + 4)
                TT(xsplit[where][1][:, k, :], src[:, k, :], xsplit[where][0][:, k, :].bitcast(F32), SUB).then_inc(s("xlo"), 1)

            def proj_lo(layer, i):
                dve.wait_ge(*at("ab"[layer] + "_hi", i + 1))
                g = (0, IN1)[layer] + i // 2
                TT(proj_parts(layer, i, 1), raw_proj(g, i % 2), proj_parts(layer, i, 0).bitcast(F32), SUB).then_inc(s("ab"[layer] + "_lo"), 1)

            for c in range(2):
                x_lo("in0", c, xT, c + 1)
            dve.wait_ge(*at("vec_pe", 1))
            CP(vec[:, 0:NVEC], PS[:, 0, 0:NVEC])
            CP(vec[:, NVEC:NVEC + NCONV], PS[:, 0, 128:128 + NCONV])
            CP(nT[:, 0:32], PS[:, 0, 256:288]).then_inc(s("vec_ev"), 1)
            for i in range(4):
                proj_lo(0, i)

            f, i_, b_, a_, M = ROW[1][:, 0:T], ROW[0][:, 0:T], ROW[2][:, 0:T], ROW[3][:, 0:T], ROW[4][:, 0:T]
            ab, l_, pk = ROW[7][:, 0:T], ROW[5][:, 0:T], ROW[6]
            dve.wait_ge(*at("small_pe", 1))
            dve.wait_ge(*at("ld_r", 48))
            TSC(i_, PS[0:4, NARROW, 0:T], gates0[0:4, 0:1], None, ADD)
            link(CP(f, PS[32:36, NARROW, 0:T]))
            link(TSC(f, f, gates0[0:4, 1:2], None, ADD))
            STT(ab, f, -1.0, f, MUL, MAX).then_inc(s("m_abs"), 1)
            dve.sem_inc(s("small_ev"), 1)
            dve.wait_ge(*at("m_lse", 1))
            link(STT(f, f, 0.0, l_, MIN, SUB))
            link(V.tensor_tensor_scan(b_, r4[0:4, 0:T], f, 0.0, MUL, ADD))
            link(TT(a_, i_, b_, SUB))
            link(CP(ab, a_))
            link(TSC(ab[:, 0:1], ab[:, 0:1], 0.0, None, MAX))
            link(TT(smp(ab)[:, :, 0], smp(ab)[:, :, 0], m0[0:4, 0:8], MAX))
            link(V.tensor_tensor_scan(M, r4[0:4, T:2 * T], ab, 0.0, ADD, MAX))
            STT(pk[:, 0:T], b_, -1.0, M, MUL, SUB)
            TT(pk[:, T:T + TS].rearrange("p (b t) -> p b t", b=NB), m0[0:4, 0:8].unsqueeze(2).to_broadcast([4, NB, NS]), smp(M), SUB)
            TT(pk[:, T + TS:T + TS + NB], m0[0:4, 0:8], smp(M)[:, :, NS - 1], SUB)
            TSC(l_[:, 0:TP], a_[:, 0:TP], M[:, TP - 1:TP], None, SUB)
            link(TT(smp(l_), smp(a_), smp(M)[:, :, NS - 1:NS].to_broadcast([4, NB, NS]), SUB))
            link(STT(m0[0:4, 0:8], smp(b_)[:, :, NS - 1], 0.0, smp(M)[:, :, NS - 1], ADD, ADD))
            TT(m0[0:4, 8:9], b_[:, TP - 1:TP], M[:, TP - 1:TP], ADD).then_inc(s("m_mt"), 1)
            dve.sem_inc(s("m_rows"), 1)

            for i in range(4, 9):
                proj_lo(0, i)
            dve.wait_ge(*at("ld_c0", 16))
            dve.wait_ge(*at("rot", 1))
            sin = const(C0, "sin").rearrange("p (a b) -> p a b", a=2)
            for a in range(2):
                last = TT(P[:, 24 + 4 * a:28 + 4 * a, :], bank4(4 * a), sin[:, a:a + 1, :].to_broadcast([128, 4, T]), MUL)
            link(last)
            dve.sem_inc(s("rotm"), 1)
            proj_lo(0, 9)
            dve.wait_ge(*at("ropec", 2))
            link(TT(P[:, 0:8, :], P[:, 0:8, :], P[:, 24:32, :], ADD))
            dve.sem_inc(s("rope"), 1)
            for i in range(10, 2 * OUT0):
                proj_lo(0, i)

            def norm(p, dst, gate0, gain, rms=False, prepare=lambda: None):
                if not rms:
                    dve.wait_ge(*at(p + "mean", 1))
                    TT(zT[:, 0:4, :], zT[:, 0:4, :], bank4(0), SUB).then_inc(s(p + "cent"), 1)
                prepare()
                dve.wait_ge(*at(p + "rstd", 1))
                link(TT(zT[:, 0:4, :], zT[:, 0:4, :], zT[:, 4:8, :], MUL))
                for h in range(H):
                    g = vec[:, VEC[gain] + h:VEC[gain] + h + 1]
                    if gate0 is None:
                        last = TSC(mix[:, dst + h, :], zT[:, h, :], g, None, MUL)
                    else:
                        last = STT(mix[:, dst + h, :], zT[:, h, :], g, P[:, gate0 + h, :], MUL, MUL)
                last.then_inc(s(p + "out"), 1)

            def state_update(p, st, h, banks, decay):
                v = st[:, h::4, :]
                if decay is None:
                    for j, b in enumerate(banks):
                        last = STT(v[:, 4 * j:4 * j + 4, :], v[:, 4 * j:4 * j + 4, :], math.exp(4 * math.log(1 - 2.0 ** (-5 - h))),
                                   PS[:, b, :].rearrange("p (a b) -> p a b", a=4), MUL, ADD)
                else:
                    link(TT(v, v, decay.unsqueeze(2).to_broadcast([128, NB, 128]), MUL))
                    for j, b in enumerate(banks):
                        last = TT(v[:, 4 * j:4 * j + 4, :], v[:, 4 * j:4 * j + 4, :], PS[:, b, :].rearrange("p (a b) -> p a b", a=4), ADD)
                last.then_inc(s(p + "stu"), 1)

            dve.wait_ge(*at("proj_ev", 32))
            TT(qs, P[:, 0:4, TP:T], const(C0, "gq").rearrange("p (a b) -> p a b", a=4), MUL).then_inc(s("r_qs"), 1)
            dec = const(C0, "dec").rearrange("p (a b) -> p a b", a=4)
            for h, b in enumerate([6, 7, 3, 4]):
                dve.wait_ge(*at("r_qk", h + 1))
                TT(att[:, h, 0:A2], PS[:, b, 0:A2], dec[:, h, 0:A2], MUL)
                TT(att[0:R2, h, A2:ATT], PS[0:R2, b, A2:ATT], dec[0:R2, h, A2:ATT], MUL).then_inc(s("r_att"), 1)
            def r_update(h):
                dve.wait_ge(*at("r_state_pe", h + 1))
                state_update("r_", stA, h, RPAIRS[h], None)

            norm("r_", 0, 12, "ret", prepare=lambda: r_update(0))
            for h in range(1, H):
                r_update(h)

            mask = const(C0, "mask")
            dve.wait_ge(*at("m_colpe", 1))
            CP(mcol[:, 0:8], PS[:, 7, 0:8])
            CP(mcol[0:R2, 8:12], PS[0:R2, 7, 8:12])
            CP(mcol[:, 12:20], PS[:, 7, 12:20])
            link(CP(mcol[0:R2, 20:24], PS[0:R2, 7, 20:24]))
            dve.sem_inc(s("m_col"), 1)
            TT(wl2[0:R2], mcol[0:R2, 20:24].unsqueeze(2).to_broadcast([R2, 4, 9]), const(C0, "blk")[0:R2].unsqueeze(1).to_broadcast([R2, 4, 9]),
               MUL).then_inc(s("m_wl2"), 1)
            for h in range(H):
                dve.wait_ge(*at("m_bc", h + 1))
                TT(att[:, h, 0:A1], mask[:, 0:A1], PS[:, h, 0:TP], SUB)
                TT(att[:, h, A1:A2], mask[:, A1:A2], PS[:, h, 128:TP], SUB)
                TT(att[0:R2, h, A2:ATT], mask[0:R2, A2:ATT], PS[0:R2, h, 256:T], SUB).then_inc(s("m_ex"), 1)
            dve.wait_ge(*at("m_ebc", 1))
            link(TT(qs, P[:, 16:20, TP:T], ebc[:, :, T:T + TS], MUL))
            TT(qn.rearrange("p h (b t) -> p h b t", b=NB), qs.rearrange("p h (b t) -> p h b t", b=NB),
               nT[:, 0:32].rearrange("p (b h) -> p h b", h=H).unsqueeze(3).to_broadcast([128, H, NB, NS]), MUL).then_inc(s("m_qs"), 1)
            for h in range(H):
                dve.wait_ge(*at("m_qk", h + 1))
                dve.wait_ge(*at("m_w", h + 1))
                TT(att[:, h, 0:A2], PS[:, h, 0:A2], att[:, h, 0:A2], MUL)
                TT(att[0:R2, h, A2:ATT], PS[0:R2, h, A2:ATT], att[0:R2, h, A2:ATT], MUL).then_inc(s("m_att"), 1)
            x_lo("out", 0, mix, 3)
            for h in range(H):
                o, d = zT[:, h, :], zT[:, 4 + h, :]
                dve.wait_ge(*at("m_o", h + 1))
                link(TT(d, PS[:, 4 + h, 0:T], ebc[:, h, 0:T], MAX))
                link(STT(d, PS[:, 4 + h, 0:T], -1.0, d, MUL, MAX))
                link(V.reciprocal(d, d))
                link(TT(d, d, P[:, 28 + h, :], MUL))
                TT(o, PS[:, h, 0:T], d, MUL).then_inc(s("m_oev"), 1)

            def m_update(h):
                dve.wait_ge(*at("m_state_pe", h + 1))
                state_update("m_", stB, h, MPAIRS[h], ebc[:, h, T + TS:T + TS + NB])

            norm("m_", 4, None, "mlstm", prepare=lambda: (m_update(0), proj_lo(0, 16)))
            for r in range(2):
                V.memset(wsm[1][:, :, 32 * r + 4:32 * r + 32], 0.0)
            m_update(1)
            x_lo("out", 1, mix, 4)
            m_update(2)
            m_update(3)
            proj_lo(0, 17)
            for h in range(H):
                n = nT[:, h:32:4]
                link(TT(n, n, ebc[:, h, T + TS:T + TS + NB], MUL))
                TT(n, n, PS[:, 5, 9 * h + 1:9 * h + 9], ADD)
                last = CP(nT[:, 32 + h:33 + h], PS[:, 5, 9 * h:9 * h + 1])
            last.then_inc(s("m_nst"), 1)

            def residual(layer):
                g0, i0 = ((OUT0, 2 * OUT0), (OUT1, 2 * (OUT1 - IN1)))[layer]
                for u in range(4):
                    if u < 2:
                        proj_lo(layer, i0 + 2 + u)
                    for k in (2 * u, 2 * u + 1):
                        g = g0 + k // 4
                        dve.wait_ge(*at("proj_pe", 4 * g + k % 4 + 1))
                        STT(zT[:, k, :], xT[:, k, :], ALPHA, PS[:, 4 * (g % 2) + k % 4, 0:T], MUL, ADD).then_inc(s("proj_ev"), 1)

            def layer_norm(p, gain, prepare=lambda: None, where=None, n=0):
                dve.wait_ge(*at(p + "mean", 1))
                for c in range(4):
                    z = zT[:, 2 * c:2 * c + 2, :]
                    TT(z, z, PS[:, LNB[p]:LNB[p] + 1, 0:T].to_broadcast([128, 2, T]), SUB).then_inc(s(p + "cent"), 1)
                prepare()
                dve.wait_ge(*at(p + "rstd", 1))
                for c in range(2):
                    z = zT[:, 4 * c:4 * c + 4, :]
                    TT(z, z, mix[:, 0:1, :].to_broadcast([128, 4, T]), MUL).then_inc(s(p + "zn"), 1)
                    if c == 1 and where:
                        dve.wait_ge(*at(p + "x", 1))
                        x_lo(where, 0, xT, n)
                    dve.wait_ge(*at(p + "zn", c + 1))
                    for k in range(4 * c, 4 * c + 4):
                        g = VEC[gain + "_g"] + k
                        last = TSC(xT[:, k, :], zT[:, k, :], vec[:, g:g + 1], vec[:, g + 8:g + 9], MUL, ADD)
                    last.then_inc(s(p + "x"), 1)
                if where:
                    dve.wait_ge(*at(p + "x", 2))
                    x_lo(where, 1, xT, n + 1)

            def hidden_lo(p, e, j):
                dve.wait_ge(*at(p + "hi", e * UN + (j + 1)))
                TT(gu_parts(j, 1), raw_gu(j), gu_parts(j, 0).bitcast(F32), SUB).then_inc(s(p + "lo"), 1)

            def ffn_first(layer):
                p = f"f{layer}_"
                dve.sem_inc(s(p + "lo"), UC)
                dve.sem_inc(s(p + "hid_ev"), 1)
                dve.sem_inc(s(p + "down_ev"), 4)
                hidden_lo(p, 0, 0)
                hidden_lo(p, 0, 1)

            def ffn(layer):
                p, E = f"f{layer}_", (FE, NE)[layer]
                steps = 1 + layer

                def hidden(e, j):
                    dve.wait_ge(*at(p + "silu", e * FT + (j + 1)))
                    a, b, n = gact[:, j % 2, :], PS[:, 2 * (j % 2) + 1, 0:T], e * (steps * FT) + (steps * j + 1)
                    if layer == 1:
                        TT(gu_raw, a, b, MUL).then_inc(s(p + "gu"), 1)
                        dve.wait_ge(*at(p + "gu", n))
                        a, b, n = gu_raw, gbc[:, e, :], n + 1
                    TT(hraw[:, j % 2, :], a, b, MUL)
                    TT(hsplit[0][:, j, :], a, b, MUL).then_inc(s(p + "gu"), 1)
                    dve.wait_ge(*at(p + "gu", n))
                    TT(hsplit[1][:, j, :], hraw[:, j % 2, :], hsplit[0][:, j, :].bitcast(F32), SUB).then_inc(s(p + "hid_ev"), 1)

                def add(e, d):
                    dve.wait_ge(*at(p + "down_pe", e * KT + (d + 2)))
                    TT(zT[:, d, :], zT[:, d, :], PS[:, 4 + d % 4, 0:T], ADD).then_inc(s(p + "down_ev"), 1)

                def body(e, is_last, with_router):
                    if with_router:
                        dve.wait_ge(*at("x_gt", 1))
                        CP(gT[0:8, :], PS[0:8, 7, 0:T]).then_inc(s("x_gtev"), 1)
                    for n in range(2, UN):
                        if n < FT:
                            hidden_lo(p, e, n)
                        else:
                            dve.wait_ge(*at(p + "hi", e * UN + (n + 1)))
                            d = n - FT
                            TT(down_parts(d, 1), raw_down(d), down_parts(d, 0).bitcast(F32), SUB).then_inc(s(p + "lo"), 1)
                        if with_router and n == 2:
                            dve.wait_ge(*at("x_bcev", 1))
                        if with_router and n == 6:
                            dve.wait_ge(*at("x_bcev", 2))
                        if n - 2 < FT:
                            hidden(e, n - 2)
                        else:
                            add(e, n - 2 - FT)
                    for j in range(2):
                        if not is_last:
                            hidden_lo(p, e + 1, j)
                        add(e, KT - 2 + j)

                over_experts(dve, E, body)

            residual(0)
            layer_norm("n0m_", "mix0", lambda: ffn_first(0), "out", 5)
            dve.wait_ge(*at("n0m_z", 1))
            dve.wait_ge(*at("st_all", 16 * 11))
            ffn(0)

            def first_lo():
                proj_lo(1, 0)
                proj_lo(1, 1)

            layer_norm("n0f_", "ffn0", first_lo, "in1", 7)

            V.memset(cin[:, :, 0:3], 0.0)
            x_, tmp, gc = GROW[1][:, 0:T], GROW[6][:, 0:T], GROW[2]
            dve.wait_ge(*at("small_pe", 2))
            dve.wait_ge(*at("ld_l1", 96))
            dve.wait_ge(*at("ld_gdn", 32))
            CP(lrT, PS[64:80, NARROW, 0:T])
            link(CP(x_, PS[32:36, NARROW, 0:T]))
            link(TSC(x_, x_, gates0[0:4, 1:2], None, ADD))
            STT(tmp, x_, -1.0, x_, MUL, MAX).then_inc(s("g_abs"), 1)
            dve.wait_ge(*at("g_beta", 1))
            dve.sem_inc(s("small_ev"), 1)
            dve.wait_ge(*at("g_lse", 1))
            link(STT(x_, x_, 0.0, tmp, MAX, ADD))
            link(TSC(x_, x_, gates0[0:4, 0:1], -1.0, MUL, MUL))
            link(V.tensor_tensor_scan(gc[:, 0:T], r4b[0:4, 2 * T:3 * T], x_, 0.0, MUL, ADD))
            CP(gc[:, T:T + 2], gc[:, 127:256:128])
            CP(gc[:, T + 2:T + 3], gc[:, TP - 1:TP])
            CP(gc[:, T + 3:T + 11], smp(gc)[:, :, NS - 1])
            TSC(GROW[4][:, 0:T], gc[:, 0:T], -1.0, None, MUL)
            for a, n in [(0, 128), (128, 128), (256, PR2)]:
                TSC(GROW[5][:, a:a + n], gc[:, a:a + n], -1.0, gc[:, a + n - 1:a + n], MUL, ADD)
            TT(smp(GROW[5]), smp(gc)[:, :, NS - 1:NS].to_broadcast([4, NB, NS]), smp(gc), SUB).then_inc(s("g_gc"), 1)
            dve.wait_ge(*at("g_eg", 1))
            TT(GROW[3][:, 0:T], GROW[3][:, 0:T], GROW[0][:, 0:T], MUL)
            CP(gc[:, T:T + 11], GROW[1][:, 0:11]).then_inc(s("g_rows"), 1)

            proj_lo(1, 2)
            dve.wait_ge(*at("halo_pe", 1))
            link(CP(convT, PS[:, 4, 0:288].rearrange("p (a b) -> p a b", a=12)))
            dve.sem_inc(s("cin0"), 1)

            n_ = CONVW - 3
            for m in range(12):
                if m % 2 == 0:
                    proj_lo(1, m // 2 + 3)
                if m >= 4:
                    dve.wait_ge(*at("conv", m - 3))
                    dve.wait_ge(*at("last", m - 3))
                dve.wait_ge(*at("cin", m + 1))
                link(CP(cins(m)[:, :, 0:3], convT[:, m, :].rearrange("p (b t) -> p b t", b=NB)))
                if m >= 2:
                    dve.wait_ge(*at("convs", m - 1))
                w = [vec[:, NVEC + 12 * j + m:NVEC + 12 * j + m + 1] for j in range(4)]
                acc, src = cacc[:, m % 2, 0:n_], cin[:, m % 4, :]
                link(TSC(acc, src[:, 0:n_], w[0], None, MUL))
                link(STT(acc, src[:, 1:1 + n_], w[1], acc, MUL, ADD))
                link(STT(acc, src[:, 2:2 + n_], w[2], acc, MUL, ADD))
                STT(acc, src[:, 3:3 + n_], w[3], acc, MUL, ADD).then_inc(s("conv"), 1)

            for i in range(9, 14):
                proj_lo(1, i)

            dve.wait_ge(*at("g_colpe", 1))
            CP(gcol[:, :, 0:2, :], PS[:, 0, 0:48].rearrange("p (a b c) -> p a b c", a=4, b=3)[:, :, 0:2, :])
            CP(gcol[0:R2, :, 2, :], PS[0:R2, 0, 0:48].rearrange("p (a b c) -> p a b c", a=4, b=3)[:, :, 2, :]).then_inc(s("g_col"), 1)
            dve.wait_ge(*at("g_bc", 1))
            CP(kb, bank4(4))
            dve.wait_ge(*at("g_eq", 1))
            incl, strict = const(C1, "incl"), const(C1, "strict")
            for h in range(H):
                TT(decI[:, h, 0:256], PS[:, h, 0:256], incl[:, 0:256], ADD)
                TT(decI[0:R2, h, 256:T], PS[0:R2, h, 256:T], incl[0:R2, 256:T], ADD).then_inc(s("g_dx"), 1)
            dve.wait_ge(*at("g_dx", 4))
            dve.sem_inc(s("g_bcev"), 1)
            dve.wait_ge(*at("g_l2r", 1))
            link(TT(P[:, 4:8, :], P[:, 4:8, :], sqn[:, 4:8, :], MUL))
            TT(kb, P[:, 4:8, :], kb, MUL).then_inc(s("g_kb"), 1)
            dve.wait_ge(*at("g_l2r", 2))
            TT(P[:, 0:4, :], P[:, 0:4, :], sqn[:, 0:4, :], MUL).then_inc(s("g_kb"), 1)
            dve.wait_ge(*at("g_kb", 2))
            TT(qe, qe, P[:, 0:4, :], MUL)

            def parts(v):
                return [v[:, :, 0:256], v[0:R2, :, 256:T]]

            def maskb(name):
                v = const(C1, name)
                return [v[:, 0:256].unsqueeze(1).to_broadcast([128, H, 256]), v[0:R2, 256:T].unsqueeze(1).to_broadcast([R2, H, R2])]

            dve.wait_ge(*at("g_aa", 4))
            dve.wait_ge(*at("g_dec", 4))
            for v, p_, d_ in zip(parts(SDT), parts(bank4(0)), parts(decI)):
                last = TT(v, p_, d_, MUL)
            link(last)
            for v, m_ in zip(parts(SDT), maskb("strict")):
                last = TT(v, v, m_, MUL)
            last.then_inc(s("g_at"), 1)
            dve.wait_ge(*at("g_qk", 4))
            for v, p_, d_ in zip(parts(attg), parts(bank4(4)), parts(decI)):
                last = TT(v, p_, d_, MUL)
            last.then_inc(s("g_att"), 1)

            def scaled_tokens(dst, i, bank, col):
                n = TILES[i][1]
                return TT(dst[0:n, i, :].rearrange("p (a b) -> p a b", a=4), PS[0:n, bank, :].rearrange("p (a b) -> p a b", a=4),
                          gcol[0:n, col, i, :].unsqueeze(2).to_broadcast([n, 4, 128]), MUL)

            dve.wait_ge(*at("g_tok_a", 3))
            for i in range(3):
                scaled_tokens(rhsk, i, i, 1).then_inc(s("g_tok_d"), 1)
            dve.wait_ge(*at("st_conv", 32))
            for i in range(3):
                dve.wait_ge(*at("g_vt", i + 1))
                scaled_tokens(rhsv, i, 4 + i, 0).then_inc(s("g_tok_d"), 1)

            def tile(v, i):
                a, n = TILES[i]
                return v[0:n, :, a:a + n]

            def tmask(name, i):
                a, n = TILES[i]
                return const(C1, name)[0:n, a:a + n].unsqueeze(1).to_broadcast([n, H, n])

            for n_, (k, i) in enumerate(ORDER):
                what, out, lhs, rhs, _ = SOLVE[k]
                n = TILES[i][1]
                dve.wait_ge(*at("sv_pe", n_ + 1))
                ps = PS[0:n, n_ % 8, 0:4 * n].rearrange("p (a b) -> p a b", a=4)
                if what == "split":
                    TT(tile(SD, i), ps, tmask("same8", i), MUL)
                    link(TT(tile(SDT, i), tile(SDT, i), tmask("same8", i), MUL))
                    TT(tile(SO, i), ps, tile(SD, i), SUB).then_inc(s("sv_ev"), 1)
                    TT(tile(SRT, i), tmask("eye", i), tile(SDT, i), SUB)
                elif what == "add":
                    TT(tile(out, i), tile(out, i), ps, ADD).then_inc(s("sv_ev"), 1)
                else:
                    last = CP(tile(out, i), ps)
                    if what == "copyz":
                        last = TT(tile(SO, i), tmask("eye", i), ps, SUB)
                    last.then_inc(s("sv_ev"), 1)

            dve.wait_ge(*at("l_alpha", 1))
            for p in range(2):
                last = TSC(bc_[:, p, :], PS[:, 6 + p, 0:T], vec[:, VEC["balpha"] + p:VEC["balpha"] + p + 1], None, ADD)
            link(last)
            STT(cb_, bc_, -1.0, bc_, MUL, MAX).then_inc(s("l_abs"), 1)

            def gla_decays():
                dve.wait_ge(*at("l_lse", 1))
                link(STT(bc_, bc_, 0.0, cb_, MIN, SUB))
                link(TSC(kx_, bc_, 1.0 / 16.0, None, MUL))
                for p in range(2):
                    last = V.tensor_tensor_scan(bc_[:, p, :], const(C1, "rst"), kx_[:, p, :], 0.0, MUL, ADD)
                link(last)
                for p in range(2):
                    for v, n, k, mid in ((slice(0, 256), 64, 4, 31), (slice(256, TP), PR2, 1, 7), (slice(TP, T), NS, NB, 1)):
                        x4 = bc_[:, p, v].rearrange("p (c t) -> p c t", t=n)
                        TT(cb_[:, p, v].rearrange("p (c t) -> p c t", t=n), x4, x4[:, :, mid:mid + 1].to_broadcast([128, k, n]), SUB)
                        last = TT(kx_[:, p, v].rearrange("p (c t) -> p c t", t=n), x4[:, :, n - 1:n].to_broadcast([128, k, n]), x4, SUB)
                last.then_inc(s("l_x"), 1)
                dve.wait_ge(*at("l_e", 1))
                TT(q1, P[:, 16:18, :], e1, MUL)
                TT(k1, P[:, 18:20, :], e2, MUL)
                link(TT(k2, P[:, 18:20, :], kx_, MUL))
                V.memset(q2[64:128, 0:4:2, :], 0.0)
                link(V.memset(q2[0:64, 1:4:2, :], 0.0))
                for h in range(H):
                    r = slice(64 * (h % 2), 64 * (h % 2) + 64)
                    last = TT(q2[r, h, :], P[r, 16 + h // 2, :], e3[r, h // 2, :], MUL)
                last.then_inc(s("l_dqk"), 1)

            for i in range(3):
                dve.wait_ge(*at("g_upe", i + 1))
                dve.wait_ge(*at("g_ua", i + 1))
                scaled_tokens(rhsk, i, 3, 3).then_inc(s("g_ue"), 1)
                if i == 0:
                    dve.wait_ge(*at("g_spe", 1))
                    CP(sg[:, 0], PS[:, 5, :].rearrange("p (a b) -> p a b", a=4)).then_inc(s("g_s"), 1)
                    dve.wait_ge(*at("g_wev", 3))
                    for h in range(H):
                        last = TT(wtm[:, h], kb[:, h:h + 1, 256:T].to_broadcast([128, SEGS, R2]),
                                  const(C1, "seg9").rearrange("p (a b) -> p a b", a=SEGS), MUL)
                    last.then_inc(s("g_wtm"), 1)
                if i == 1:
                    dve.wait_ge(*at("g_spe", 2))
                    for h in range(H):
                        last = STT(sg[:, 1, h, :], sg[:, 0, h, :], dbc[:, h, 1:2], PS[:, 5, 128 * h:128 * h + 128], MUL, ADD)
                    last.then_inc(s("g_s"), 1)

            gla_decays()

            def g_update(h):
                dve.wait_ge(*at("g_state_pe", h + 1))
                state_update("g_", stA, h, GPAIRS[h], dbc[:, h, 3:11])

            norm("g_", 0, 12, "gdn", rms=True, prepare=lambda: g_update(0))
            for h in range(1, H):
                g_update(h)
            for h in range(H):
                last = STT(sg[:, 2, h, :], sg[:, 1, h, :], dbc[:, h, 2:3], PS[:, 6, 128 * h:128 * h + 128], MUL, ADD)
            last.then_inc(s("g_pst"), 1)

            for h, b in enumerate([5, 6, 7, 0]):
                dve.wait_ge(*at("l_qk", h + 1))
                if h == 0:
                    dve.wait_ge(*at("st_gp", 16))
                gm = const(C1, "gla")
                TT(attl[:, h, 0:256], PS[:, b, 0:256], gm[:, 0:256], MUL)
                TT(attl[0:R2, h, 256:T], PS[0:R2, b, 256:T], gm[0:R2, 256:T], MUL).then_inc(s("l_att"), 1)
            for p in range(2):
                dve.wait_ge(*at("l_upe", p + 1))
                for c in range(5):
                    for q in range(2):
                        r = slice(64 * q, 64 * q + 64)
                        u = PS[r, LCHUNK[p][2], 128 * q:128 * q + 128] if c == 4 else PS[r, LCHUNK[p][c % 2], 256 * (c // 2) + 128 * q:256 * (c // 2) + 128 * q + 128]
                        end = 64 * c + 63 if c < 4 else TP - 1
                        if c == 0:
                            last = CP(sc[r, 0, p, :], u)
                        else:
                            last = STT(sc[r, c, p, :], sc[r, c - 1, p, :], e3[r, p, end:end + 1], u, MUL, ADD)
                    link(last)
                dve.sem_inc(s("l_sc"), 1)

            def l_update(h):
                r, p = slice(64 * (h % 2), 64 * (h % 2) + 64), h // 2
                dve.wait_ge(*at("l_state_pe", h + 1))
                v = stG[r, p::2, :]
                link(TT(v, v, smp(e3[r, p, :])[:, :, NS - 1:NS].to_broadcast([64, NB, 128]), MUL))
                for j, b in enumerate(LPAIRS[h]):
                    last = TT(v[:, 4 * j:4 * j + 4, :], v[:, 4 * j:4 * j + 4, :], PS[r, b, :].rearrange("p (a b) -> p a b", a=4), ADD)
                last.then_inc(s("l_stu"), 1)

            x_lo("out", 0, mix, 9)
            norm("l_", 4, 24, "gla", prepare=lambda: (l_update(0), proj_lo(1, 14)))
            l_update(1)
            x_lo("out", 1, mix, 10)
            l_update(2)
            l_update(3)
            proj_lo(1, 15)

            residual(1)
            layer_norm("n1m_", "mix1", lambda: ffn_first(1), "out", 11)

            link(V.memset(lt, 0.0))
            dve.wait_ge(*at("x_log", 1))
            CP(lt[:, 0:2, :], PS[:, 5:7, 0:8])
            link(CP(lt[0:R2, 2, :], PS[0:R2, 7, 0:8]))
            link(V.tensor_reduce(st3[:, :, 0], lt, AX.X, MAX))
            TT(lt, lt, st3[:, :, 0:1].to_broadcast([128, 3, NE]), SUB).then_inc(s("x_lm"), 1)
            dve.wait_ge(*at("x_exp", 1))
            link(V.tensor_reduce(st3[:, :, 1], lt, AX.X, ADD))
            link(V.reciprocal(st3[:, :, 2], st3[:, :, 1]))
            link(TT(lt, lt, st3[:, :, 2:3].to_broadcast([128, 3, NE]), MUL))
            for i in range(3):
                other = lt[:, i:i + 1, :].to_broadcast([128, NE, NE])
                own = lt[:, i, :].unsqueeze(2).to_broadcast([128, NE, NE])
                TT(gcmp[:, i, :].rearrange("p (a b) -> p a b", a=NE), other, own, ALU.is_gt)
                last = TT(geq[:, i, :].rearrange("p (a b) -> p a b", a=NE), other, own, ALU.is_equal)
            link(last)
            link(TT(geq, geq, const(C1, "tri").unsqueeze(1).to_broadcast([128, 3, 64]), MUL))
            link(TT(gcmp, gcmp, geq, ADD))
            link(V.tensor_reduce(lm, gcmp.rearrange("p a (b c) -> p a b c", b=NE), AX.X, ADD))
            link(TSC(lm, lm, 1.5, None, ALU.is_lt))
            link(TT(gate, lm, lt, MUL))
            link(V.tensor_reduce(st3[:, :, 3], gate, AX.X, ADD))
            link(V.reciprocal(st3[:, :, 4], st3[:, :, 3]))
            TT(gate, gate, st3[:, :, 4:5].to_broadcast([128, 3, NE]), MUL).then_inc(s("x_gate"), 1)
            dve.wait_ge(*at("n1m_z", 1))
            dve.wait_ge(*at("st_all", 16 * 19))
            dve.wait_ge(*at("st_conv", 32))
            ffn(1)
            layer_norm("n1f_", "ffn1")
            for i in (0, 2):
                n = TILES[i][1]
                dve.wait_ge(*at("y_pe", 3 + i + 1))
                CP(proj[0:n, 1024 * i + 512:1024 * i + 1024], PS[0:n, 2 * i + 1, :]).then_inc(s("y_ev"), 1)


def _constants(np):
    f = np.float32
    cc = np.zeros((128, 512), f)
    cc[:, 0:128] = np.eye(128)
    cc[:, 128:256] = 1.0 / D
    cc[:, 256:384] = 1.0 / 128
    cc[:, 384:512] = 1.0
    c0 = np.zeros((128, N0), f)

    def put(c, table, name, v):
        a, n = table[name]
        v = np.asarray(v, np.float64).reshape(v.shape[0], n)
        c[:v.shape[0], a:a + n] = v

    rot = np.zeros((128, 128))
    for j in range(64):
        rot[64 + j, j] = -1.0
        rot[j, 64 + j] = 1.0
    put(c0, C0, "rot", rot)
    pos = np.concatenate([np.arange(TP), np.tile(2048 + np.arange(NS), NB)]).astype(f)
    inv = (10000.0 ** (-np.arange(64, dtype=f) / f(64))).astype(f)
    ang = np.tile((pos[None, :] * inv[:, None]).astype(f), (2, 1)).astype(np.float64)
    for name, v in (("cos", np.cos(ang)), ("sin", np.sin(ang))):
        put(c0, C0, name, np.stack([v, v * 128 ** -0.5], 1))
    seq = np.concatenate([np.zeros(TP, int), 1 + np.arange(TS) // NS])
    idx = np.concatenate([np.arange(TP), np.arange(TS) % NS])
    ln = np.concatenate([np.full(TP, TP), np.full(TS, NS)])
    gam = 1.0 - 2.0 ** (-5.0 - np.arange(H))
    ok = (seq[:, None] == seq[None, :]) & (idx[None, :] >= idx[:, None])
    diff = np.where(ok, idx[None, :] - idx[:, None], 0)
    dec = np.zeros((128, H, ATT))
    mask = np.full((128, ATT), -1e30)
    for (a, n), (lo, hi), at in zip(TILES, ((0, TP), (128, TP), (256, T)), (0, A1, A2)):
        w = hi - lo
        mask[:n, at:at + w] = np.where(ok[a:a + n, lo:hi], 0.0, -1e30)
        for h in range(H):
            dec[:n, h, at:at + w] = np.where(ok[a:a + n, lo:hi], gam[h] ** diff[a:a + n, lo:hi], 0.0)
    put(c0, C0, "dec", dec)
    put(c0, C0, "mask", mask)
    put(c0, C0, "gq", np.broadcast_to((gam[:, None] ** (idx[TP:] + 1.0)[None, :])[None], (128, H, TS)))
    gk = gam[None, :] ** (ln - 1 - idx)[:, None]
    put(c0, C0, "gk", np.stack([gk[0:128], gk[128:256]], 1))
    blk = (seq[256:, None] == np.arange(SEGS)[None, :]).astype(f)
    put(c0, C0, "gk2", gk[256:, :, None] * blk[:, None, :])
    put(c0, C0, "blk", blk)
    c1 = np.zeros((128, N1), f)
    chunk = np.concatenate([np.arange(256) // 64, np.full(PR2, 4), 5 + np.arange(TS) // NS])
    tabs = {n: np.zeros((128, T)) for n in ("strict", "same8", "eye", "gla")}
    incl = np.full((128, T), -1e30)
    for a, n in TILES:
        q = ok[a:a + n, a:a + n]
        r = np.arange(n)
        incl[:n, a:a + n] = np.where(q, 0.0, -1e30)
        tabs["strict"][:n, a:a + n] = q & (r[None, :] > r[:, None])
        tabs["same8"][:n, a:a + n] = (r[None, :] // 8) == (r[:, None] // 8)
        tabs["eye"][:n, a:a + n] = np.eye(n)
        tabs["gla"][:n, a:a + n] = q & (chunk[a:a + n, None] == chunk[None, a:a + n])
    put(c1, C1, "incl", incl)
    for n_, v in tabs.items():
        put(c1, C1, n_, v)
    start = np.ones(T)
    start[[0, 64, 128, 192, 256, *range(TP, T, NS)]] = 0
    put(c1, C1, "rst", np.broadcast_to(start, (128, T)))
    put(c1, C1, "seg9", np.broadcast_to(blk.T[None], (128, SEGS, R2)))
    put(c1, C1, "blk", blk)
    put(c1, C1, "tri", np.broadcast_to(np.tril(np.ones((NE, NE)), -1)[None], (128, NE, NE)))
    r4 = np.zeros((4, N4), f)
    first = idx == 0
    r4[:, 0:T] = np.where(first, 0.0, 1.0)
    r4[:, T:2 * T] = np.where(first, -3e38, 0.0)
    g = np.where(first, 0.0, 1.0)
    g[[128, 256]] = 0.0
    r4[:, 2 * T:3 * T] = g
    return {"c_common": cc, "c_layer0": c0, "c_layer1": c1, "c_rows": r4}


_DIRECT = ["state_ret", "state_mlstm_c", "state_mlstm_n", "state_gdn", "state_gdn_conv", "state_gla", "w_in0", "w_out0",
           "ffn0_w_gate", "ffn0_w_up", "ffn0_w_down", "w_in1", "gla_w_alpha", "w_out1", "moe_w_router", "moe_b_router",
           "moe_w_gate", "moe_w_up", "moe_w_down"]
_OUTS = {"y_all": (T, D), "prompt_ret": (1, 4, 128, 128), "prompt_c": (1, 4, 128, 128), "prompt_n": (1, 4, 128), "m_rows": (4, 9),
         "prompt_gdn": (1, 4, 128, 128), "prompt_conv": (1, 3, QKV), "prompt_gla": (1, 4, 64, 128), "sample_ret": (NB, 4, 128, 128),
         "sample_c": (NB, 4, 128, 128), "sample_n": (NB, 4, 128), "sample_gdn": (NB, 4, 128, 128), "sample_conv": (NB, 3, QKV),
         "sample_gla": (NB, 4, 64, 128)}


def kernel(**inputs):
    import numpy as np
    import concourse.bacc as bacc
    from concourse.bass_utils import run_bass_kernel_spmd

    x = {k: np.asarray(v) for k, v in inputs.items()}
    arrays = {n: np.ascontiguousarray(x[n]) for n in _DIRECT}
    arrays["x_all"] = np.concatenate([x["meta_tokens"], x["x_prompt"].reshape(SEQ, D), x["x_sample"].reshape(TS, D)])
    norms = [x[n] for n in ("ln0_mix_g", "ln0_mix_b", "ln0_ffn_g", "ln0_ffn_b", "ln1_mix_g", "ln1_mix_b", "ln1_ffn_g", "ln1_ffn_b",
                            "ret_norm_g", "mlstm_norm_g", "gdn_norm_g", "gla_norm_g", "gla_b_alpha")]
    arrays["vec_rows"] = np.concatenate([v.reshape(-1, 128) for v in norms])
    arrays["conv_rows"] = np.ascontiguousarray(x["gdn_conv_w"]).reshape(NCONV, 128)
    arrays["gate_cols"] = np.stack([x["mlstm_gate_bias"][0:4], x["mlstm_gate_bias"][4:8], x["gdn_a_log"], x["gdn_dt_bias"]], 1)
    arrays["m_rows"] = np.ascontiguousarray(x["state_mlstm_m"].T)
    arrays |= _constants(np)
    nc = bacc.Bacc("TRN2", target_bir_lowering=False, num_devices=1)
    I = {n: nc.dram_tensor("in_" + n, a.shape, mybir.dt.float32, kind="ExternalInput").ap() for n, a in arrays.items()}
    O = {n: nc.dram_tensor("out_" + n, shape, mybir.dt.float32, kind="ExternalOutput").ap() for n, shape in _OUTS.items()}
    build(nc, I, O)
    r = run_bass_kernel_spmd(nc, [{"in_" + n: a for n, a in arrays.items()}], core_ids=[0]).results[0]
    o = {n: r["out_" + n] for n in _OUTS}
    y, m = o["y_all"], o["m_rows"]
    return (y[NMETA:TP].reshape(1, SEQ, D), y[TP:].reshape(NB, NS, D),
            o["prompt_ret"], o["prompt_c"], o["prompt_n"], np.ascontiguousarray(m[:, 8:9].T), o["prompt_gdn"], o["prompt_conv"], o["prompt_gla"],
            o["sample_ret"], o["sample_c"], o["sample_n"], np.ascontiguousarray(m[:, 0:8].T), o["sample_gdn"], o["sample_conv"], o["sample_gla"])
```
